# Optimizing a Trainium2 kernel written in Bass

```python
import math
import jax, jax.numpy as jnp
from jax import lax
import numpy as np

D_MODEL = 1024
BATCH = 1
SEQ = 256
DEPTH = 1

RWKV_HEADS = 8
RWKV_HEAD_DIM = 64
RWKV_WIDTH = RWKV_HEADS * RWKV_HEAD_DIM
DECAY_LORA = 64
AAA_LORA = 64
MV_LORA = 32
GATE_LORA = 128
LN_X_EPS = 64e-5
MOBA_HEADS = 8
MOBA_HEAD_DIM = 64
MOBA_WIDTH = MOBA_HEADS * MOBA_HEAD_DIM
MOBA_BLOCK = 256
MOBA_TOPK = 3
Q_CHUNK = 128
REL_BUCKETS = 32
REL_MAX_DIST = 128
N_GROUPS = 4
EXPERTS_PER_GROUP = 8
N_EXPERTS = N_GROUPS * EXPERTS_PER_GROUP
FINE_TOPK = 2
D_EXPERT = 512
MOE_CHUNK = 1024
NORM_EPS = 1e-6
QK_EPS = 1e-6
IN_WIDTH = 3 * RWKV_WIDTH + 3 * MOBA_WIDTH + 2 * D_MODEL
SPLITS = [RWKV_WIDTH, 2 * RWKV_WIDTH, 3 * RWKV_WIDTH,
          3 * RWKV_WIDTH + MOBA_WIDTH, 3 * RWKV_WIDTH + 2 * MOBA_WIDTH,
          3 * RWKV_WIDTH + 3 * MOBA_WIDTH, 3 * RWKV_WIDTH + 3 * MOBA_WIDTH + D_MODEL]

kernel_name = 'hybrid_rwkv7_moba_hmoe'

def rms_norm(x, g, eps=NORM_EPS):
    xf = x.astype(jnp.float32)
    y = xf * lax.rsqrt(jnp.mean(xf * xf, axis=-1, keepdims=True) + eps)
    return (y * g.astype(jnp.float32)).astype(x.dtype)

def token_shift(x):
    return jnp.pad(x, ((0, 0), (1, 0), (0, 0)))[:, :-1]

def t5_bucket(rel):
    n = jnp.maximum(-rel, 0)
    max_exact = REL_BUCKETS // 2
    nf = jnp.maximum(n, 1).astype(jnp.float32)
    large = max_exact + (jnp.log(nf / max_exact) / math.log(REL_MAX_DIST / max_exact)
                         * (REL_BUCKETS - max_exact)).astype(jnp.int32)
    large = jnp.minimum(large, REL_BUCKETS - 1)
    return jnp.where(n < max_exact, n, large)

def rwkv7_scan(r, w, k, v, a, b):
    B_, S_, H, N = r.shape

    def step(state, inp):
        r_t, w_t, k_t, v_t, a_t, b_t = inp
        sa = jnp.einsum('bhvk,bhk->bhv', state, a_t)
        state = (state * w_t[:, :, None, :] + sa[..., None] * b_t[:, :, None, :]
                 + v_t[..., None] * k_t[:, :, None, :])
        return state, jnp.einsum('bhvk,bhk->bhv', state, r_t)

    xs = tuple(jnp.moveaxis(t, 1, 0) for t in (r, w, k, v, a, b))
    s0 = jnp.zeros((B_, H, N, N), jnp.float32)
    _, y = lax.scan(step, s0, xs)
    return jnp.moveaxis(y, 0, 1)

def rwkv7_branch(xn, r_p, k_p, v_p, mu_rkv, mu_x, w0, w1, w2, a0, a1, a2, g1, g2,
                 k_k, k_a, r_k, lnx_g, lnx_b, v_first, vres):
    B_, S_, _ = xn.shape
    H, N = RWKV_HEADS, RWKV_HEAD_DIM
    f32 = jnp.float32
    r = r_p + (token_shift(r_p) - r_p) * mu_rkv[0]
    k = k_p + (token_shift(k_p) - k_p) * mu_rkv[1]
    v = v_p + (token_shift(v_p) - v_p) * mu_rkv[2]
    xx = token_shift(xn) - xn
    xw = xn + xx * mu_x[0]
    xa = xn + xx * mu_x[1]
    xg = xn + xx * mu_x[2]
    w = -jax.nn.softplus(-(w0 + jnp.tanh(xw @ w1) @ w2).astype(f32)) - 0.5
    decay = jnp.exp(-jnp.exp(w))
    a = jax.nn.sigmoid(a0 + (xa @ a1) @ a2)
    g = jax.nn.sigmoid(xg @ g1) @ g2
    if vres is None:
        v_first = v
    else:
        v_mu, v0, v1, v2 = vres
        xv = xn + xx * v_mu
        v = v + (v_first - v) * jax.nn.sigmoid(v0 + (xv @ v1) @ v2)
    heads = lambda t: t.reshape(B_, S_, H, N).astype(f32)
    kk = heads(k * k_k)
    kk = kk / jnp.maximum(jnp.sqrt(jnp.sum(kk * kk, axis=-1, keepdims=True)), 1e-12)
    k = k * (1.0 + (a - 1.0) * k_a)
    rh, kh, vh, ah = heads(r), heads(k), heads(v), heads(a)
    y = rwkv7_scan(rh, heads(decay), kh, vh, -kk, kk * ah)
    mean = jnp.mean(y, axis=-1, keepdims=True)
    var = jnp.mean(jnp.square(y - mean), axis=-1, keepdims=True)
    y = ((y - mean) * lax.rsqrt(var + LN_X_EPS)).reshape(B_, S_, H * N)
    y = y * lnx_g.astype(f32) + lnx_b.astype(f32)
    bonus = jnp.sum(rh * kh * r_k.astype(f32), axis=-1, keepdims=True) * vh
    y = (y + bonus.reshape(B_, S_, H * N)) * g.astype(f32)
    return y.astype(xn.dtype), v_first

def moba_branch(q, k, v, q_gain, k_gain, rel_table):
    B_, S_, _ = q.shape
    H, Dh = MOBA_HEADS, MOBA_HEAD_DIM
    f32 = jnp.float32
    q = rms_norm(q.reshape(B_, S_, H, Dh), q_gain, QK_EPS).transpose(0, 2, 1, 3) * (Dh ** -0.5)
    k = rms_norm(k.reshape(B_, S_, H, Dh), k_gain, QK_EPS).transpose(0, 2, 1, 3)
    v = v.reshape(B_, S_, H, Dh).transpose(0, 2, 1, 3)
    S_pad = -(-S_ // MOBA_BLOCK) * MOBA_BLOCK
    pad = ((0, 0), (0, 0), (0, S_pad - S_), (0, 0))
    k_pad, v_pad = jnp.pad(k, pad), jnp.pad(v, pad)
    nb = S_pad // MOBA_BLOCK
    topk = min(MOBA_TOPK, nb)
    k_blocks = k_pad.reshape(B_, H, nb, MOBA_BLOCK, Dh)
    v_blocks = v_pad.reshape(B_, H, nb, MOBA_BLOCK, Dh)
    k_mean = jnp.mean(k_blocks.astype(f32), axis=3)
    table_t = rel_table.T.astype(f32)
    b_ix = jnp.arange(B_)[:, None, None, None]
    h_ix = jnp.arange(H)[None, :, None, None]
    h_ix5 = jnp.arange(H)[None, :, None, None, None]
    offs = jnp.arange(MOBA_BLOCK)

    def chunk_fn(c):
        q0 = c * Q_CHUNK
        qc = lax.dynamic_slice_in_dim(q, q0, Q_CHUNK, axis=2)
        blk = q0 // MOBA_BLOCK
        qpos = q0 + jnp.arange(Q_CHUNK)
        sc = jnp.einsum('bhqd,bhnd->bhqn', qc.astype(f32), k_mean)
        sc = jnp.where(jnp.arange(nb) < blk, sc, -jnp.inf)
        _, idx = lax.top_k(sc, topk)
        valid = jnp.arange(topk) < blk
        kg = k_blocks[b_ix, h_ix, idx]
        vg = v_blocks[b_ix, h_ix, idx]
        kpos = idx[..., None] * MOBA_BLOCK + offs
        rb = table_t[h_ix5, t5_bucket(kpos - qpos[:, None, None])]
        ls = jnp.einsum('bhqd,bhqstd->bhqst', qc, kg).astype(f32) + rb
        ls = jnp.where(valid[:, None], ls, -jnp.inf).reshape(B_, H, Q_CHUNK, topk * MOBA_BLOCK)
        k_own = lax.dynamic_slice_in_dim(k_pad, blk * MOBA_BLOCK, MOBA_BLOCK, axis=2)
        v_own = lax.dynamic_slice_in_dim(v_pad, blk * MOBA_BLOCK, MOBA_BLOCK, axis=2)
        rel = (blk * MOBA_BLOCK + offs)[None, :] - qpos[:, None]
        lo = jnp.einsum('bhqd,bhtd->bhqt', qc, k_own).astype(f32) + table_t[:, t5_bucket(rel)]
        lo = jnp.where(rel <= 0, lo, -jnp.inf)
        p = jax.nn.softmax(jnp.concatenate([ls, lo], axis=-1), axis=-1)
        ps = p[..., :topk * MOBA_BLOCK].reshape(B_, H, Q_CHUNK, topk, MOBA_BLOCK).astype(v.dtype)
        po = p[..., topk * MOBA_BLOCK:].astype(v.dtype)
        return (jnp.einsum('bhqst,bhqstd->bhqd', ps, vg)
                + jnp.einsum('bhqt,bhtd->bhqd', po, v_own))

    outs = lax.map(chunk_fn, jnp.arange(S_ // Q_CHUNK))
    return outs.transpose(1, 0, 3, 2, 4).reshape(B_, S_, H * Dh)

def hier_moe(xn, w_grp, b_grp, w_exp, b_exp, w_gate, w_up, w_down):
    B_, S_, D = xn.shape
    t = xn.reshape(-1, D)
    T = t.shape[0]
    f32 = jnp.float32
    lg = (t @ w_grp + b_grp).astype(f32)
    pg = jax.nn.softmax(lg, axis=-1)
    g_sel = jnp.argmax(lg, axis=-1)
    p_top = jnp.take_along_axis(pg, g_sel[:, None], axis=-1)
    le = (t @ w_exp + b_exp).astype(f32).reshape(T, N_GROUPS, EXPERTS_PER_GROUP)
    le_sel = jnp.take_along_axis(le, g_sel[:, None, None], axis=1)[:, 0]
    pe = jax.nn.softmax(le_sel, axis=-1)
    v2, i2 = lax.top_k(pe, FINE_TOPK)
    gates = p_top * (v2 / jnp.sum(v2, axis=-1, keepdims=True))
    eid = g_sel[:, None] * EXPERTS_PER_GROUP + i2
    comb = jnp.sum(jax.nn.one_hot(eid, N_EXPERTS, dtype=f32) * gates[..., None], axis=1)
    chunk = math.gcd(T, MOE_CHUNK)

    def chunk_fn(args):
        tc, cc = args
        h = jax.nn.silu(jnp.einsum('td,edh->teh', tc, w_gate)) * jnp.einsum('td,edh->teh', tc, w_up)
        h = h * cc[..., None].astype(h.dtype)
        return jnp.einsum('teh,ehd->td', h, w_down)

    y = lax.map(chunk_fn, (t.reshape(-1, chunk, D), comb.reshape(-1, chunk, N_EXPERTS)))
    return y.reshape(B_, S_, D)

def setup_inputs(seed: int = 0) -> dict:
    key = jax.random.key(seed)
    ks = iter(jax.random.split(key, 48))
    f32 = jnp.float32

    def nrm(shape, scale):
        return scale * jax.random.normal(next(ks), shape, f32)

    def uni(shape, lo, hi):
        return jax.random.uniform(next(ks), shape, f32, lo, hi)

    L, D, CR, CM = DEPTH, D_MODEL, RWKV_WIDTH, MOBA_WIDTH
    LV = DEPTH - 1
    return {
        'x': nrm((BATCH, SEQ, D), 1.0),
        'norm_mix_g': 1.0 + nrm((L, D), 0.02),
        'norm_ffn_g': 1.0 + nrm((L, D), 0.02),
        'w_in': nrm((L, D, IN_WIDTH), D ** -0.5),
        'mu_rkv': uni((L, 3, CR), 0.0, 1.0),
        'mu_x': uni((L, 3, D), 0.0, 1.0),
        'w0': uni((L, CR), -6.5, -1.5),
        'w1': nrm((L, D, DECAY_LORA), D ** -0.5),
        'w2': nrm((L, DECAY_LORA, CR), 0.1 * DECAY_LORA ** -0.5),
        'a0': nrm((L, CR), 0.1),
        'a1': nrm((L, D, AAA_LORA), D ** -0.5),
        'a2': nrm((L, AAA_LORA, CR), 0.5 * AAA_LORA ** -0.5),
        'g1': nrm((L, D, GATE_LORA), D ** -0.5),
        'g2': nrm((L, GATE_LORA, CR), GATE_LORA ** -0.5),
        'k_k': 0.85 + nrm((L, CR), 0.05),
        'k_a': 1.0 + nrm((L, CR), 0.05),
        'r_k': nrm((L, RWKV_HEADS, RWKV_HEAD_DIM), 0.1),
        'lnx_g': 1.0 + nrm((L, CR), 0.02),
        'lnx_b': nrm((L, CR), 0.02),
        'vres_mu': uni((LV, D), 0.0, 1.0),
        'vres_v0': nrm((LV, CR), 0.1),
        'vres_v1': nrm((LV, D, MV_LORA), D ** -0.5),
        'vres_v2': nrm((LV, MV_LORA, CR), 0.5 * MV_LORA ** -0.5),
        'q_gain': 1.0 + nrm((L, MOBA_HEAD_DIM), 0.02),
        'k_gain': 1.0 + nrm((L, MOBA_HEAD_DIM), 0.02),
        'rel_bias': nrm((REL_BUCKETS, MOBA_HEADS), 0.5),
        'w_br_rwkv': nrm((L, CR, D), CR ** -0.5),
        'w_br_moba': nrm((L, CM, D), CM ** -0.5),
        'w_out': nrm((L, D, D), D ** -0.5),
        'w_grp': nrm((L, D, N_GROUPS), D ** -0.5),
        'b_grp': nrm((L, N_GROUPS), 0.01),
        'w_exp': nrm((L, D, N_EXPERTS), D ** -0.5),
        'b_exp': nrm((L, N_EXPERTS), 0.01),
        'w_gate': nrm((L, N_EXPERTS, D, D_EXPERT), D ** -0.5),
        'w_up': nrm((L, N_EXPERTS, D, D_EXPERT), D ** -0.5),
        'w_down': nrm((L, N_EXPERTS, D_EXPERT, D), D_EXPERT ** -0.5),
    }

def reference(x, norm_mix_g, norm_ffn_g, w_in, mu_rkv, mu_x, w0, w1, w2, a0, a1, a2, g1, g2,
              k_k, k_a, r_k, lnx_g, lnx_b, vres_mu, vres_v0, vres_v1, vres_v2,
              q_gain, k_gain, rel_bias, w_br_rwkv, w_br_moba, w_out,
              w_grp, b_grp, w_exp, b_exp, w_gate, w_up, w_down):
    v_first = None
    for l in range(DEPTH):
        xn = rms_norm(x, norm_mix_g[l])
        proj = xn @ w_in[l]
        r_p, k_p, v_p, q_m, k_m, v_m, gate_r, gate_m = jnp.split(proj, SPLITS, axis=-1)
        vres = None if l == 0 else (vres_mu[l - 1], vres_v0[l - 1], vres_v1[l - 1], vres_v2[l - 1])
        y_r, v_first = rwkv7_branch(xn, r_p, k_p, v_p, mu_rkv[l], mu_x[l], w0[l], w1[l], w2[l],
                                    a0[l], a1[l], a2[l], g1[l], g2[l], k_k[l], k_a[l], r_k[l],
                                    lnx_g[l], lnx_b[l], v_first, vres)
        y_m = moba_branch(q_m, k_m, v_m, q_gain[l], k_gain[l], rel_bias)
        h = (jax.nn.sigmoid(gate_r) * (y_r @ w_br_rwkv[l])
             + jax.nn.sigmoid(gate_m) * (y_m @ w_br_moba[l]))
        x = x + h @ w_out[l]
        xn = rms_norm(x, norm_ffn_g[l])
        x = x + hier_moe(xn, w_grp[l], b_grp[l], w_exp[l], b_exp[l], w_gate[l], w_up[l], w_down[l])
    return x


_drawn_inputs = setup_inputs


def setup_inputs(seed=0):
    import zlib

    import numpy as np

    out = dict(_drawn_inputs(seed))
    spreads = {}
    factors = {'w1': 8.0,
     'w2': 8.0,
     'lnx_g': 4.066,
     'lnx_b': 3.364,
     'q_gain': 8.0,
     'k_gain': 5.52,
     'b_grp': 3.856,
     'b_exp': 6.253}
    for name, (base, spread) in spreads.items():
        noise = np.random.default_rng([zlib.crc32(name.encode()), seed]).standard_normal(out[name].shape)
        drawn = base * np.exp(spread * noise) if base else spread * noise
        out[name] = __import__('jax').numpy.asarray(drawn.astype(out[name].dtype))
    for name, factor in factors.items():
        out[name] = (out[name] * factor).astype(out[name].dtype)
    return out
```

```python
from contextlib import ExitStack

import concourse.bass as bass
from concourse import mybir

F32 = mybir.dt.float32
F32R = mybir.dt.float32r
I32 = mybir.dt.int32
U32 = mybir.dt.uint32
ALU = mybir.AluOpType
ACT = mybir.ActivationFunctionType
AX = mybir.AxisListType

P = 128
T, D = 256, 1024
TT, KD = T // P, D // P
CW = 512
CT = CW // P
H, HD = 8, 64
NG, EG = 4, 8
NE = NG * EG
FE = 512
S = 64
NC = T // S
MAXO = 2 * T // (S + 1)
NV = 2 * T - 129
DECAY = 0.6065306597126334
NORM_EPS, QK_EPS, LNX_EPS = 1e-6, 1e-6, 64e-5
BIG = 1e30

CHUNK = 4096
HALF = CHUNK // 2
NB = 3
NS = 6
PRE = 14
PCH = [3 * CW, 4 * CW, 5 * CW, CW, 0, 2 * CW] + [6 * CW + CW * i for i in range(4)]

C_ID, C_BO, C_MK, C_TRI, C_ONE = 0, 128, 256, 256 + 7 * 128, 256 + 8 * 128
C_DESC = C_ONE + 128
C_EB = C_DESC + NG + NE
C_IP = C_EB + NE
C_UE = C_IP + 8
C_UB = C_UE + 3 * NE
C_M0T = C_UB + 3 * NE
NCONST = C_M0T + P
V_GMIX, V_MRKV, V_MX, V_W0, V_A0, V_KK, V_KA, V_RK, V_LG, V_LB, V_QG, V_KG = 0, 8, 20, 44, 48, 52, 56, 60, 64, 68, 72, 73
NVEC = 74


def bcast(ap, axis, n):
    dims = [list(d) for d in ap.ap]
    dims.insert(axis, [0, n])
    return bass.AP(ap.tensor, ap.offset, dims)


def build(nc, x, norm_mix_g, norm_ffn_g, w_in, mu_rkv, mu_x, w0, w1, w2, a0, a1, a2, g1, g2, k_k, k_a, r_k,
          lnx_g, lnx_b, q_gain, k_gain, rel_bias, w_br_rwkv, w_br_moba, w_out, w_grp, b_grp, w_exp, b_exp,
          w_gate, w_up, w_down, consts, bias_consts, slot_rows, out):
    with ExitStack() as ctx:
        def sb(name, shape, dt=F32):
            return ctx.enter_context(nc.sbuf_tensor(name, shape, dt))

        ring = sb("ring", [P, NS, CHUNK])
        wh = sb("wh", [P, NB, HALF], F32R)
        wl = sb("wl", [P, NB, HALF], F32R)
        xs = sb("xs", [P, 4096], F32R)
        reg = sb("reg", [P, 12248])
        banks = [ctx.enter_context(nc.psum_tensor(f"bank{i}", [P, 512], F32)) for i in range(8)]

        sem_names = (
            "consts vecs lora_w lora2 biasc xin xre "
            "rms0 rms1 xsn vecT PT xT xnT xsplit musplit "
            "hi lo_d lo_p half projev "
            "prefill prefset vecmm vec vecst hank lora lt sgm loraout gout "
            "sq ssum qkv qks qkn vtT vtok score nmx prob pnorm pT pTc av avc "
            "rk_sq rk_ss rk_nr cs cbias ebc expd ar bk bonus bons bonv tokT tok v_ch "
            "gram gcp gsel gl x0 nt t1 t1c dx xx z zc u uc y yc st stc st1 "
            "lnm lnc lnsq lnv lnve lnsd yr ysplit "
            "hm hsplit x2 r2 r2s r2q xn2 gbc xn2st xn2T xn2Tc wr logit rt rte cum cumd gates addr lists ovf zero "
            "tidx vg xg xgT xsx tg gf sg m tu uf h hT hs ty y_ sc "
            "ychunk fin out ch_d ch_a ch_p"
        ).split()
        s = {n: ctx.enter_context(nc.semaphore("s_" + n)) for n in sem_names}
        pre_in = [ctx.enter_context(nc.semaphore(f"s_pre{i}")) for i in range(2)]
        slot_in = [ctx.enter_context(nc.semaphore(f"s_slot{i}")) for i in range(NS)]

        bias_rows = nc.dram_tensor("bias_rows", [H, 384], F32).ap()
        xn2_dram = nc.dram_tensor("xn2_rows", [T, D], F32).ap()
        lists = nc.dram_tensor("slot_lists", [NE * T, 4], F32).ap()
        y_dram = nc.dram_tensor("expert_rows", [2 * T, D], F32).ap()

        def R(off, *dims, p0=0, p1=P):
            n = 1
            for d in dims:
                n *= d
            v = reg[p0:p1, off:off + n]
            if len(dims) == 2:
                return v.rearrange("p (a b) -> p a b", a=dims[0])
            if len(dims) == 3:
                return v.rearrange("p (a b c) -> p a b c", a=dims[0], b=dims[1])
            if len(dims) == 4:
                return v.rearrange("p (a b c d) -> p a b c d", a=dims[0], b=dims[1], c=dims[2])
            return v

        flat = ring[:, :, :].rearrange("p s n -> p (s n)")

        def A(off, *dims, p0=0, p1=P):
            n = 1
            for d in dims:
                n *= d
            o = 2 * CHUNK + off
            v = flat[p0:p1, o:o + n]
            if len(dims) == 2:
                return v.rearrange("p (a b) -> p a b", a=dims[0])
            if len(dims) == 3:
                return v.rearrange("p (a b c) -> p a b c", a=dims[0], b=dims[1])
            if len(dims) == 4:
                return v.rearrange("p (a b c d) -> p a b c d", a=dims[0], b=dims[1], c=dims[2])
            return v

        cst = R(0, NCONST)
        ident, bones, tri, ones = (cst[:, o:o + P] for o in (C_ID, C_BO, C_TRI, C_ONE))
        masks = cst[:, C_MK:C_MK + 7 * P].rearrange("p (l n) -> p l n", l=7)
        VT = R(NCONST, NVEC)
        SM = NCONST + NVEC
        st_ = R(SM, 16)
        mx = R(SM + 16, H, 2)
        rs = R(SM + 32, H, 2)
        cb = R(SM + 48, CT, 2)
        ncb = R(SM + 56, CT, 2)
        sc1 = R(SM + 64, CT)
        gqk = R(SM + 68, 2)
        tidx = R(SM + 72, 2, 4)
        vgb = R(SM + 16, 2, 4)
        over = R(SM + 80, 20)
        rowv = R(SM + 100, 2, 2, 4)
        addr = R(SM + 116, 2, 2)
        assert SM + 120 <= 2000
        O_XNT, O_AR, O_B, O_K, O_V, O_G, O_YR, O_YM = 2000, 4056, 6104, 7128, 8152, 9176, 10200, 11224
        xnT = R(O_XNT, KD, T + 1)
        xin = R(O_AR, TT, D)
        xrs = R(O_V, TT, D)
        AR = R(O_AR, CT, 2, 2, P)
        Bc = R(O_B, CT, T)
        Kc = R(O_K, CT, T)
        vc = R(O_V, CT, T)
        gg = R(O_G, CT, T)
        yr = R(O_YR, CT, T)
        ym = R(O_YM, CT, T)
        assert O_YM + 1024 <= 12248
        Z = A(3 * CHUNK, 16, T)
        pads = [A(3 * CHUNK + i * CT * (T + 1), CT, T + 1) for i in range(3)]

        WL, WM = A(0, KD, 256), A(2048, KD, 256)
        PR, PT_ = A(0, H, 384), A(3072, H, 3, P)
        HK, JJ = A(6144, H, 256), A(8192, P)
        qb, kb, vtm = A(8320, CT, T), A(9344, CT, T), A(10368, TT, CW)
        sqb = A(3072, 2, CT * T)

        df, rr, kk, kn, nr = (A(1024 * i, CT, T) for i in range(5))
        EP = A(5120, CT, 2, P + 1)
        EN, cs = A(6160, CT, T), A(7184, CT, T)
        Btok, Ktok, Vtok = (A(9216 + 1024 * i, 2, CW) for i in range(3))

        GRo = [A(0, 4, 4, P), A(4608, 4, 4, P)]
        XXo = [A(2048, 4, 2, P), A(4608 + 2048, 4, 2, P)]
        NTo = [A(3072, 4, P), A(4608 + 3072, 4, P)]
        T1o = [A(3584, 4, P), A(4608 + 3584, 4, P)]
        Zb, Ub = A(4096, CW), R(O_XNT, CW)
        St = R(O_XNT + 512, CT, HD)

        xh, xl = (xs[:, i * 2048:(i + 1) * 2048].rearrange("p (k t) -> p k t", k=KD) for i in range(2))
        ysp = xs[:, :].rearrange("p (b q c t) -> p b q c t", b=2, q=2, c=CT)
        xsx = [xs[:, b * 1024:(b + 1) * 1024].rearrange("p (k m) -> p k m", k=KD) for b in range(2)]
        xsh = xs[:, 2048:2560].rearrange("p (k m) -> p k m", k=FE // P)
        hTm = R(O_AR, KD, T)

        xg = [R(O_AR + 1024 * b, D, p1=S) for b in range(2)]
        tg, tu, gf, sg = (R(O_XNT + 512 * i, FE, p1=S) for i in range(4))
        ysb = [R(O_B + 1024 * b, 2, 512, p1=S) for b in range(2)]
        ty = R(O_YR, 512, p1=S)
        ub = R(O_YR + 512, 512, p1=S)
        hb = R(O_YM, 512, p1=S)
        Wr = R(O_YM, KD, NG + NE)
        brc = R(O_YM + KD * (NG + NE), NG + NE)
        gbc = R(O_YR, D)
        yall = A(CHUNK, TT, 2 * D)

        def chunk_view(slot, kind):
            k = 8 if kind in ("cols", "rows") else 4
            return ring[:, slot, :].rearrange("p (k n) -> p k n", k=k)

        def half_view(slot, kind, j):
            v = chunk_view(slot, kind)
            if kind == "cols":
                return v[:, :, 256 * j:256 * j + 256]
            if kind == "rows":
                return v[:, 4 * j:4 * j + 4, :]
            return v[:, :, 512 * j:512 * j + 512]

        def part_view(w, b, kind):
            k = 8 if kind == "cols" else 4
            return w[:, b, :].rearrange("p (k n) -> p k n", k=k)

        def split_hi(eng, g, b, slot, kind, j, landed):
            landed()
            if not isinstance(g, int) or g >= NB:
                eng.wait_ge(s["half"], g - NB + 1)
            eng.activation(part_view(wh, b, kind), half_view(slot, kind, j), ACT.Copy).then_inc(s["hi"], 1)

        def split_lo(eng, g, b, slot, kind, j, which):
            k = 8 if kind == "cols" else 4
            q = slice(0, 3 * k // 4) if which == "lo_d" else slice(3 * k // 4, k)
            eng.wait_ge(s["hi"], g + 1)
            eng.tensor_tensor(part_view(wl, b, kind)[:, q, :], half_view(slot, kind, j)[:, q, :],
                              part_view(wh, b, kind)[:, q, :].bitcast(F32), ALU.subtract).then_inc(s[which], 1)

        def pre_kind(c):
            return "br" if c in (10, 11) else "cols"

        def pre_hi(eng, g):
            c = g // 2
            split_hi(eng, g, g % NB, c % 2, pre_kind(c), g % 2, lambda: eng.wait_ge(pre_in[c % 2], 16 * (c // 2 + 1)))

        def pre_lo(eng, g, which):
            c = g // 2
            split_lo(eng, g, g % NB, c % 2, pre_kind(c), g % 2, which)

        def moe_half(n, i):
            idx = 3 * n - 1 + i // 2
            return 2 * PRE + 2 * idx + i % 2

        KINDS = ("rows", "rows", "down", "down", "rows", "rows")

        def moe_place(n0, i):
            idx = 3 * n0 - 1 + i // 2
            return (2 * PRE + 2 * idx + i % 2) % NB, idx % NS

        def moe_hi(eng, n, n0, i):
            b, slot = moe_place(n0, i)
            use = (n - n0) // 2 if isinstance(n, int) else None
            base = (3 * n0 - 1 + i // 2) // NS + 1
            count = 16 * (base + use) if use is not None else 8 * (n - n0) + 16 * base
            split_hi(eng, moe_half(n, i), b, slot, KINDS[i], i % 2, lambda: eng.wait_ge(slot_in[slot], count))

        def moe_lo(eng, n, n0, i, which):
            b, slot = moe_place(n0, i)
            split_lo(eng, moe_half(n, i), b, slot, KINDS[i], i % 2, which)

        FIRST = [(0, 0, "rows", 0), (0, 1, "rows", 1), (1, 0, "rows", 2), (1, 1, "rows", 3)]
        LAST = 3 * NE - 1

        def first_hi(eng, i):
            c, j, kind, o = FIRST[i]
            split_hi(eng, 2 * PRE + o, (2 * PRE + o) % NB, c, kind, j, lambda: eng.wait_ge(slot_in[c], 16))

        def first_lo(eng, i, which):
            c, j, kind, o = FIRST[i]
            split_lo(eng, 2 * PRE + o, (2 * PRE + o) % NB, c, kind, j, which)

        def last_hi(eng, j):
            g = 2 * PRE + 2 * LAST + j
            split_hi(eng, g, g % NB, LAST % NS, "down", j,
                     lambda: eng.wait_ge(slot_in[LAST % NS], 16 * (LAST // NS + 1)))

        def last_lo(eng, j, which):
            g = 2 * PRE + 2 * LAST + j
            split_lo(eng, g, g % NB, LAST % NS, "down", j, which)

        OKIND = ("rows", "rows", "rows", "rows", "down", "down")

        def over_half(i, q):
            return 2 * PRE + 6 * NE + 6 * i + q

        def over_hi(eng, i, q):
            split_hi(eng, over_half(i, q), (2 * PRE + q) % NB, q // 2, OKIND[q], q % 2,
                     lambda: eng.wait_ge(slot_in[q // 2], 16 * (3 * NE // NS) + 16 + 16 * i))

        def over_lo(eng, i, q, which):
            split_lo(eng, over_half(i, q), (2 * PRE + q) % NB, q // 2, OKIND[q], q % 2, which)

        def gate_done(n, extra=False):
            return 6 * n + 2 * PRE + (2 if extra or (isinstance(n, int) and n == 0) else 0)

        def up_done(n):
            return 6 * n + 2 * PRE + 4

        def down_done(n, j, late=False):
            return 6 * n + 2 * PRE + 7 + j - (2 if late else 0)

        def over_count(eng):
            eng.wait_ge(s["ovf"], 1)
            return eng.value_load(over[0:1, 0:1].bitcast(I32), min_val=0, max_val=MAXO)

        wg_v = w_gate[0].rearrange("e (p k) n -> e p (k n)", p=P)
        wu_v = w_up[0].rearrange("e (p k) n -> e p (k n)", p=P)
        wd_v = w_down[0].rearrange("e (p k) n -> e p (k n)", p=P)

        block = ctx.enter_context(nc.Block())

        @block.sync
        def _(sp):
            sp.dma_start(xin, x[0].rearrange("(a p) d -> p a d", p=P)).then_inc(s["xin"], 16)
            sp.dma_start(cst, consts[:, :]).then_inc(s["consts"], 16)

            def freed(c):
                sp.wait_ge(s["lo_d"], 2 * c + 2)
                sp.wait_ge(s["lo_p"], 2 * c + 2)

            def pre_load(c):
                if c >= 2:
                    freed(c - 2)
                dst = ring[:, c % 2, :]
                if c < 10:
                    src = w_in[0].rearrange("(k p) n -> p k n", p=P)[:, :, PCH[c]:PCH[c] + 512]
                    dst = dst.rearrange("p (k n) -> p k n", k=8)
                elif c < 12:
                    src = (w_br_rwkv if c == 10 else w_br_moba)[0].rearrange("(k p) n -> p k n", p=P)
                    dst = dst.rearrange("p (k n) -> p k n", k=4)
                else:
                    src = w_out[0].rearrange("(k p) n -> p k n", p=P)[:, :, 512 * (c - 12):512 * (c - 11)]
                    dst = dst.rearrange("p (k n) -> p k n", k=8)
                sp.dma_start(dst, src).then_inc(pre_in[c % 2], 16)

            for c in range(PRE):
                pre_load(c)

            def moe_load(slot, view, e):
                src = view[e] if isinstance(e, int) else view[bass.ds(e, 1)].rearrange("o p n -> (o p) n")
                sp.dma_start(ring[:, slot, :], src).then_inc(slot_in[slot], 16)

            freed(PRE - 2)
            moe_load(0, wg_v, 0)
            freed(PRE - 1)
            moe_load(1, wu_v, 0)
            sp.wait_ge(s["yc"], 2)
            sp.wait_ge(s["stc"], 1)
            sp.wait_ge(s["half"], 12)
            moe_load(2, wg_v, 1)
            moe_load(3, wd_v, 0)
            moe_load(4, wu_v, 1)
            sp.wait_ge(s["hm"], 8)
            moe_load(5, wg_v, 2)

            def step_loads(n, parity, first=True):
                for q, (view, e) in enumerate(((wg_v, n), (wd_v, n - 1), (wu_v, n))):
                    if q == 0 and not first:
                        continue
                    g = 2 * PRE + 2 * (3 * n - 1 + q - NS) + 2
                    sp.wait_ge(s["lo_d"], g)
                    sp.wait_ge(s["lo_p"], g)
                    moe_load((3 * parity - 1 + q) % NS, view, e)

            step_loads(2, 2, first=False)
            step_loads(3, 3)
            with sp.Fori(0, (NE - 4) // 2) as it:
                for j in range(2):
                    step_loads(2 * it + 4 + j, 4 + j)
            g = 2 * PRE + 2 * (LAST - NS) + 2
            sp.wait_ge(s["lo_d"], g)
            sp.wait_ge(s["lo_p"], g)
            moe_load(LAST % NS, wd_v, NE - 1)

            n_over = over_count(sp)
            with sp.If(n_over > 0):
                with sp.Fori(0, n_over) as i:
                    e = sp.value_load(over[0:1, bass.ds(i + 1, 1)].bitcast(I32), min_val=0, max_val=NE - 1)
                    g = 2 * PRE + 6 * NE + 6 * i
                    sp.wait_ge(s["lo_d"], g)
                    sp.wait_ge(s["lo_p"], g)
                    for q, view in enumerate((wg_v, wu_v, wd_v)):
                        moe_load(q, view, e)
            sp.wait_ge(s["lo_d"], 2 * PRE + 6 * NE)
            sp.wait_ge(s["lo_p"], 2 * PRE + 6 * NE)
            sp.wait_ge(s["sc"], 16 * NE + 16 * n_over)
            for a in range(TT):
                sp.dma_start(yall[:, a, :], y_dram[2 * P * a:2 * P * (a + 1), :].rearrange("(p k) d -> p (k d)", k=2))\
                  .then_inc(s["ychunk"], 16)
            sp.wait_ge(s["fin"], 1)
            sp.dma_start(out[0].rearrange("(a p) d -> p a d", p=P), xrs).then_inc(s["out"], 16)
            sp.wait_ge(s["out"], 16)

        @block.gpsimd
        def _(pool):
            chain = [0]

            def link(ins):
                chain[0] += 1
                ins.then_inc(s["ch_p"], 1)
                pool.wait_ge(s["ch_p"], chain[0])

            last_slot, last_token, last_row = (pool.to_reg(v) for v in (NE * T - 1, T - 1, 2 * T - 1))
            sent = A(3 * CHUNK, NE * T * 4 // P).bitcast(I32)
            pool.memset(sent, 1 << 20).then_inc(s["prefset"], 1)
            pool.wait_ge(s["prefset"], 1)
            pool.dma_start(lists.rearrange("(p a) w -> p (a w)", p=P).bitcast(I32), sent).then_inc(s["prefill"], 16)
            pool.wait_ge(s["lora_w"], 48)
            pool.wait_ge(s["PT"], 1)
            for i, (lo, hi) in enumerate(((0, 64), (64, 128), (128, 256))):
                mu = VT[:, V_MX + KD * i:V_MX + KD * (i + 1)]
                link(pool.tensor_tensor(WM[:, :, lo:hi], WL[:, :, lo:hi], bcast(mu, 2, hi - lo), ALU.mult))
            pool.tensor_tensor(WL, WL, WM, ALU.subtract).then_inc(s["musplit"], 1)
            for g in range(20):
                pre_lo(pool, g, "lo_p")

            for c in range(2):
                for b in range(2):
                    for u in range(4):
                        pool.wait_ge(s["gcp"], 8 * c + 4 * b + u + 1)
                        v = GRo[b][:, u].rearrange("p (a s) i -> p a s i", a=2)
                        pool.affine_select(out=v, in_=v, pattern=[[0, 2], [1, 2], [1, P]], compare_op=ALU.is_gt,
                                           fill=0.0, base=0, channel_multiplier=-1).then_inc(s["gsel"], 1)
                for lev in range(1, 7):
                    for b in range(2):
                        n = (c * 6 + lev - 1) * 2 + b
                        pool.wait_ge(s["gsel"], 8 * c + 4 * b + 4)
                        if n >= 2:
                            pool.wait_ge(s["t1"], n - 1)
                        pool.tensor_tensor(NTo[b], GRo[b][:, :, 0, :], bcast(masks[:, lev, :], 1, 4), ALU.mult)\
                            .then_inc(s["nt"], 1)
            for g in range(20, 28):
                pre_lo(pool, g, "lo_p")

            pool.wait_ge(s["prefill"], 16)
            pool.wait_ge(s["addr"], 1)
            for a in range(TT):
                for k in range(2):
                    pool.indirect_dma_start(
                        out=lists[:, :], out_offset=bass.IndirectOffsetOnAxis(ap=addr[:, a, k:k + 1].bitcast(U32), axis=0),
                        in_=rowv[:, a, k, :], in_offset=None, bounds_check=last_slot, oob_is_err=False)\
                        .then_inc(s["lists"], 16)
            pool.wait_ge(s["logit"], 1)
            for b in range(2):
                pool.memset(xg[b], 0.0).then_inc(s["zero"], 1)
            pool.wait_ge(s["zero"], 2)
            pool.wait_ge(s["lists"], 64)
            pool.wait_ge(s["xn2st"], 16)

            lview = lists.rearrange("(c s) w -> c s w", s=S)

            def list_rows(block_):
                return lview[block_] if isinstance(block_, int) else lview[bass.ds(block_, 1)].rearrange("o s w -> (o s) w")

            def load_tidx(n, b, row):
                if not isinstance(n, int) or n >= 2:
                    pool.wait_ge(s["xg"], 16 * (n - 1))
                pool.dma_start(tidx[0:S, b, :], list_rows(row)).then_inc(s["tidx"], 16)

            def gather(n, b):
                pool.wait_ge(s["tidx"], 16 * (n + 1))
                if not isinstance(n, int) or n >= 1:
                    pool.wait_ge(s["xg"], 16 * n)
                if not isinstance(n, int) or n >= 2:
                    pool.wait_ge(s["xgT"], n - 1)
                pool.nop(nofuse=True)
                pool.indirect_dma_start(
                    out=xg[b], out_offset=None, in_=xn2_dram[:, :],
                    in_offset=bass.IndirectOffsetOnAxis(ap=tidx[0:S, b, 0:1].bitcast(U32), axis=0),
                    bounds_check=last_token, oob_is_err=False).then_inc(s["xg"], 16)

            def load_vg(n, b, row):
                if not isinstance(n, int) or n >= 1:
                    pool.wait_ge(s["vg"], 16 * n)
                if not isinstance(n, int) or n >= 2:
                    pool.wait_ge(s["sc"], 16 * (n - 1))
                    pool.wait_ge(s["m"], n - 1)
                pool.dma_start(vgb[0:S, b, :], list_rows(row)).then_inc(s["vg"], 16)

            def scatter(n, b):
                pool.wait_ge(s["vg"], 16 * (n + 1))
                pool.wait_ge(s["y_"], 2 * n + 2)
                pool.nop(nofuse=True)
                pool.indirect_dma_start(
                    out=y_dram[:, :], out_offset=bass.IndirectOffsetOnAxis(ap=vgb[0:S, b, 1:2].bitcast(U32), axis=0),
                    in_=ysb[b].rearrange("p a n -> p (a n)"), in_offset=None, bounds_check=last_row,
                    oob_is_err=False).then_inc(s["sc"], 16)

            load_tidx(0, 0, 0)
            gather(0, 0)
            load_tidx(1, 1, NC)
            load_vg(0, 0, 0)
            for i in range(4):
                first_lo(pool, i, "lo_p")

            def step(n, n0, tail=False):
                b = n0 % 2
                moe_lo(pool, n, n0, 0, "lo_p")
                if not tail:
                    gather(n + 1, 1 - b)
                moe_lo(pool, n, n0, 1, "lo_p")
                scatter(n - 2, b)
                moe_lo(pool, n, n0, 2, "lo_p")
                moe_lo(pool, n, n0, 3, "lo_p")
                load_vg(n, b, NC * n)
                moe_lo(pool, n, n0, 4, "lo_p")
                if not tail:
                    load_tidx(n + 2, b, NC * (n + 2))
                moe_lo(pool, n, n0, 5, "lo_p")

            gather(1, 1)
            load_tidx(2, 0, 2 * NC)

            def step1():
                moe_lo(pool, 1, 1, 0, "lo_p")
                gather(2, 0)
                for i in (1, 2, 3):
                    moe_lo(pool, 1, 1, i, "lo_p")
                load_vg(1, 1, NC)
                moe_lo(pool, 1, 1, 4, "lo_p")
                load_tidx(3, 1, 3 * NC)
                moe_lo(pool, 1, 1, 5, "lo_p")

            step1()
            with pool.Fori(0, (NE - 4) // 2) as it:
                for j in range(2):
                    step(2 * it + 2 + j, 2 + j)
            moe_lo(pool, NE - 2, NE - 2, 0, "lo_p")
            gather(NE - 1, 1)
            moe_lo(pool, NE - 2, NE - 2, 1, "lo_p")
            scatter(NE - 4, 0)
            moe_lo(pool, NE - 2, NE - 2, 2, "lo_p")
            moe_lo(pool, NE - 2, NE - 2, 3, "lo_p")
            load_vg(NE - 2, 0, NC * (NE - 2))
            moe_lo(pool, NE - 2, NE - 2, 4, "lo_p")
            moe_lo(pool, NE - 2, NE - 2, 5, "lo_p")
            step(NE - 1, NE - 1, tail=True)
            last_lo(pool, 0, "lo_p")
            last_lo(pool, 1, "lo_p")
            scatter(NE - 2, 0)
            scatter(NE - 1, 1)

            n_over = over_count(pool)
            with pool.If(n_over > 0):
                with pool.Fori(0, n_over) as i:
                    n = NE + i
                    row = pool.value_load(over[0:1, bass.ds(i + 9, 1)].bitcast(I32), min_val=0, max_val=NE * NC - 1)
                    pool.wait_ge(s["sc"], 16 * n)
                    pool.dma_start(tidx[0:S, 0, :], list_rows(row)).then_inc(s["tidx"], 16)
                    pool.dma_start(vgb[0:S, 0, :], list_rows(row)).then_inc(s["vg"], 16)
                    pool.wait_ge(s["tidx"], 16 * (n + 1))
                    pool.nop(nofuse=True)
                    pool.indirect_dma_start(
                        out=xg[0], out_offset=None, in_=xn2_dram[:, :],
                        in_offset=bass.IndirectOffsetOnAxis(ap=tidx[0:S, 0, 0:1].bitcast(U32), axis=0),
                        bounds_check=last_token, oob_is_err=False).then_inc(s["xg"], 16)
                    for q in range(6):
                        over_lo(pool, i, q, "lo_p")
                    scatter(n, 0)

        @block.scalar
        def _(act):
            rows = R(O_K, P, p1=NVEC)

            def vec_in(v, row, n):
                act.dma_start(rows[row:row + n, :], v).then_inc(s["vecs"], 16)

            vec_in(norm_mix_g.rearrange("a (n p) -> (a n) p", p=P), V_GMIX, KD)
            vec_in(mu_rkv[0].rearrange("a (n p) -> (a n) p", p=P), V_MRKV, 3 * CT)
            vec_in(mu_x[0].rearrange("a (n p) -> (a n) p", p=P), V_MX, 3 * KD)
            for v, row in ((w0, V_W0), (a0, V_A0), (k_k, V_KK), (k_a, V_KA), (lnx_g, V_LG), (lnx_b, V_LB)):
                vec_in(v.rearrange("a (n p) -> (a n) p", p=P), row, CT)
            vec_in(r_k[0].rearrange("(n b) d -> n (b d)", b=2), V_RK, CT)
            for v, row in ((q_gain, V_QG), (k_gain, V_KG)):
                for i in range(2):
                    act.dma_start(rows[row:row + 1, 64 * i:64 * i + 64], v[:, :]).then_inc(s["vecs"], 16)
            for w, lo, hi in ((w1, 0, 64), (a1, 64, 128), (g1, 128, 256)):
                act.dma_start(WL[:, :, lo:hi], w[0].rearrange("(k p) n -> p k n", p=P)).then_inc(s["lora_w"], 16)
            act.dma_start(R(O_YR, CW, p1=64), w2[0]).then_inc(s["lora2"], 16)
            act.dma_start(R(O_YR, CW, p0=64), a2[0]).then_inc(s["lora2"], 16)
            act.dma_start(R(O_YR + CW, CW), g2[0]).then_inc(s["lora2"], 16)
            act.dma_start(R(O_G, 768, p1=32), bias_consts[0:32, 0:768]).then_inc(s["biasc"], 16)
            act.dma_start(R(O_G + 768, 8, p1=32), rel_bias[:, :]).then_inc(s["biasc"], 16)
            act.dma_start(JJ, bias_consts[:, 768:896]).then_inc(s["biasc"], 16)
            act.dma_start(rowv.rearrange("p a k w -> p (a k w)").bitcast(I32), slot_rows[:, :]).then_inc(s["rte"], 16)

            junk = R(O_V, D)
            act.wait_ge(s["xin"], 16)
            for a in range(TT):
                act.activation(junk, xin[:, a, :], ACT.Square, accum_out=st_[:, a:a + 1]).then_inc(s["rms0"], 1)
                act.wait_ge(s["rms0"], a + 1)
            act.wait_ge(s["rms1"], 1)
            act.activation(st_[:, 4:6], st_[:, 2:4], ACT.Sqrt).then_inc(s["rms0"], 1)
            act.wait_ge(s["xnT"], KD)
            act.activation(xh, xnT[:, :, 1:T + 1], ACT.Copy).then_inc(s["xsplit"], 1)

            def evac(g):
                act.wait_ge(s["half"], g + 1)
                src = banks[g % 2][:, :].rearrange("p (a t) -> p a t", a=2)
                if g < 4:
                    dst, f = (qb, kb)[g // 2][:, 2 * (g % 2):2 * (g % 2) + 2, :], ACT.Copy
                elif g < 6:
                    dst, f = ym[:, 2 * (g % 2):2 * (g % 2) + 2, :], ACT.Copy
                elif g < 12:
                    if g == 6:
                        act.wait_ge(s["prefill"], 16)
                    dst, f = pads[g // 2 - 3][:, 2 * (g % 2):2 * (g % 2) + 2, 1:T + 1], ACT.Copy
                else:
                    if g == 12:
                        act.wait_ge(s["ar"], 1)
                    dst, f = Z[:, 2 * (g - 12):2 * (g - 12) + 2, :], ACT.Sigmoid
                act.activation(dst, src, f).then_inc(s["projev"], 1)

            pre_hi(act, 0)
            for g in range(12):
                if g + 1 < 12:
                    pre_hi(act, g + 1)
                evac(g)

            act.wait_ge(s["lora"], 1)
            lt = R(O_V, 2, T)
            act.activation(lt[0:64, 0, :], banks[2][0:64, 0:T], ACT.Tanh).then_inc(s["lt"], 1)
            act.activation(lt[64:128, 0, :], banks[2][64:128, 0:T], ACT.Copy).then_inc(s["lt"], 1)
            act.activation(lt[:, 1, :], banks[2][:, T:2 * T], ACT.Sigmoid).then_inc(s["lt"], 1)
            act.wait_ge(s["vec"], 1)
            act.dma_start(bias_rows[:, 0:NV], R(O_B, NV, p1=H)).then_inc(s["vecst"], 16)
            act.wait_ge(s["loraout"], 1)
            for ct in range(CT):
                act.activation(Kc[:, ct, :], banks[3 + ct // 2][:, T * (ct % 2):T * (ct % 2) + T], ACT.Sigmoid,
                               bias=VT[:, V_W0 + ct:V_W0 + ct + 1]).then_inc(s["sgm"], 1)
            act.wait_ge(s["vecst"], 16)
            for ct in range(CT):
                act.activation(Bc[:, ct, :], banks[5 + ct // 2][:, T * (ct % 2):T * (ct % 2) + T], ACT.Sigmoid,
                               bias=VT[:, V_A0 + ct:V_A0 + ct + 1]).then_inc(s["sgm"], 1)
            for i in range(2):
                act.activation(gg[:, 2 * i:2 * i + 2, :], banks[(7, 2)[i]][:, :].rearrange("p (a t) -> p a t", a=2),
                               ACT.Copy).then_inc(s["gout"], 1)

            act.dma_start(HK, bass.AP(bias_rows.tensor, 0, [[1, P], [384, H], [1, 2 * P]])).then_inc(s["hank"], 16)
            act.wait_ge(s["qkv"], 2)
            act.activation(sqb, sqb, ACT.Sqrt).then_inc(s["qks"], 1)
            for a in range(TT):
                act.wait_ge(s["vtT"], a + 1)
                act.activation(vtm[:, a, :], banks[6 + a][:, :], ACT.Copy).then_inc(s["vtok"], 1)

            def exps(h):
                act.wait_ge(s["nmx"], h + 1)
                for q, (lo, hi) in enumerate(((0, 256), (256, 384))):
                    act.activation(PR[:, h, lo:hi], banks[2 + h % 4][:, lo:hi], ACT.Exp, bias=mx[:, h, q:q + 1],
                                   accum_out=rs[:, h, q:q + 1]).then_inc(s["prob"], 1)

            def pt_copy(h):
                act.wait_ge(s["pT"], h + 1)
                act.activation(PT_[:, h].rearrange("p a t -> p (a t)"), banks[h % 2][:, 0:384], ACT.Copy)\
                   .then_inc(s["pTc"], 1)

            for h in range(H + 1):
                if h < H:
                    exps(h)
                if h >= 1:
                    pt_copy(h - 1)
            for i in range(2):
                act.wait_ge(s["av"], 1)
                act.activation(ym[:, 2 * i:2 * i + 2, :], banks[6 + i][:, :].rearrange("p (a t) -> p a t", a=2),
                               ACT.Copy).then_inc(s["avc"], 1)

            act.wait_ge(s["rk_ss"], 1)
            for i in range(2):
                act.activation(nr[:, 2 * i:2 * i + 2, :], banks[2 + i][:, :].rearrange("p (a t) -> p a t", a=2),
                               ACT.Sqrt).then_inc(s["rk_nr"], 1)
            act.wait_ge(s["cbias"], 2)
            act.activation(EP[:, :, :, 0], cb, ACT.Exp).then_inc(s["ebc"], 1)
            act.activation(st_[:, 8:12], ncb[:, :, 1], ACT.Exp).then_inc(s["ebc"], 1)
            for ct in range(CT):
                for c in range(2):
                    act.activation(EP[:, ct, c, 1:P + 1], cs[:, ct, P * c:P * c + P], ACT.Exp, scale=-DECAY,
                                   bias=cb[:, ct, c:c + 1]).then_inc(s["expd"], 1)
                    act.activation(EN[:, ct, P * c:P * c + P], cs[:, ct, P * c:P * c + P], ACT.Exp, scale=DECAY,
                                   bias=ncb[:, ct, c:c + 1]).then_inc(s["expd"], 1)
            for i in range(6):
                act.wait_ge(s["tokT"], i + 1)
                act.activation((Btok, Ktok, Vtok)[(2, 0, 1)[i // 2]][:, i % 2, :], banks[(6, 7)[i % 2]][:, :], ACT.Copy)\
                   .then_inc(s["tok"], 1)
            pre_hi(act, 12)
            for g in range(12, 20):
                if g + 1 < 20:
                    pre_hi(act, g + 1)
                evac(g)

            for c in range(2):
                for b in range(2):
                    for u in range(4):
                        act.wait_ge(s["gram"], 8 * c + 4 * b + u + 1)
                        if c == 1 and u == 0 and b == 0:
                            act.wait_ge(s["y"], 1)
                        act.activation(GRo[b][:, u].rearrange("p a i -> p (a i)"), banks[u][:, :], ACT.Copy)\
                           .then_inc(s["gcp"], 1)
                for lev in range(1, 7):
                    for b in range(2):
                        n = (c * 6 + lev - 1) * 2 + b
                        act.wait_ge(s["t1"], n + 1)
                        if n >= 2:
                            act.wait_ge(s["dx"], n - 1)
                        act.activation(T1o[b].rearrange("p u i -> p (u i)"), banks[3 * b][:, :], ACT.Copy)\
                           .then_inc(s["t1c"], 1)
                act.wait_ge(s["z"], c + 1)
                for q in range(2):
                    act.activation(Zb.rearrange("p (v q n) -> p q v n", v=CT, q=2)[:, q],
                                   banks[3 * q][:, 0:CT * HD].rearrange("p (v n) -> p v n", v=CT), ACT.Copy)\
                       .then_inc(s["zc"], 1)
                act.wait_ge(s["u"], c + 1)
                act.activation(Ub, banks[1][:, :], ACT.Copy).then_inc(s["uc"], 1)
                act.wait_ge(s["y"], c + 1)
                act.activation(yr[:, :, P * c:P * c + P], banks[2][:, :].rearrange("p (a i) -> p a i", a=CT), ACT.Copy)\
                   .then_inc(s["yc"], 1)

            act.wait_ge(s["lnve"], 1)
            act.activation(Bc, Bc, ACT.Sqrt).then_inc(s["lnsd"], 1)

            def y_hi(b, src):
                act.activation(ysp[:, b, 0], src, ACT.Copy).then_inc(s["ysplit"], 1)

            act.wait_ge(s["half"], 20)
            y_hi(1, ym)
            pre_hi(act, 20)
            pre_hi(act, 21)
            pre_hi(act, 22)
            act.wait_ge(s["yr"], 1)
            y_hi(0, yr)
            act.dma_start(xrs, x[0].rearrange("(a p) d -> p a d", p=P)).then_inc(s["xre"], 16)
            pre_hi(act, 23)
            pre_hi(act, 24)
            pre_hi(act, 25)
            act.wait_ge(s["ysplit"], 4)
            act.dma_start(gbc, bcast(norm_ffn_g[0], 0, P)).then_inc(s["gbc"], 16)
            act.dma_start(Wr[:, :, 0:NG], w_grp[0].rearrange("(k p) n -> p k n", p=P)).then_inc(s["wr"], 16)
            act.dma_start(Wr[:, :, NG:NG + NE], w_exp[0].rearrange("(k p) n -> p k n", p=P)).then_inc(s["wr"], 16)
            act.dma_start(brc[:, 0:NG], bcast(b_grp[0], 0, P)).then_inc(s["wr"], 16)
            act.dma_start(brc[:, NG:NG + NE], bcast(b_exp[0], 0, P)).then_inc(s["wr"], 16)
            act.wait_ge(s["hm"], 8)
            act.wait_ge(s["half"], 24)
            act.activation(xh, hTm, ACT.Copy).then_inc(s["hsplit"], 1)
            pre_hi(act, 26)
            pre_hi(act, 27)

            act.wait_ge(s["x2"], 4)
            junk2 = R(O_B, D)
            for a in range(TT):
                act.activation(junk2, xrs[:, a, :], ACT.Square, accum_out=st_[:, a:a + 1]).then_inc(s["r2"], 1)
                act.wait_ge(s["r2"], a + 1)
            act.wait_ge(s["r2s"], 1)
            act.activation(st_[:, 4:6], st_[:, 2:4], ACT.Sqrt).then_inc(s["r2q"], 1)
            act.wait_ge(s["xn2"], TT)
            act.dma_start(xn2_dram.rearrange("(a p) d -> p a d", p=P), R(O_XNT, TT, D)).then_inc(s["xn2st"], 16)
            for q in range(4):
                act.wait_ge(s["xn2T"], q + 1)
                act.activation(hTm[:, 2 * q:2 * q + 2, :], banks[q][:, :].rearrange("p (a t) -> p a t", a=2), ACT.Copy)\
                   .then_inc(s["xn2Tc"], 1)
            act.wait_ge(s["rt"], 1)
            act.activation(R(O_B + 80, 2, NG), R(O_B + 80, 2, NG), ACT.Exp).then_inc(s["gates"], 1)
            act.wait_ge(s["rt"], 2)
            act.activation(R(O_B + 100, 2), R(O_B + 100, 2), ACT.Exp).then_inc(s["gates"], 1)

            def t_gate(n, extra=False):
                act.wait_ge(s["half"], gate_done(n, extra))
                if not isinstance(n, int) or n >= 1:
                    act.wait_ge(s["gf"], n)
                act.activation(tg, banks[0][S:2 * S, :], ACT.Copy).then_inc(s["tg"], 1)

            def t_up(n):
                act.wait_ge(s["half"], up_done(n))
                if not isinstance(n, int) or n >= 1:
                    act.wait_ge(s["uf"], n)
                act.activation(tu, banks[1][S:2 * S, :], ACT.Copy).then_inc(s["tu"], 1)

            def sigm(n):
                act.wait_ge(s["gf"], n + 1)
                if not isinstance(n, int) or n >= 1:
                    act.wait_ge(s["m"], n)
                act.activation(sg, gf, ACT.Sigmoid).then_inc(s["sg"], 1)

            def t_down(n, j, late=False):
                act.wait_ge(s["half"], down_done(n, j, late))
                if not isinstance(n, int) or n >= 1 or j:
                    act.wait_ge(s["y_"], 2 * n + j)
                act.activation(ty, banks[2 + j][S:2 * S, :], ACT.Copy).then_inc(s["ty"], 1)

            for i in range(4):
                first_hi(act, i)
                if i == 3:
                    t_gate(0)
                    sigm(0)

            def step(n, n0):
                moe_hi(act, n, n0, 0)
                if not isinstance(n, int) or n >= 2:
                    t_down(n - 2, 1)
                moe_hi(act, n, n0, 1)
                moe_hi(act, n, n0, 2)
                t_up(n - 1)
                moe_hi(act, n, n0, 3)
                moe_hi(act, n, n0, 4)
                t_gate(n)
                moe_hi(act, n, n0, 5)
                sigm(n)
                t_down(n - 1, 0)

            step(1, 1)
            with act.Fori(0, (NE - 2) // 2) as it:
                for j in range(2):
                    step(2 * it + 2 + j, 2 + j)
            last_hi(act, 0)
            t_down(NE - 2, 1)
            last_hi(act, 1)
            t_up(NE - 1)
            t_down(NE - 1, 0, late=True)
            t_down(NE - 1, 1, late=True)

            n_over = over_count(act)
            with act.If(n_over > 0):
                with act.Fori(0, n_over) as i:
                    n = NE + i
                    for q in range(3):
                        over_hi(act, i, q)
                    t_gate(n, extra=True)
                    sigm(n)
                    for q in range(3, 6):
                        over_hi(act, i, q)
                    t_up(n)
                    t_down(n, 0, late=True)
                    t_down(n, 1, late=True)

        @block.vector
        def _(dve):
            chain = [0]

            def link(ins):
                chain[0] += 1
                ins.then_inc(s["ch_d"], 1)
                dve.wait_ge(s["ch_d"], chain[0])

            def flink(ins, name, count):
                ins.then_inc(s[name], 1)
                dve.wait_ge(s[name], count)

            dve.memset(xnT[:, :, 0:1], 0.0)
            dve.wait_ge(s["rms0"], 2)
            link(dve.tensor_scalar(st_[:, 2:4], st_[:, 0:2], 1.0 / D, NORM_EPS, ALU.mult, ALU.add))
            dve.sem_inc(s["rms1"], 1)
            dve.wait_ge(s["rms0"], 3)
            link(dve.reciprocal(st_[:, 6:8], st_[:, 4:6]))
            for a in range(TT):
                dve.tensor_scalar(xin[:, a, :], xin[:, a, :], st_[:, 6 + a:7 + a], None, ALU.mult).then_inc(s["xsn"], 1)
            dve.wait_ge(s["vecT"], 1)
            flink(dve.tensor_copy(VT, banks[6][:, 0:NVEC]), "PT", 1)
            link(dve.tensor_scalar(gqk[:, 0:1], VT[:, V_QG:V_QG + 1], HD ** -0.5, None, ALU.mult))
            dve.wait_ge(s["vecmm"], 1)
            dve.tensor_tensor(R(O_B, NV, p1=H), banks[7][0:H, 0:NV], R(O_G + 384, NV, p1=H), ALU.add).then_inc(s["vec"], 1)
            for k in range(KD):
                dve.wait_ge(s["xT"], k // 2 + 1)
                dve.tensor_scalar(xnT[:, k, 1:T + 1], banks[2 + k // 2][:, T * (k % 2):T * (k % 2) + T],
                                  VT[:, V_GMIX + k:V_GMIX + k + 1], None, ALU.mult).then_inc(s["xnT"], 1)
            dve.wait_ge(s["xsplit"], 1)
            dve.wait_ge(s["xnT"], KD)
            dve.tensor_tensor(xl, xnT[:, :, 1:T + 1], xh.bitcast(F32), ALU.subtract).then_inc(s["xsplit"], 1)
            for g in range(12):
                pre_lo(dve, g, "lo_d")

            dve.wait_ge(s["projev"], 4)
            dve.wait_ge(s["lora"], 1)
            for i, t in enumerate((qb, kb)):
                tf = t.rearrange("p c t -> p (c t)")
                dve.tensor_tensor(sqb[:, i, :], tf, tf, ALU.mult).then_inc(s["sq"], 1)
            dve.wait_ge(s["ssum"], 1)
            dve.wait_ge(s["sq"], 2)
            for i in range(2):
                for j in range(2):
                    ins = dve.tensor_scalar(sqb[:, i, 512 * j:512 * j + 512], banks[2 + 2 * i + j][:, :], 1.0 / HD, QK_EPS,
                                            ALU.mult, ALU.add)
                ins.then_inc(s["qkv"], 1)
            dve.wait_ge(s["qks"], 1)
            link(dve.reciprocal(sqb, sqb))
            for i, (t, gain) in enumerate(((qb, gqk[:, 0:1]), (kb, VT[:, V_KG:V_KG + 1]))):
                tf = t.rearrange("p c t -> p (c t)")
                dve.scalar_tensor_tensor(out=tf, in0=tf, scalar=gain, in1=sqb[:, i, :], op0=ALU.mult, op1=ALU.mult)\
                   .then_inc(s["qkn"], 1)

            def hmax(h):
                dve.wait_ge(s["score"], h + 1)
                bk_ = banks[2 + h % 4]
                dve.reduce_max(mx[:, h, 0:1], bk_[:, 0:256], AX.X)
                link(dve.reduce_max(mx[:, h, 1:2], bk_[:, 256:384], AX.X))
                dve.tensor_scalar(mx[:, h, :], mx[:, h, :], -1.0, None, ALU.mult).then_inc(s["nmx"], 1)

            def hnorm(h):
                dve.wait_ge(s["prob"], 2 * h + 2)
                link(dve.reciprocal(rs[:, h, :], rs[:, h, :]))
                for q, (lo, hi) in enumerate(((0, 256), (256, 384))):
                    ins = dve.tensor_scalar(PR[:, h, lo:hi], PR[:, h, lo:hi], rs[:, h, q:q + 1], None, ALU.mult)
                ins.then_inc(s["pnorm"], 1)

            for h in range(H + 1):
                if h < H:
                    hmax(h)
                if h >= 1:
                    hnorm(h - 1)

            dve.wait_ge(s["projev"], 12)
            dve.wait_ge(s["avc"], 2)
            for p_ in pads:
                link(dve.memset(p_[:, :, 0:1], 0.0))

            def shift_mix(i, dst):
                p_ = pads[i]
                mi = (1, 0, 2)[i]
                link(dve.tensor_tensor(df, p_[:, :, 0:T], p_[:, :, 1:T + 1], ALU.subtract))
                for ct in range(CT):
                    ins = dve.scalar_tensor_tensor(out=dst[:, ct, :], in0=df[:, ct, :],
                                                   scalar=VT[:, V_MRKV + CT * mi + ct:V_MRKV + CT * mi + ct + 1],
                                                   in1=p_[:, ct, 1:T + 1], op0=ALU.mult, op1=ALU.add)
                link(ins)

            shift_mix(0, kk)
            for ct in range(CT):
                ins = dve.tensor_scalar(kn[:, ct, :], kk[:, ct, :], VT[:, V_KK + ct:V_KK + ct + 1], None, ALU.mult)
            link(ins)
            dve.tensor_tensor(nr, kn, kn, ALU.mult).then_inc(s["rk_sq"], 1)
            dve.wait_ge(s["sgm"], 8)
            for ct in range(CT):
                for c in range(2):
                    ins = dve.tensor_tensor_scan(cs[:, ct, P * c:P * c + P], ones,
                                                 Kc[:, ct, P * c:P * c + P], 0.0, ALU.mult, ALU.add)
            link(ins)
            mid = cs.rearrange("p c (b t) -> p c b t", b=2)[:, :, :, P // 2 - 1]
            dve.tensor_scalar(cb, mid, DECAY, None, ALU.mult).then_inc(s["cbias"], 1)
            dve.tensor_scalar(ncb, mid, -DECAY, None, ALU.mult).then_inc(s["cbias"], 1)
            shift_mix(2, vc)
            dve.sem_inc(s["v_ch"], 1)
            shift_mix(1, rr)
            for ct in range(CT):
                ins = dve.tensor_scalar(df[:, ct, :], Bc[:, ct, :], 1.0, VT[:, V_KA + ct:V_KA + ct + 1],
                                        ALU.subtract, ALU.mult)
            link(ins)
            link(dve.scalar_tensor_tensor(out=kk, in0=df, scalar=1.0, in1=kk, op0=ALU.add, op1=ALU.mult))
            for ct in range(CT):
                ins = dve.scalar_tensor_tensor(out=df[:, ct, :], in0=rr[:, ct, :], scalar=VT[:, V_RK + ct:V_RK + ct + 1],
                                               in1=kk[:, ct, :], op0=ALU.mult, op1=ALU.mult)
            flink(ins, "bonus", 1)
            dve.wait_ge(s["rk_nr"], 2)
            link(dve.tensor_scalar(nr, nr, 1e-12, None, ALU.max))
            link(dve.reciprocal(nr, nr))
            link(dve.tensor_tensor(kn, kn, nr, ALU.mult))
            link(dve.tensor_tensor(Bc, Bc, kn, ALU.mult))
            dve.wait_ge(s["expd"], 16)
            dve.wait_ge(s["ebc"], 2)

            def c4(t):
                return t.rearrange("p c (b t) -> p c b t", b=2)

            link(dve.tensor_tensor(sc1, st_[:, 8:12], EP[:, :, 0, P], ALU.mult))
            dve.tensor_tensor(Bc, Bc, EN, ALU.mult).then_inc(s["bk"], 1)
            dve.tensor_tensor(Kc, kk, EN, ALU.mult).then_inc(s["bk"], 1)
            for ct in range(CT):
                dve.tensor_tensor(AR[:, ct, :, 1, :], c4(rr)[:, ct], EP[:, ct, :, 1:P + 1], ALU.mult)
                ins = dve.scalar_tensor_tensor(out=AR[:, ct, :, 0, :], in0=c4(kn)[:, ct], scalar=-1.0,
                                               in1=EP[:, ct, :, 0:P], op0=ALU.mult, op1=ALU.mult)
            ins.then_inc(s["ar"], 1)
            dve.wait_ge(s["bons"], 1)
            dve.wait_ge(s["tokT"], 2)
            for i in range(2):
                ins = dve.tensor_tensor(vc[:, 2 * i:2 * i + 2, :], vc[:, 2 * i:2 * i + 2, :],
                                        banks[4 + i][:, :].rearrange("p (a t) -> p a t", a=2), ALU.mult)
            ins.then_inc(s["bonv"], 1)
            for g in range(12, 20):
                pre_lo(dve, g, "lo_d")

            for c in range(2):
                for b in range(2):
                    n = 2 * c + b
                    dve.wait_ge(s["gl"], n + 1)
                    dve.wait_ge(s["gsel"], 4 * n + 4)
                    for q in range(2):
                        v = XXo[b].rearrange("p (v q) x i -> p q v x i", q=2)[:, q, :, 0, :]
                        link(dve.tensor_tensor(v, banks[4 + q][:, 0:2 * P].rearrange("p (u i) -> p u i", u=2),
                                               bcast(cst[:, C_M0T:C_M0T + P], 1, 2), ALU.mult))
                    link(dve.tensor_tensor(XXo[b][:, :, 1, :], GRo[b][:, :, 0, :], bcast(masks[:, 0, :], 1, 4), ALU.mult))
                    for q in range(2):
                        ins = dve.tensor_tensor(XXo[b][:, :, q, :], XXo[b][:, :, q, :], bcast(ident, 1, 4), ALU.add)
                    ins.then_inc(s["x0"], 1)
                for lev in range(1, 7):
                    for b in range(2):
                        n = (c * 6 + lev - 1) * 2 + b
                        dve.wait_ge(s["dx"], n + 1)
                        dve.wait_ge(s["x0"], 2 * c + 2)
                        if n >= 2:
                            dve.wait_ge(s["xx"], n - 1)
                        for i in range(2):
                            v = XXo[b][:, 2 * i:2 * i + 2]
                            ins = dve.tensor_tensor(v, v, banks[3 * b + 1 + i][:, :].rearrange("p (u q i) -> p u q i", u=2, q=2),
                                                    ALU.add)
                        ins.then_inc(s["xx"], 1)
                if c == 0:
                    dve.wait_ge(s["st"], 1)
                    for ct in range(CT):
                        ins = dve.tensor_scalar(St[:, ct, :], banks[3][:, HD * ct:HD * ct + HD], sc1[:, ct:ct + 1], None,
                                                ALU.mult)
                    ins.then_inc(s["stc"], 1)

            dve.wait_ge(s["lnm"], 1)

            def two(i):
                return banks[i][:, :].rearrange("p (a t) -> p a t", a=2)

            for i in range(2):
                ins = dve.scalar_tensor_tensor(out=yr[:, 2 * i:2 * i + 2, :], in0=two(i), scalar=-1.0 / HD,
                                               in1=yr[:, 2 * i:2 * i + 2, :], op0=ALU.mult, op1=ALU.add)
            link(ins)
            dve.tensor_tensor(Kc, yr, yr, ALU.mult).then_inc(s["lnsq"], 1)
            dve.wait_ge(s["lnv"], 1)
            for i in range(2):
                ins = dve.tensor_scalar(Bc[:, 2 * i:2 * i + 2, :], two(2 + i), 1.0 / HD, LNX_EPS, ALU.mult, ALU.add)
            ins.then_inc(s["lnve"], 1)
            dve.wait_ge(s["lnsd"], 1)
            link(dve.reciprocal(Bc, Bc))
            link(dve.tensor_tensor(yr, yr, Bc, ALU.mult))
            for ct in range(CT):
                ins = dve.tensor_scalar(yr[:, ct, :], yr[:, ct, :], VT[:, V_LG + ct:V_LG + ct + 1],
                                        VT[:, V_LB + ct:V_LB + ct + 1], ALU.mult, ALU.add)
            link(ins)
            link(dve.tensor_tensor(yr, yr, vc, ALU.add))
            dve.wait_ge(s["gout"], 2)
            flink(dve.tensor_tensor(yr, yr, gg, ALU.mult), "yr", 1)
            dve.wait_ge(s["ysplit"], 1)
            dve.tensor_tensor(ysp[:, 1, 1], ym, ysp[:, 1, 0].bitcast(F32), ALU.subtract).then_inc(s["ysplit"], 1)
            dve.wait_ge(s["ysplit"], 3)
            dve.tensor_tensor(ysp[:, 0, 1], yr, ysp[:, 0, 0].bitcast(F32), ALU.subtract).then_inc(s["ysplit"], 1)
            for g in range(20, 22):
                pre_lo(dve, g, "lo_d")

            def mix(g):
                j, br = (g - 20) % 2, (g - 20) // 2
                for i in range(2):
                    q = 4 * j + 2 * i
                    dve.wait_ge(s["half"], g + 1)
                    src = two(2 * (g % 2) + i)
                    sig = Z[:, 8 * br + q:8 * br + q + 2, :]
                    if br == 0:
                        dve.tensor_tensor(hTm[:, q:q + 2, :], src, sig, ALU.mult).then_inc(s["hm"], 1)
                    else:
                        link(dve.tensor_tensor(Bc[:, 2 * i:2 * i + 2, :], src, sig, ALU.mult))
                        dve.wait_ge(s["hm"], 4)
                        dve.tensor_tensor(hTm[:, q:q + 2, :], hTm[:, q:q + 2, :], Bc[:, 2 * i:2 * i + 2, :], ALU.add)\
                           .then_inc(s["hm"], 1)

            mix(20)
            pre_lo(dve, 22, "lo_d")
            mix(21)
            pre_lo(dve, 23, "lo_d")
            mix(22)
            pre_lo(dve, 24, "lo_d")
            mix(23)
            pre_lo(dve, 25, "lo_d")
            dve.wait_ge(s["hsplit"], 1)
            dve.tensor_tensor(xl, hTm, xh.bitcast(F32), ALU.subtract).then_inc(s["hsplit"], 1)
            dve.wait_ge(s["xre"], 16)
            for g in range(24, 28):
                if g < 26:
                    pre_lo(dve, g + 2, "lo_d")
                dve.wait_ge(s["half"], g + 1)
                v = xrs[:, :, 256 * (g - 24):256 * (g - 23)]
                dve.tensor_tensor(v, v, two(4 + g % 2), ALU.add).then_inc(s["x2"], 1)
            dve.wait_ge(s["r2"], 2)
            link(dve.tensor_scalar(st_[:, 2:4], st_[:, 0:2], 1.0 / D, NORM_EPS, ALU.mult, ALU.add))
            dve.sem_inc(s["r2s"], 1)
            dve.wait_ge(s["r2q"], 1)
            link(dve.reciprocal(st_[:, 6:8], st_[:, 4:6]))
            dve.wait_ge(s["gbc"], 16)
            dve.wait_ge(s["x2"], 4)
            xn2 = R(O_XNT, TT, D)
            for a in range(TT):
                dve.scalar_tensor_tensor(out=xn2[:, a, :], in0=xrs[:, a, :], scalar=st_[:, 6 + a:7 + a], in1=gbc,
                                         op0=ALU.mult, op1=ALU.mult).then_inc(s["xn2"], 1)

            lg = R(O_B, 2, NG + NE)
            eg = R(O_B + 80, 2, NG)
            d21 = R(O_B + 100, 2)
            one1, one2, sel, key = (R(O_B + 128 + 64 * i, 2, NE) for i in range(4))
            lem = R(O_B + 384, 2, NE)
            cum = R(O_B + 448, 2, NE)
            sm = R(O_B + 520, 8, 2)
            ggrp = R(O_B + 540, 2, NG)
            gk = R(O_B + 550, 2, NG)
            cnt = R(O_B + 560, NE)
            descg, desce = cst[:, C_DESC:C_DESC + NG], cst[:, C_DESC + NG:C_DESC + NG + NE]
            dve.wait_ge(s["wr"], 64)
            dve.wait_ge(s["logit"], 1)
            link(dve.tensor_tensor(lg, banks[4][:, 0:2 * (NG + NE)].rearrange("p (a n) -> p a n", a=2), bcast(brc, 1, 2), ALU.add))

            def first_max(onehot, tmp, val, m_, desc, n, km):
                link(dve.tensor_reduce(m_, val, AX.X, ALU.max))
                link(dve.tensor_tensor(tmp, val, bcast(m_, 2, n), ALU.is_equal))
                link(dve.tensor_tensor(tmp, tmp, bcast(desc, 1, 2), ALU.mult))
                link(dve.tensor_reduce(km, tmp, AX.X, ALU.max))
                link(dve.tensor_tensor(onehot, tmp, bcast(km, 2, n), ALU.is_equal))

            first_max(ggrp, gk, lg[:, :, 0:NG], sm[:, 0, :], descg, NG, sm[:, 1, :])
            flink(dve.tensor_tensor(eg, lg[:, :, 0:NG], bcast(sm[:, 0, :], 2, NG), ALU.subtract), "rt", 1)
            link(dve.tensor_scalar(gk, ggrp, 1.0, BIG, ALU.subtract, ALU.mult))
            for a in range(2):
                ins = dve.tensor_tensor(lem[:, a, :].rearrange("p (g e) -> p g e", g=NG),
                                        lg[:, a, NG:NG + NE].rearrange("p (g e) -> p g e", g=NG),
                                        bcast(gk[:, a, :], 2, EG), ALU.add)
            link(ins)
            first_max(one1, key, lem, sm[:, 2, :], desce, NE, sm[:, 3, :])
            link(dve.scalar_tensor_tensor(out=lem, in0=one1, scalar=-3.0 * BIG, in1=lem, op0=ALU.mult, op1=ALU.add))
            first_max(one2, key, lem, sm[:, 4, :], desce, NE, sm[:, 5, :])
            flink(dve.tensor_tensor(d21, sm[:, 4, :], sm[:, 2, :], ALU.subtract), "rt", 2)
            flink(dve.tensor_tensor(sel, one1, one2, ALU.add), "cum", 1)
            dve.wait_ge(s["gates"], 2)
            link(dve.tensor_reduce(sm[:, 6, :], eg, AX.X, ALU.add))
            link(dve.tensor_scalar(sm[:, 7, :], d21, 1.0, None, ALU.add))
            link(dve.tensor_tensor(sm[:, 6, :], sm[:, 6, :], sm[:, 7, :], ALU.mult))
            link(dve.reciprocal(sm[:, 6, :], sm[:, 6, :]))
            dve.wait_ge(s["rte"], 16)
            dve.tensor_copy(rowv[:, :, 0, 2], sm[:, 6, :])
            dve.tensor_tensor(rowv[:, :, 1, 2], sm[:, 6, :], d21, ALU.mult)
            dve.wait_ge(s["cumd"], 1)
            link(dve.tensor_tensor(cum, banks[5][:, 0:2 * NE].rearrange("p (a n) -> p a n", a=2),
                                   bcast(cst[:, C_EB:C_EB + NE], 1, 2), ALU.add))
            for k, oh in enumerate((one1, one2)):
                link(dve.tensor_tensor(key, oh, cum, ALU.mult))
                link(dve.tensor_reduce(sm[:, k, :], key, AX.X, ALU.add))
                ins = dve.tensor_copy(addr[:, :, k].bitcast(U32), sm[:, k, :])
            ins.then_inc(s["addr"], 1)
            fl = R(O_B + 600, 3, NE, p1=1)
            fl96 = R(O_B + 600, 3 * NE, p1=1)
            inc = R(O_B + 700, 3 * NE, p1=1)
            of = R(O_B + 100 + 4, 20, p1=1)
            link(dve.tensor_copy(cnt[0:1, :], banks[5][0:1, 2 * NE:3 * NE]))
            for c in range(3):
                ins = dve.tensor_scalar(fl[:, c, :], cnt[0:1, :], S * (c + 1) + 0.5, None, ALU.is_gt)
            link(ins)
            link(dve.tensor_tensor_scan(inc, ones[0:1, 0:3 * NE], fl96, 0.0, ALU.mult, ALU.add))
            link(dve.tensor_copy(over[0:1, 0:1].bitcast(I32), inc[:, 3 * NE - 1:3 * NE]))
            link(dve.tensor_tensor(inc, inc, fl96, ALU.mult))
            for w_, (o, col) in enumerate(((1, C_UE), (9, C_UB))):
                for i in range(MAXO):
                    link(dve.tensor_scalar(fl96, inc, float(i + 1), None, ALU.is_equal))
                    link(dve.tensor_tensor(fl96, fl96, cst[0:1, col:col + 3 * NE], ALU.mult))
                    link(dve.tensor_reduce(of[:, 0:1], fl96, AX.X, ALU.add))
                    link(dve.tensor_copy(over[0:1, o + i:o + i + 1].bitcast(I32), of[:, 0:1]))
            dve.sem_inc(s["ovf"], 1)

            def xsplit(n, b):
                dve.wait_ge(s["xgT"], n + 1)
                if not isinstance(n, int) or n >= 2:
                    dve.wait_ge(s["half"], up_done(n - 2))
                src = banks[6][:, :].rearrange("p (k t) -> p k t", k=KD)
                flink(dve.tensor_copy(xsx[b][:, :, 0:S], src), "xsx", 2 * n + 1)
                dve.tensor_tensor(xsx[b][:, :, S:2 * S], src, xsx[b][:, :, 0:S].bitcast(F32), ALU.subtract)\
                   .then_inc(s["xsx"], 1)

            def fold_gate(n):
                dve.wait_ge(s["tg"], n + 1)
                dve.tensor_tensor(gf, banks[0][0:S, :], tg, ALU.add).then_inc(s["gf"], 1)

            def gated(n, b):
                dve.wait_ge(s["sg"], n + 1)
                dve.wait_ge(s["vg"], 16 * (n + 1))
                dve.scalar_tensor_tensor(out=gf, in0=gf, scalar=vgb[0:S, b, 2:3], in1=sg, op0=ALU.mult, op1=ALU.mult)\
                   .then_inc(s["m"], 1)

            def hidden(n):
                dve.wait_ge(s["tu"], n + 1)
                flink(dve.tensor_tensor(ub, banks[1][0:S, :], tu, ALU.add), "uf", n + 1)
                if not isinstance(n, int) or n >= 1:
                    dve.wait_ge(s["hT"], n)
                dve.wait_ge(s["m"], n + 1)
                dve.tensor_tensor(hb, ub, gf, ALU.mult).then_inc(s["h"], 1)

            def hsplit(n, late=False):
                dve.wait_ge(s["hT"], n + 1)
                if not isinstance(n, int) or n >= 1:
                    dve.wait_ge(s["half"], down_done(n - 1, 1, late))
                src = banks[7][:, 0:256].rearrange("p (k t) -> p k t", k=4)
                flink(dve.tensor_copy(xsh[:, :, 0:S], src), "hs", 2 * n + 1)
                dve.tensor_tensor(xsh[:, :, S:2 * S], src, xsh[:, :, 0:S].bitcast(F32), ALU.subtract)\
                   .then_inc(s["hs"], 1)

            def fold_down(n, b, j):
                dve.wait_ge(s["ty"], 2 * n + j + 1)
                if j == 0 and (not isinstance(n, int) or n >= 2):
                    dve.wait_ge(s["sc"], 16 * (n - 1))
                dve.tensor_tensor(ysb[b][:, j, :], banks[2 + j][0:S, :], ty, ALU.add).then_inc(s["y_"], 1)

            dve.wait_ge(s["half"], 2 * PRE)
            xsplit(0, 0)
            for i in range(4):
                first_lo(dve, i, "lo_d")
            fold_gate(0)

            def step(n, n0, head=False, tail=False):
                b = n0 % 2
                moe_lo(dve, n, n0, 0, "lo_d")
                gated(n - 1, 1 - b)
                if not head:
                    fold_down(n - 2, b, 1)
                moe_lo(dve, n, n0, 1, "lo_d")
                moe_lo(dve, n, n0, 2, "lo_d")
                hidden(n - 1)
                moe_lo(dve, n, n0, 3, "lo_d")
                hsplit(n - 1)
                if not tail:
                    xsplit(n + 1, 1 - b)
                moe_lo(dve, n, n0, 4, "lo_d")
                fold_gate(n)
                moe_lo(dve, n, n0, 5, "lo_d")
                fold_down(n - 1, 1 - b, 0)

            xsplit(1, 1)
            step(1, 1, head=True)
            with dve.Fori(0, (NE - 4) // 2) as it:
                for j in range(2):
                    step(2 * it + 2 + j, 2 + j)
            step(NE - 2, NE - 2)
            step(NE - 1, NE - 1, tail=True)
            last_lo(dve, 0, "lo_d")
            gated(NE - 1, 1)
            fold_down(NE - 2, 0, 1)
            last_lo(dve, 1, "lo_d")
            hidden(NE - 1)
            hsplit(NE - 1)
            fold_down(NE - 1, 1, 0)
            fold_down(NE - 1, 1, 1)

            n_over = over_count(dve)
            with dve.If(n_over > 0):
                with dve.Fori(0, n_over) as i:
                    n = NE + i
                    xsplit(n, 0)
                    for q in range(3):
                        over_lo(dve, i, q, "lo_d")
                    fold_gate(n)
                    gated(n, 0)
                    for q in range(3, 6):
                        over_lo(dve, i, q, "lo_d")
                    hidden(n)
                    hsplit(n, late=True)
                    dve.wait_ge(s["sc"], 16 * n)
                    for j in range(2):
                        dve.wait_ge(s["ty"], 2 * n + j + 1)
                        dve.tensor_tensor(ysb[0][:, j, :], banks[2 + j][0:S, :], ty, ALU.add).then_inc(s["y_"], 1)

            dve.wait_ge(s["ychunk"], 32)
            link(dve.tensor_tensor(xrs, xrs, yall[:, :, 0:D], ALU.add))
            dve.tensor_tensor(xrs, xrs, yall[:, :, D:2 * D], ALU.add).then_inc(s["fin"], 1)

        @block.tensor
        def _(pe):
            pe.wait_ge(s["consts"], 16)
            pe.wait_ge(s["vecs"], 16 * 14)
            pe.transpose(banks[6][:, 0:NVEC], R(O_K, P, p1=NVEC), ident[0:NVEC, 0:NVEC]).then_inc(s["vecT"], 1)
            pe.wait_ge(s["biasc"], 48)
            pe.matmul(banks[7][0:H, 0:NV], R(O_G + 768, H, p1=32), R(O_G, NV, p1=32), start=True, stop=True)\
              .then_inc(s["vecmm"], 1)
            pe.wait_ge(s["xsn"], TT)
            for q in range(4):
                for k in (2 * q, 2 * q + 1):
                    for a in range(TT):
                        o = T * (k % 2) + P * a
                        ins = pe.transpose(banks[2 + q][:, o:o + P], xin[:, a, P * k:P * k + P], ident)
                ins.then_inc(s["xT"], 1)

            def passes(bank_ap, stat, mov, first, last, fresh):
                for i, (a, b) in enumerate(((0, 0), (0, 1), (1, 0))):
                    ins = pe.matmul(bank_ap, stat[a], mov[b], start=(first and i == 0 and fresh),
                                    stop=(last and i == 2), skip_group_check=True)
                return ins

            def ready(g):
                pe.wait_ge(s["lo_d"], g + 1)
                pe.wait_ge(s["lo_p"], g + 1)

            for g in range(12):
                ready(g)
                if g == 0:
                    pe.wait_ge(s["xsplit"], 2)
                if g >= 2:
                    pe.wait_ge(s["projev"], g - 1)
                h_, l_ = part_view(wh, g % NB, "cols"), part_view(wl, g % NB, "cols")
                for a in range(2):
                    for k in range(KD):
                        ins = passes(banks[g % 2][:, T * a:T * a + T],
                                     (h_[:, k, P * a:P * a + P], l_[:, k, P * a:P * a + P]),
                                     (xh[:, k, :], xl[:, k, :]), k == 0, k == KD - 1, True)
                ins.then_inc(s["half"], 1)

            pe.wait_ge(s["musplit"], 1)
            for a in range(2):
                for k in range(KD):
                    pe.matmul(banks[2][:, T * a:T * a + T], WL[:, k, P * a:P * a + P], xnT[:, k, 1:T + 1],
                              start=(k == 0), stop=False)
                    ins = pe.matmul(banks[2][:, T * a:T * a + T], WM[:, k, P * a:P * a + P], xnT[:, k, 0:T],
                                    start=False, stop=(k == KD - 1))
            ins.then_inc(s["lora"], 1)
            pe.wait_ge(s["lt"], 3)
            pe.wait_ge(s["lora2"], 48)
            pe.wait_ge(s["vec"], 1)
            lt = R(O_V, 2, T)
            w2s = R(O_YR, CW)
            g2s = R(O_YR + CW, CW)
            for ct in range(CT):
                o = T * (ct % 2)
                pe.matmul(banks[3 + ct // 2][:, o:o + T], w2s[0:64, P * ct:P * ct + P], lt[0:64, 0, :], start=True, stop=True)
                pe.matmul(banks[5 + ct // 2][:, o:o + T], w2s[64:128, P * ct:P * ct + P], lt[64:128, 0, :],
                          start=True, stop=True)
                ins = pe.matmul(banks[(7, 2)[ct // 2]][:, o:o + T], g2s[:, P * ct:P * ct + P], lt[:, 1, :], start=True, stop=True)
            ins.then_inc(s["loraout"], 1)

            pe.wait_ge(s["sq"], 2)
            pe.wait_ge(s["sgm"], 8)
            pe.wait_ge(s["gout"], 2)
            for i in range(2):
                for j in range(2):
                    ins = pe.matmul(banks[2 + 2 * i + j][:, :], bones, sqb[:, i, 512 * j:512 * j + 512], start=True, stop=True)
            ins.then_inc(s["ssum"], 1)
            pe.wait_ge(s["projev"], 6)
            for a in range(TT):
                for ct in range(CT):
                    ins = pe.transpose(banks[6 + a][:, P * ct:P * ct + P], ym[:, ct, P * a:P * a + P], ident)
                ins.then_inc(s["vtT"], 1)

            def heads_of(h):
                return slice(HD * (h % 2), HD * (h % 2) + HD), h // 2

            def scores(h):
                hp, ct = heads_of(h)
                if h < 4:
                    pe.wait_ge(s["qkv"], 2)
                    pe.wait_ge(s["qkn"], 2)
                    pe.wait_ge(s["hank"], 16)
                else:
                    pe.wait_ge(s["prob"], 2 * (h - 4) + 2)
                bk_ = banks[2 + h % 4]
                pe.matmul(bk_[:, 0:256], JJ, HK[:, h, :], start=True, stop=False)
                pe.matmul(bk_[:, 0:256], qb[hp, ct, P:T], kb[hp, ct, :], start=False, stop=True)
                pe.matmul(bk_[:, 256:384], JJ, HK[:, h, P:2 * P], start=True, stop=False)
                pe.matmul(bk_[:, 256:384], qb[hp, ct, 0:P], kb[hp, ct, 0:P], start=False, stop=True)\
                  .then_inc(s["score"], 1)

            def turn(h):
                pe.wait_ge(s["pnorm"], h + 1)
                if h >= 2:
                    pe.wait_ge(s["pTc"], h - 1)
                else:
                    pe.wait_ge(s["projev"], 12)
                for a in range(3):
                    ins = pe.transpose(banks[h % 2][:, P * a:P * a + P], PR[:, h, P * a:P * a + P], ident)
                ins.then_inc(s["pT"], 1)

            def values(h):
                hp, ct = heads_of(h)
                pe.wait_ge(s["pTc"], h + 1)
                if h == 0:
                    pe.wait_ge(s["vtok"], 2)
                o = banks[6 + ct // 2]
                c0 = T * (ct % 2)
                pe.matmul(o[hp, c0:c0 + P], vtm[:, 0, HD * h:HD * h + HD], PT_[:, h, 2, :], start=True, stop=True)
                pe.matmul(o[hp, c0 + P:c0 + T], vtm[:, 0, HD * h:HD * h + HD], PT_[:, h, 0, :], start=True, stop=False)
                return pe.matmul(o[hp, c0 + P:c0 + T], vtm[:, 1, HD * h:HD * h + HD], PT_[:, h, 1, :], start=False, stop=True)

            for h in range(4):
                scores(h)
            for h in range(H):
                turn(h)
                if h + 4 < H:
                    scores(h + 4)
                if h >= 1:
                    values(h - 1)
            values(H - 1).then_inc(s["av"], 1)

            pe.wait_ge(s["rk_sq"], 1)
            for i in range(2):
                ins = pe.matmul(banks[2 + i][:, :], bones, nr.rearrange("p c t -> p (c t)")[:, 512 * i:512 * i + 512],
                                start=True, stop=True)
            ins.then_inc(s["rk_ss"], 1)
            pe.wait_ge(s["bonus"], 1)
            for i in range(2):
                ins = pe.matmul(banks[4 + i][:, :], bones, df.rearrange("p c t -> p (c t)")[:, 512 * i:512 * i + 512],
                                start=True, stop=True)
            ins.then_inc(s["bons"], 1)
            pe.wait_ge(s["avc"], 2)
            for i in range(6):
                if i == 0:
                    pe.wait_ge(s["v_ch"], 1)
                if i == 2:
                    pe.wait_ge(s["bk"], 2)
                if i >= 2:
                    pe.wait_ge(s["tok"], i - 1)
                for ct in range(CT):
                    src = (vc, Bc, Kc)[i // 2]
                    ins = pe.transpose(banks[6 + i % 2][:, P * ct:P * ct + P], src[:, ct, P * (i % 2):P * (i % 2) + P], ident)
                ins.then_inc(s["tokT"], 1)
            for g in range(12, 20):
                ready(g)
                if g >= 14:
                    pe.wait_ge(s["projev"], g - 1)
                else:
                    pe.wait_ge(s["pTc"], H)
                h_, l_ = part_view(wh, g % NB, "cols"), part_view(wl, g % NB, "cols")
                for a in range(2):
                    for k in range(KD):
                        ins = passes(banks[g % 2][:, T * a:T * a + T],
                                     (h_[:, k, P * a:P * a + P], l_[:, k, P * a:P * a + P]),
                                     (xh[:, k, :], xl[:, k, :]), k == 0, k == KD - 1, True)
                ins.then_inc(s["half"], 1)

            pe.wait_ge(s["ar"], 1)
            pe.wait_ge(s["projev"], 20)
            pe.wait_ge(s["rk_nr"], 2)
            pe.wait_ge(s["bonv"], 1)
            for c in range(2):
                tok = slice(P * c, P * c + P)
                if c == 1:
                    pe.wait_ge(s["yc"], 1)
                    pe.wait_ge(s["stc"], 1)
                for b in range(2):
                    if b == 1:
                        pe.wait_ge(s["x0"], 2 * c + 1)
                    for u in range(4):
                        hp, ct = heads_of(4 * b + u)
                        if b == 1:
                            pe.wait_ge(s["gcp"], 8 * c + u + 1)
                        ar = AR[hp, ct, c].rearrange("p a i -> p (a i)")
                        pe.matmul(banks[u][:, 0:256], Bc[hp, ct, tok], ar, start=True, stop=True)
                        pe.matmul(banks[u][:, 256:512], Kc[hp, ct, tok], ar, start=True, stop=True).then_inc(s["gram"], 1)
                        ins = pe.matmul(banks[4 + u % 2][:, P * (u // 2):P * (u // 2) + P], AR[hp, ct, c, 0, :], Bc[hp, ct, tok],
                                        start=True, stop=True)
                    ins.then_inc(s["gl"], 1)
                for lev in range(1, 7):
                    for b in range(2):
                        n = (c * 6 + lev - 1) * 2 + b
                        pe.wait_ge(s["nt"], n + 1)
                        pe.wait_ge(s["x0"], 2 * c + 2)
                        if n >= 2:
                            pe.wait_ge(s["xx"], n - 1)
                            pe.wait_ge(s["t1c"], n - 1)
                        if lev == 1:
                            pe.wait_ge(s["gcp"], 8 * c + 8)
                        for u in range(4):
                            ins = pe.matmul(banks[3 * b][:, P * u:P * u + P], NTo[b][:, u, :], XXo[b][:, u, 0, :],
                                            start=True, stop=True)
                        ins.then_inc(s["t1"], 1)
                    for b in range(2):
                        n = (c * 6 + lev - 1) * 2 + b
                        pe.wait_ge(s["t1c"], n + 1)
                        for u in range(4):
                            o = banks[3 * b + 1 + u // 2]
                            c0 = 256 * (u % 2)
                            pe.matmul(o[:, c0:c0 + P], XXo[b][:, u, 1, :], T1o[b][:, u, :], start=True, stop=True)
                            ins = pe.matmul(o[:, c0 + P:c0 + 2 * P], T1o[b][:, u, :], XXo[b][:, u, 1, :],
                                            start=True, stop=True)
                        ins.then_inc(s["dx"], 1)
                pe.wait_ge(s["xx"], 12 * c + 12)
                if c == 0:
                    pe.wait_ge(s["tok"], 6)
                for h in range(H):
                    hp, ct = heads_of(h)
                    v_ = Vtok[:, c, HD * h:HD * h + HD]
                    zo = banks[3 * (h % 2)][:, HD * ct:HD * ct + HD]
                    ins = pe.matmul(zo, GRo[h // 4][:, h % 4, 2, :], v_, start=True, stop=(c == 0))
                    if c == 1:
                        ins = pe.matmul(zo, AR[hp, ct, 1, 0, :], St[hp, ct, :], start=False, stop=True)
                ins.then_inc(s["z"], 1)
                pe.wait_ge(s["zc"], 2 * c + 2)
                for h in range(H):
                    ins = pe.matmul(banks[1][:, HD * h:HD * h + HD], XXo[h // 4][:, h % 4, 1, :],
                                    Zb[:, HD * h:HD * h + HD], start=True, stop=True)
                ins.then_inc(s["u"], 1)
                pe.wait_ge(s["uc"], c + 1)
                if c == 0:
                    for h in range(H):
                        hp, ct = heads_of(h)
                        so = banks[3][hp, HD * ct:HD * ct + HD]
                        pe.matmul(so, Btok[:, 0, HD * h:HD * h + HD], Ub[:, HD * h:HD * h + HD], start=True, stop=False)
                        ins = pe.matmul(so, Ktok[:, 0, HD * h:HD * h + HD], Vtok[:, 0, HD * h:HD * h + HD],
                                        start=False, stop=True)
                    ins.then_inc(s["st"], 1)
                for h in range(H):
                    hp, ct = heads_of(h)
                    yo = banks[2][hp, P * ct:P * ct + P]
                    G_ = GRo[h // 4][:, h % 4]
                    pe.matmul(yo, Vtok[:, c, HD * h:HD * h + HD], G_[:, 3, :], start=True, stop=False)
                    ins = pe.matmul(yo, Ub[:, HD * h:HD * h + HD], G_[:, 1, :], start=False, stop=(c == 0))
                    if c == 1:
                        ins = pe.matmul(yo, St[hp, ct, :], AR[hp, ct, 1, 1, :], start=False, stop=True)
                ins.then_inc(s["y"], 1)

            pe.wait_ge(s["yc"], 2)
            yf, kf = yr.rearrange("p c t -> p (c t)"), Kc.rearrange("p c t -> p (c t)")
            for i in range(2):
                ins = pe.matmul(banks[i][:, :], bones, yf[:, 512 * i:512 * i + 512], start=True, stop=True)
            ins.then_inc(s["lnm"], 1)
            pe.wait_ge(s["lnsq"], 1)
            for i in range(2):
                ins = pe.matmul(banks[2 + i][:, :], bones, kf[:, 512 * i:512 * i + 512], start=True, stop=True)
            ins.then_inc(s["lnv"], 1)

            pe.wait_ge(s["lnve"], 1)
            pe.wait_ge(s["ysplit"], 4)
            for g in range(20, 24):
                ready(g)
                if g >= 22:
                    pe.wait_ge(s["hm"], 2 * (g - 21))
                br = (g - 20) // 2
                h_, l_ = part_view(wh, g % NB, "br"), part_view(wl, g % NB, "br")
                for q in range(4):
                    for k in range(CT):
                        ins = passes(banks[2 * (g % 2) + q // 2][:, T * (q % 2):T * (q % 2) + T],
                                     (h_[:, k, P * q:P * q + P], l_[:, k, P * q:P * q + P]),
                                     (ysp[:, br, 0, k, :], ysp[:, br, 1, k, :]), k == 0, k == CT - 1, True)
                ins.then_inc(s["half"], 1)
            pe.wait_ge(s["hsplit"], 2)
            for g in range(24, 28):
                ready(g)
                if g >= 26:
                    pe.wait_ge(s["x2"], g - 25)
                h_, l_ = part_view(wh, g % NB, "cols"), part_view(wl, g % NB, "cols")
                for a in range(TT):
                    tk = slice(P * a, P * a + P)
                    for k in range(KD):
                        ins = passes(banks[4 + g % 2][:, T * a:T * a + T], (xh[:, k, tk], xl[:, k, tk]),
                                     (h_[:, k, :], l_[:, k, :]), k == 0, k == KD - 1, True)
                ins.then_inc(s["half"], 1)

            pe.wait_ge(s["xn2"], TT)
            xn2 = R(O_XNT, TT, D)
            for q in range(4):
                for k in (2 * q, 2 * q + 1):
                    for a in range(TT):
                        o = T * (k % 2) + P * a
                        ins = pe.transpose(banks[q][:, o:o + P], xn2[:, a, P * k:P * k + P], ident)
                ins.then_inc(s["xn2T"], 1)
            pe.wait_ge(s["xn2Tc"], 4)
            pe.wait_ge(s["wr"], 64)
            pe.wait_ge(s["x2"], 4)
            NR_ = NG + NE
            for a in range(TT):
                for k in range(KD):
                    ins = pe.matmul(banks[4][:, NR_ * a:NR_ * a + NR_], hTm[:, k, P * a:P * a + P], Wr[:, k, :],
                                    start=(k == 0), stop=(k == KD - 1))
            ins.then_inc(s["logit"], 1)
            pe.wait_ge(s["cum"], 1)
            sel = R(O_B + 256, 2, NE)
            pe.matmul(banks[5][:, 0:NE], tri, sel[:, 0, :], start=True, stop=True)
            pe.matmul(banks[5][:, NE:2 * NE], tri, sel[:, 1, :], start=True, stop=False)
            pe.matmul(banks[5][:, NE:2 * NE], ones, sel[:, 0, :], start=False, stop=True)
            pe.matmul(banks[5][:, 2 * NE:3 * NE], ones, sel[:, 0, :], start=True, stop=False)
            pe.matmul(banks[5][:, 2 * NE:3 * NE], ones, sel[:, 1, :], start=False, stop=True).then_inc(s["cumd"], 1)

            def turn_x(n, b):
                pe.wait_ge(s["xg"], 16 * (n + 1))
                if not isinstance(n, int) or n >= 1:
                    pe.wait_ge(s["xsx"], 2 * n)
                pe.nop(nofuse=True)
                v = xg[b].rearrange("p (q k) -> p q k", k=KD)
                for k in range(KD):
                    ins = pe.transpose(banks[6][:, S * k:S * k + S], v[:, :, k], ident[0:S, 0:S])
                ins.then_inc(s["xgT"], 1)

            def wide(bank_i, stat, buf, k0, first, last):
                h_, l_ = part_view(wh, buf, "rows"), part_view(wl, buf, "rows")
                for k in range(4):
                    pe.matmul(banks[bank_i][:, :], stat[:, k0 + k, :], h_[:, k, :], start=(first and k == 0), stop=False)
                    ins = pe.matmul(banks[bank_i][:, :], stat[:, k0 + k, :], l_[:, k, :], start=False,
                                    stop=(last and k == 3))
                return ins

            def gate_half(n, b, g, buf, j):
                ready(g)
                if j == 0:
                    pe.wait_ge(s["xsx"], 2 * n + 2)
                    if not isinstance(n, int) or n >= 1:
                        pe.wait_ge(s["gf"], n)
                ins = wide(0, xsx[b], buf, 4 * j, j == 0, j == 1)
                ins.then_inc(s["half"], 1)

            def up_half(n, b, g, buf, j):
                ready(g)
                if j == 0 and (not isinstance(n, int) or n >= 1):
                    pe.wait_ge(s["uf"], n)
                ins = wide(1, xsx[b], buf, 4 * j, j == 0, j == 1)
                ins.then_inc(s["half"], 1)

            def turn_h(n):
                pe.wait_ge(s["h"], n + 1)
                if not isinstance(n, int) or n >= 1:
                    pe.wait_ge(s["hs"], 2 * n)
                pe.nop(nofuse=True)
                v = hb.rearrange("p (q k) -> p q k", k=4)
                for k in range(4):
                    ins = pe.transpose(banks[7][:, S * k:S * k + S], v[:, :, k], ident[0:S, 0:S])
                ins.then_inc(s["hT"], 1)

            def down_half(n, g, buf, j):
                ready(g)
                if j == 0:
                    pe.wait_ge(s["hs"], 2 * n + 2)
                if not isinstance(n, int) or n >= 1:
                    pe.wait_ge(s["y_"], 2 * n - 1 + j)
                ins = wide(2 + j, xsh, buf, 0, True, True)
                ins.then_inc(s["half"], 1)

            turn_x(0, 0)
            for j in range(2):
                gate_half(0, 0, 2 * PRE + j, (2 * PRE + j) % NB, j)
            turn_x(1, 1)
            for j in range(2):
                up_half(0, 0, 2 * PRE + 2 + j, (2 * PRE + 2 + j) % NB, j)

            def step(n, n0, tail=False):
                b = n0 % 2
                place = [moe_place(n0, i)[0] for i in range(6)]
                for j in range(2):
                    gate_half(n, b, moe_half(n, j), place[j], j)
                turn_h(n - 1)
                if not tail:
                    turn_x(n + 1, 1 - b)
                for j in range(2):
                    down_half(n - 1, moe_half(n, 2 + j), place[2 + j], j)
                for j in range(2):
                    up_half(n, b, moe_half(n, 4 + j), place[4 + j], j)

            step(1, 1)
            with pe.Fori(0, (NE - 4) // 2) as it:
                for j in range(2):
                    step(2 * it + 2 + j, 2 + j)
            step(NE - 2, NE - 2)
            step(NE - 1, NE - 1, tail=True)
            turn_h(NE - 1)
            for j in range(2):
                g = 2 * PRE + 2 * LAST + j
                down_half(NE - 1, g, g % NB, j)

            n_over = over_count(pe)
            with pe.If(n_over > 0):
                with pe.Fori(0, n_over) as i:
                    n = NE + i
                    turn_x(n, 0)
                    for j in range(2):
                        gate_half(n, 0, over_half(i, j), (2 * PRE + j) % NB, j)
                    for j in range(2):
                        up_half(n, 0, over_half(i, 2 + j), (2 * PRE + 2 + j) % NB, j)
                    turn_h(n)
                    for j in range(2):
                        down_half(n, over_half(i, 4 + j), (2 * PRE + 4 + j) % NB, j)


_INS = ['x', 'norm_mix_g', 'norm_ffn_g', 'w_in', 'mu_rkv', 'mu_x', 'w0', 'w1', 'w2', 'a0', 'a1', 'a2', 'g1', 'g2',
        'k_k', 'k_a', 'r_k', 'lnx_g', 'lnx_b', 'q_gain', 'k_gain', 'rel_bias', 'w_br_rwkv', 'w_br_moba', 'w_out',
        'w_grp', 'b_grp', 'w_exp', 'b_exp', 'w_gate', 'w_up', 'w_down']


def shape_constants():
    import math

    import numpy as np
    i = np.arange(P)
    c = np.zeros((P, NCONST), np.float32)
    c[:, C_ID:C_ID + P] = np.eye(P)
    c[:, C_BO:C_BO + P] = (i[:, None] // HD == i[None, :] // HD)
    for lev in range(7):
        half = 1 << lev
        m = (i[:, None] // (2 * half) == i[None, :] // (2 * half)) & (i[:, None] % (2 * half) < half) \
            & (i[None, :] % (2 * half) >= half)
        c[:, C_MK + lev * P:C_MK + (lev + 1) * P] = m
    c[:, C_TRI:C_TRI + P] = i[:, None] < i[None, :]
    c[:, C_ONE:C_ONE + P] = 1
    c[:, C_DESC:C_DESC + NG] = np.arange(NG, 0, -1)
    c[:, C_DESC + NG:C_DESC + NG + NE] = np.arange(NE, 0, -1)
    c[:, C_EB:C_EB + NE] = T * np.arange(NE)
    e = np.tile(np.arange(NE), 3)
    c[:, C_UE:C_UE + 3 * NE] = e
    c[:, C_UB:C_UB + 3 * NE] = e * NC + 1 + np.arange(3 * NE) // NE
    c[:, C_M0T:C_M0T + P] = c[:, C_MK:C_MK + P].T
    bc_ = np.zeros((P, 896), np.float32)
    for m in range(NV):
        n = T - 1 - m
        if n < 0:
            bc_[:, 384 + m] = -BIG
            continue
        if n < 16:
            b = n
        else:
            b = min(31, 16 + int(np.float32(np.log(np.float32(n) / np.float32(16))) / np.float32(math.log(8)) * np.float32(16)))
        bc_[b, m] = 1
    bc_[:, 768:896] = np.eye(P)[::-1]
    rows = np.zeros((P, 2, 2, 4), np.int32)
    for a in range(2):
        for k in range(2):
            rows[:, a, k, 0] = P * a + i
            rows[:, a, k, 1] = 2 * (P * a + i) + k
    return c, bc_, rows.reshape(P, 16)


def kernel(**inputs):
    import numpy as _np
    import concourse.bacc as _bacc
    from concourse import mybir as _mybir
    from concourse.bass_utils import run_bass_kernel_spmd as _run

    nc = _bacc.Bacc("TRN2", target_bir_lowering=False, num_devices=1)
    arrays, args = {}, []

    def give(name, a):
        arrays[f"in_{name}_dram"] = a
        args.append(nc.dram_tensor(f"in_{name}_dram", a.shape, _mybir.dt.from_np(a.dtype), kind="ExternalInput").ap())

    for name in _INS:
        give(name, _np.ascontiguousarray(inputs[name]))
    for name, a in zip(("consts", "bias_consts", "slot_rows"), shape_constants()):
        give(name, a)
    args.append(nc.dram_tensor("out_0_dram", (1, T, D), _mybir.dt.float32, kind="ExternalOutput").ap())
    build(nc, *args)
    r = _run(nc, [arrays], core_ids=[0])
    return r.results[0]["out_0_dram"]
```

```python
from contextlib import ExitStack

import concourse.bass as bass
from concourse import mybir

F32 = mybir.dt.float32
F32R = mybir.dt.float32r
I32 = mybir.dt.int32
U32 = mybir.dt.uint32
ALU = mybir.AluOpType
ACT = mybir.ActivationFunctionType
AX = mybir.AxisListType

P = 128
T, D = 256, 1024
TT, KD = T // P, D // P
CW = 512
CT = CW // P
H, HD = 8, 64
NG, EG = 4, 8
NE = NG * EG
FE = 512
S = 64
NC = T // S
MAXO = 2 * T // (S + 1)
NV = 2 * T - 129
DECAY = 0.6065306597126334
NORM_EPS, LNX_EPS = 1e-6, 64e-5
BIG = 1e30

CHUNK = 4096
HALF = CHUNK // 2
NB = 3
NS = 6
PRE = 14
PCH = [CW, 0, 2 * CW, 3 * CW, 4 * CW, 5 * CW] + [6 * CW + CW * i for i in range(4)]

C_ID, C_BO, C_MK, C_TRI, C_ONE = 0, 128, 256, 256 + 7 * 128, 256 + 8 * 128
C_DESC = C_ONE + 128
C_EB = C_DESC + NG + NE
C_IP = C_EB + NE
C_UE = C_IP + 8
C_UB = C_UE + 3 * NE
C_M0T = C_UB + 3 * NE
C_EPS = C_M0T + P
NCONST = C_EPS + 2
V_GMIX, V_MRKV, V_MX, V_W0, V_A0, V_KK, V_KA, V_RK, V_LG, V_LB, V_QG, V_KG = 0, 8, 20, 44, 48, 52, 56, 60, 64, 68, 72, 73
NVEC = 74


def bcast(ap, axis, n):
    dims = [list(d) for d in ap.ap]
    dims.insert(axis, [0, n])
    return bass.AP(ap.tensor, ap.offset, dims)


def build(nc, x, norm_mix_g, norm_ffn_g, w_in, mu_rkv, mu_x, w0, w1, w2, a0, a1, a2, g1, g2, k_k, k_a, r_k,
          lnx_g, lnx_b, q_gain, k_gain, rel_bias, w_br_rwkv, w_br_moba, w_out, w_grp, b_grp, w_exp, b_exp,
          w_gate, w_up, w_down, consts, bias_consts, slot_rows, out):
    with ExitStack() as ctx:
        def sb(name, shape, dt=F32):
            return ctx.enter_context(nc.sbuf_tensor(name, shape, dt))

        ring = sb("ring", [P, NS, CHUNK])
        wh = sb("wh", [P, NB, HALF], F32R)
        wl = sb("wl", [P, NB, HALF], F32R)
        xs = sb("xs", [P, 4096], F32R)
        reg = sb("reg", [P, 12248])
        banks = [ctx.enter_context(nc.psum_tensor(f"bank{i}", [P, 512], F32)) for i in range(8)]

        sem_names = (
            "consts vecs lora_w lora2 biasc xin xre "
            "rms0 rms1 xsn vecT PT xT xnT xsplit musplit "
            "hi lo_d lo_p half projev "
            "prefill prefset vecmm vec vecst hank lora lt sgm loraout gout "
            "sq ssum qkv qks qkn vtT vtok score nmx prob pnorm pT pTc av avc "
            "rk_sq rk_ss rk_nr cs cbias ebc expd ar bk bonus bons bonv tokT tok v_ch "
            "gram gcp gsel gl x0 nt t1 t1c dx xx z zc u uc y yc st stc st1 "
            "lnm lnc lnsq lnv lnve lnsd yr ysplit ylo "
            "hm hsplit x2 r2 r2s r2q xn2 gbc xn2st xn2T xn2Tc wr logit rt rte cum cumd gates addr lists ovf zero "
            "tidx vg xg xgT xsx tg gf sg m tu uf h hT hs ty y_ sc "
            "ychunk fin out ch_d ch_a ch_p"
        ).split()
        s = {n: ctx.enter_context(nc.semaphore("s_" + n)) for n in sem_names}
        pre_in = [ctx.enter_context(nc.semaphore(f"s_pre{i}")) for i in range(2)]
        slot_in = [ctx.enter_context(nc.semaphore(f"s_slot{i}")) for i in range(NS)]

        bias_rows = nc.dram_tensor("bias_rows", [H, 384], F32).ap()
        xn2_dram = nc.dram_tensor("xn2_rows", [T, D], F32).ap()
        lists = nc.dram_tensor("slot_lists", [NE * T, 4], F32).ap()
        y_dram = nc.dram_tensor("expert_rows", [2 * T, D], F32).ap()

        def R(off, *dims, p0=0, p1=P):
            n = 1
            for d in dims:
                n *= d
            v = reg[p0:p1, off:off + n]
            if len(dims) == 2:
                return v.rearrange("p (a b) -> p a b", a=dims[0])
            if len(dims) == 3:
                return v.rearrange("p (a b c) -> p a b c", a=dims[0], b=dims[1])
            if len(dims) == 4:
                return v.rearrange("p (a b c d) -> p a b c d", a=dims[0], b=dims[1], c=dims[2])
            return v

        flat = ring[:, :, :].rearrange("p s n -> p (s n)")

        def A(off, *dims, p0=0, p1=P):
            n = 1
            for d in dims:
                n *= d
            o = 2 * CHUNK + off
            v = flat[p0:p1, o:o + n]
            if len(dims) == 2:
                return v.rearrange("p (a b) -> p a b", a=dims[0])
            if len(dims) == 3:
                return v.rearrange("p (a b c) -> p a b c", a=dims[0], b=dims[1])
            if len(dims) == 4:
                return v.rearrange("p (a b c d) -> p a b c d", a=dims[0], b=dims[1], c=dims[2])
            return v

        cst = R(0, NCONST)
        ident, bones, tri, ones = (cst[:, o:o + P] for o in (C_ID, C_BO, C_TRI, C_ONE))
        masks = cst[:, C_MK:C_MK + 7 * P].rearrange("p (l n) -> p l n", l=7)
        VT = R(NCONST, NVEC)
        SM = NCONST + NVEC
        st_ = R(SM, 16)
        mx = R(SM + 16, H, 2)
        rs = R(SM + 32, H, 2)
        cb = R(SM + 48, CT, 2)
        ncb = R(SM + 56, CT, 2)
        sc1 = R(SM + 64, CT)
        gqk = R(SM + 68, 2)
        tidx = R(SM + 72, 2, 4)
        vgb = R(SM + 16, 2, 4)
        over = R(SM + 80, 20)
        rowv = R(SM + 100, 2, 2, 4)
        addr = R(SM + 116, 2, 2)
        assert SM + 120 <= 2000
        eps, lnx_eps = (cst[:, C_EPS + i:C_EPS + i + 1] for i in range(2))
        O_XNT, O_AR, O_B, O_K, O_V, O_G, O_YR, O_YM = 2000, 4056, 6104, 7128, 8152, 9176, 10200, 11224
        xnT = R(O_XNT, KD, T + 1)
        xin = R(O_AR, TT, D)
        xrs = R(O_V, TT, D)
        AR = R(O_AR, CT, 2, 2, P)
        Bc = R(O_B, CT, T)
        Kc = R(O_K, CT, T)
        vc = R(O_V, CT, T)
        gg = R(O_G, CT, T)
        yr = R(O_YR, CT, T)
        ym = R(O_YM, CT, T)
        assert O_YM + 1024 <= 12248
        HK = R(O_XNT, H, 256)

        df, rr, kk, kn, nr = (A(1024 * i, CT, T) for i in range(5))
        EP = A(5120, CT, 2, P + 1)
        EN, cs = A(6160, CT, T), A(7184, CT, T)
        pads = [A(8208 + i * CT * (T + 1), CT, T + 1) for i in range(3)]
        sent = A(11296, NE * T * 4 // P).bitcast(I32)
        JJ = A(11552, P)
        GRo = [A(4608 * b, 4, 4, P) for b in range(2)]
        XXo = [A(4608 * b + 2048, 4, 2, P) for b in range(2)]
        NTo = [A(4608 * b + 3072, 4, P) for b in range(2)]
        T1o = [A(4608 * b + 3584, 4, P) for b in range(2)]
        Zb, Ub = A(4096, CW), A(8704, CW)
        Btok, Ktok, Vtok = A(9216, CW), A(9728, CW), A(10240, 2, CW)
        yraw = AR[:, :, :, 0, :]
        St = AR[:, :, 0, 1, 0:HD]

        WL, WM = A(3 * CHUNK, KD, 256), A(3 * CHUNK + 2048, KD, 256)
        qb, kb = A(3 * CHUNK, CT, T), A(3 * CHUNK + 1024, CT, T)
        sqb = A(3 * CHUNK + 2048, 2, CT * T)
        PR = A(3 * CHUNK + 2048, 3, 384)
        PT_ = A(3 * CHUNK + 3200, 2, 384)
        Z = A(3 * CHUNK, 16, T)
        vtm = R(O_YR, TT, CW)

        xh, xl = (xs[:, i * 2048:(i + 1) * 2048].rearrange("p (k t) -> p k t", k=KD) for i in range(2))
        ysp = xs[:, :].rearrange("p (b q c t) -> p b q c t", b=2, q=2, c=CT)
        xsx = [xs[:, b * 1024:(b + 1) * 1024].rearrange("p (k m) -> p k m", k=KD) for b in range(2)]
        xsh = xs[:, 2048:2560].rearrange("p (k m) -> p k m", k=FE // P)
        hTm = R(O_AR, KD, T)

        LEVEL_LO = {0: 13, 1: 14, 10: 15, 11: 16}

        xg = [R(O_AR + 1024 * b, D, p1=S) for b in range(2)]
        tg, tu, gf, sg = (R(O_XNT + 512 * i, FE, p1=S) for i in range(4))
        ysb = [R(O_B + 1024 * b, 2, 512, p1=S) for b in range(2)]
        ty = R(O_YR, 512, p1=S)
        ub = R(O_YR + 512, 512, p1=S)
        hb = R(O_YM, 512, p1=S)
        Wr = R(O_YM, KD, NG + NE)
        brc = R(O_YM + KD * (NG + NE), NG + NE)
        gbc = R(O_YR, D)
        yall = A(CHUNK, TT, 2 * D)

        def chunk_view(slot, kind):
            k = 8 if kind in ("cols", "rows") else 4
            return ring[:, slot, :].rearrange("p (k n) -> p k n", k=k)

        def half_view(slot, kind, j):
            v = chunk_view(slot, kind)
            if kind == "cols":
                return v[:, :, 256 * j:256 * j + 256]
            if kind == "rows":
                return v[:, 4 * j:4 * j + 4, :]
            return v[:, :, 512 * j:512 * j + 512]

        def part_view(w, b, kind):
            k = 8 if kind == "cols" else 4
            return w[:, b, :].rearrange("p (k n) -> p k n", k=k)

        def split_hi(eng, g, b, slot, kind, j, landed):
            landed()
            if not isinstance(g, int) or g >= NB:
                eng.wait_ge(s["half"], g - NB + 1)
            eng.activation(part_view(wh, b, kind), half_view(slot, kind, j), ACT.Copy).then_inc(s["hi"], 1)

        def split_lo(eng, g, b, slot, kind, j, which):
            k = 8 if kind == "cols" else 4
            q = slice(0, 3 * k // 4) if which == "lo_d" else slice(3 * k // 4, k)
            eng.wait_ge(s["hi"], g + 1)
            eng.tensor_tensor(part_view(wl, b, kind)[:, q, :], half_view(slot, kind, j)[:, q, :],
                              part_view(wh, b, kind)[:, q, :].bitcast(F32), ALU.subtract).then_inc(s[which], 1)

        def pre_kind(c):
            return "br" if c in (10, 11) else "cols"

        def pre_hi(eng, g):
            c = g // 2
            split_hi(eng, g, g % NB, c % 2, pre_kind(c), g % 2, lambda: eng.wait_ge(pre_in[c % 2], 16 * (c // 2 + 1)))

        def pre_lo(eng, g, which):
            c = g // 2
            split_lo(eng, g, g % NB, c % 2, pre_kind(c), g % 2, which)

        def moe_half(n, i):
            idx = 3 * n - 1 + i // 2
            return 2 * PRE + 2 * idx + i % 2

        KINDS = ("rows", "rows", "down", "down", "rows", "rows")

        def moe_place(n0, i):
            idx = 3 * n0 - 1 + i // 2
            return (2 * PRE + 2 * idx + i % 2) % NB, idx % NS

        def moe_hi(eng, n, n0, i):
            b, slot = moe_place(n0, i)
            use = (n - n0) // 2 if isinstance(n, int) else None
            base = (3 * n0 - 1 + i // 2) // NS + 1
            count = 16 * (base + use) if use is not None else 8 * (n - n0) + 16 * base
            split_hi(eng, moe_half(n, i), b, slot, KINDS[i], i % 2, lambda: eng.wait_ge(slot_in[slot], count))

        def moe_lo(eng, n, n0, i, which):
            b, slot = moe_place(n0, i)
            split_lo(eng, moe_half(n, i), b, slot, KINDS[i], i % 2, which)

        FIRST = [(0, 0, "rows", 0), (0, 1, "rows", 1), (1, 0, "rows", 2), (1, 1, "rows", 3)]
        LAST = 3 * NE - 1

        def first_hi(eng, i):
            c, j, kind, o = FIRST[i]
            split_hi(eng, 2 * PRE + o, (2 * PRE + o) % NB, c, kind, j, lambda: eng.wait_ge(slot_in[c], 16))

        def first_lo(eng, i, which):
            c, j, kind, o = FIRST[i]
            split_lo(eng, 2 * PRE + o, (2 * PRE + o) % NB, c, kind, j, which)

        def last_hi(eng, j):
            g = 2 * PRE + 2 * LAST + j
            split_hi(eng, g, g % NB, LAST % NS, "down", j,
                     lambda: eng.wait_ge(slot_in[LAST % NS], 16 * (LAST // NS + 1)))

        def last_lo(eng, j, which):
            g = 2 * PRE + 2 * LAST + j
            split_lo(eng, g, g % NB, LAST % NS, "down", j, which)

        OKIND = ("rows", "rows", "rows", "rows", "down", "down")

        def over_half(i, q):
            return 2 * PRE + 6 * NE + 6 * i + q

        def over_hi(eng, i, q):
            split_hi(eng, over_half(i, q), (2 * PRE + q) % NB, q // 2, OKIND[q], q % 2,
                     lambda: eng.wait_ge(slot_in[q // 2], 16 * (3 * NE // NS) + 16 + 16 * i))

        def over_lo(eng, i, q, which):
            split_lo(eng, over_half(i, q), (2 * PRE + q) % NB, q // 2, OKIND[q], q % 2, which)

        def gate_done(n, extra=False):
            return 6 * n + 2 * PRE + (2 if extra or (isinstance(n, int) and n == 0) else 0)

        def up_done(n):
            return 6 * n + 2 * PRE + 4

        def down_done(n, j, late=False):
            return 6 * n + 2 * PRE + 7 + j - (2 if late else 0)

        def over_count(eng):
            eng.wait_ge(s["ovf"], 1)
            return eng.value_load(over[0:1, 0:1].bitcast(I32), min_val=0, max_val=MAXO)

        wg_v = w_gate[0].rearrange("e (p k) n -> e p (k n)", p=P)
        wu_v = w_up[0].rearrange("e (p k) n -> e p (k n)", p=P)
        wd_v = w_down[0].rearrange("e (p k) n -> e p (k n)", p=P)

        rows = R(O_K, P, p1=NVEC)

        block = ctx.enter_context(nc.Block())

        @block.sync
        def _(sp):
            sp.dma_start(xin, x[0].rearrange("(a p) d -> p a d", p=P)).then_inc(s["xin"], 16)
            sp.dma_start(cst, consts[:, :]).then_inc(s["consts"], 16)
            for v, row in ((w0, V_W0), (a0, V_A0), (k_k, V_KK), (k_a, V_KA), (lnx_g, V_LG), (lnx_b, V_LB)):
                sp.dma_start(rows[row:row + CT, :], v.rearrange("a (n p) -> (a n) p", p=P)).then_inc(s["vecs"], 16)

            def freed(c):
                sp.wait_ge(s["lo_d"], 2 * c + 2)
                sp.wait_ge(s["lo_p"], 2 * c + 2)

            def pre_load(c):
                if c >= 2:
                    freed(c - 2)
                dst = ring[:, c % 2, :]
                if c < 10:
                    src = w_in[0].rearrange("(k p) n -> p k n", p=P)[:, :, PCH[c]:PCH[c] + 512]
                    dst = dst.rearrange("p (k n) -> p k n", k=8)
                elif c < 12:
                    src = (w_br_moba if c == 10 else w_br_rwkv)[0].rearrange("(k p) n -> p k n", p=P)
                    dst = dst.rearrange("p (k n) -> p k n", k=4)
                else:
                    src = w_out[0].rearrange("(k p) n -> p k n", p=P)[:, :, 512 * (c - 12):512 * (c - 11)]
                    dst = dst.rearrange("p (k n) -> p k n", k=8)
                sp.dma_start(dst, src).then_inc(pre_in[c % 2], 16)

            for c in range(PRE):
                pre_load(c)

            def moe_load(slot, view, e):
                src = view[e] if isinstance(e, int) else view[bass.ds(e, 1)].rearrange("o p n -> (o p) n")
                sp.dma_start(ring[:, slot, :], src).then_inc(slot_in[slot], 16)

            freed(PRE - 2)
            moe_load(0, wg_v, 0)
            freed(PRE - 1)
            moe_load(1, wu_v, 0)
            sp.wait_ge(s["prefill"], 16)
            sp.wait_ge(s["y"], 2)
            moe_load(2, wg_v, 1)
            moe_load(3, wd_v, 0)
            moe_load(4, wu_v, 1)
            sp.wait_ge(s["hm"], 8)
            moe_load(5, wg_v, 2)

            def step_loads(n, parity, first=True):
                for q, (view, e) in enumerate(((wg_v, n), (wd_v, n - 1), (wu_v, n))):
                    if q == 0 and not first:
                        continue
                    g = 2 * PRE + 2 * (3 * n - 1 + q - NS) + 2
                    sp.wait_ge(s["lo_d"], g)
                    sp.wait_ge(s["lo_p"], g)
                    moe_load((3 * parity - 1 + q) % NS, view, e)

            step_loads(2, 2, first=False)
            step_loads(3, 3)
            with sp.Fori(0, (NE - 4) // 2) as it:
                for j in range(2):
                    step_loads(2 * it + 4 + j, 4 + j)
            g = 2 * PRE + 2 * (LAST - NS) + 2
            sp.wait_ge(s["lo_d"], g)
            sp.wait_ge(s["lo_p"], g)
            moe_load(LAST % NS, wd_v, NE - 1)

            n_over = over_count(sp)
            with sp.If(n_over > 0):
                with sp.Fori(0, n_over) as i:
                    e = sp.value_load(over[0:1, bass.ds(i + 1, 1)].bitcast(I32), min_val=0, max_val=NE - 1)
                    g = 2 * PRE + 6 * NE + 6 * i
                    sp.wait_ge(s["lo_d"], g)
                    sp.wait_ge(s["lo_p"], g)
                    for q, view in enumerate((wg_v, wu_v, wd_v)):
                        moe_load(q, view, e)
            sp.wait_ge(s["lo_d"], 2 * PRE + 6 * NE)
            sp.wait_ge(s["lo_p"], 2 * PRE + 6 * NE)
            sp.wait_ge(s["sc"], 16 * NE + 16 * n_over)
            for a in range(TT):
                sp.dma_start(yall[:, a, :], y_dram[2 * P * a:2 * P * (a + 1), :].rearrange("(p k) d -> p (k d)", k=2))\
                  .then_inc(s["ychunk"], 16)
            sp.wait_ge(s["fin"], 1)
            sp.dma_start(out[0].rearrange("(a p) d -> p a d", p=P), xrs).then_inc(s["out"], 16)
            sp.wait_ge(s["out"], 16)

        @block.gpsimd
        def _(pool):
            chain = [0]

            def link(ins):
                chain[0] += 1
                ins.then_inc(s["ch_p"], 1)
                pool.wait_ge(s["ch_p"], chain[0])

            last_slot, last_token, last_row = (pool.to_reg(v) for v in (NE * T - 1, T - 1, 2 * T - 1))
            for w, lo, hi in ((w1, 0, 64), (a1, 64, 128), (g1, 128, 256)):
                pool.dma_start(WL[:, :, lo:hi], w[0].rearrange("(k p) n -> p k n", p=P)).then_inc(s["lora_w"], 16)
            pool.dma_start(R(O_G, 768, p1=32), bias_consts[0:32, 0:768]).then_inc(s["biasc"], 16)
            pool.dma_start(R(O_G + 768, 8, p1=32), rel_bias[:, :]).then_inc(s["biasc"], 16)
            pool.memset(sent, 1 << 20).then_inc(s["prefset"], 1)
            pool.wait_ge(s["prefset"], 1)
            pool.dma_start(lists.rearrange("(p a) w -> p (a w)", p=P).bitcast(I32), sent).then_inc(s["prefill"], 16)
            pre_lo(pool, 0, "lo_p")
            pre_lo(pool, 1, "lo_p")
            pool.wait_ge(s["lora_w"], 48)
            pool.wait_ge(s["PT"], 1)
            for i, (lo, hi) in enumerate(((0, 64), (64, 128), (128, 256))):
                mu = VT[:, V_MX + KD * i:V_MX + KD * (i + 1)]
                link(pool.tensor_tensor(WM[:, :, lo:hi], WL[:, :, lo:hi], bcast(mu, 2, hi - lo), ALU.mult))
            pool.tensor_tensor(WL, WL, WM, ALU.subtract).then_inc(s["musplit"], 1)

            def square(i):
                pool.wait_ge(s["projev"], 8 + 2 * i)
                tf = (qb, kb)[i].rearrange("p c t -> p (c t)")
                pool.tensor_tensor(sqb[:, i, :], tf, tf, ALU.mult).then_inc(s["sq"], 1)

            for g in range(2, 13):
                pre_lo(pool, g, "lo_p")
                if g == 9:
                    square(0)
                if g == 11:
                    square(1)

            for c in range(2):
                for b in range(2):
                    for u in range(4):
                        pool.wait_ge(s["gcp"], 8 * c + 4 * b + u + 1)
                        v = GRo[b][:, u].rearrange("p (a s) i -> p a s i", a=2)
                        pool.affine_select(out=v, in_=v, pattern=[[0, 2], [1, 2], [1, P]], compare_op=ALU.is_gt,
                                           fill=0.0, base=0, channel_multiplier=-1).then_inc(s["gsel"], 1)
                for lev in range(1, 7):
                    L = 6 * c + lev - 1
                    for b in range(2):
                        n = 2 * L + b
                        pool.wait_ge(s["gsel"], 8 * c + 4 * b + 4)
                        if n >= 2:
                            pool.wait_ge(s["t1"], n - 1)
                        pool.tensor_tensor(NTo[b], GRo[b][:, :, 0, :], bcast(masks[:, lev, :], 1, 4), ALU.mult)\
                            .then_inc(s["nt"], 1)
                    if L in LEVEL_LO:
                        pre_lo(pool, LEVEL_LO[L], "lo_p")
            for g in range(17, 28):
                pre_lo(pool, g, "lo_p")

            pool.wait_ge(s["prefill"], 16)
            pool.wait_ge(s["addr"], 1)
            for a in range(TT):
                for k in range(2):
                    pool.indirect_dma_start(
                        out=lists[:, :], out_offset=bass.IndirectOffsetOnAxis(ap=addr[:, a, k:k + 1].bitcast(U32), axis=0),
                        in_=rowv[:, a, k, :], in_offset=None, bounds_check=last_slot, oob_is_err=False)\
                        .then_inc(s["lists"], 16)
            pool.wait_ge(s["logit"], 1)
            for b in range(2):
                pool.memset(xg[b], 0.0).then_inc(s["zero"], 1)
            pool.wait_ge(s["zero"], 2)
            pool.wait_ge(s["lists"], 64)
            pool.wait_ge(s["xn2st"], 16)

            lview = lists.rearrange("(c s) w -> c s w", s=S)

            def list_rows(block_):
                return lview[block_] if isinstance(block_, int) else lview[bass.ds(block_, 1)].rearrange("o s w -> (o s) w")

            def load_tidx(n, b, row):
                if not isinstance(n, int) or n >= 2:
                    pool.wait_ge(s["xg"], 16 * (n - 1))
                pool.dma_start(tidx[0:S, b, :], list_rows(row)).then_inc(s["tidx"], 16)

            def gather(n, b):
                pool.wait_ge(s["tidx"], 16 * (n + 1))
                if not isinstance(n, int) or n >= 1:
                    pool.wait_ge(s["xg"], 16 * n)
                if not isinstance(n, int) or n >= 2:
                    pool.wait_ge(s["xgT"], n - 1)
                pool.nop(nofuse=True)
                pool.indirect_dma_start(
                    out=xg[b], out_offset=None, in_=xn2_dram[:, :],
                    in_offset=bass.IndirectOffsetOnAxis(ap=tidx[0:S, b, 0:1].bitcast(U32), axis=0),
                    bounds_check=last_token, oob_is_err=False).then_inc(s["xg"], 16)

            def load_vg(n, b, row):
                if not isinstance(n, int) or n >= 1:
                    pool.wait_ge(s["vg"], 16 * n)
                if not isinstance(n, int) or n >= 2:
                    pool.wait_ge(s["sc"], 16 * (n - 1))
                    pool.wait_ge(s["m"], n - 1)
                pool.dma_start(vgb[0:S, b, :], list_rows(row)).then_inc(s["vg"], 16)

            def scatter(n, b):
                pool.wait_ge(s["vg"], 16 * (n + 1))
                pool.wait_ge(s["y_"], 2 * n + 2)
                pool.nop(nofuse=True)
                pool.indirect_dma_start(
                    out=y_dram[:, :], out_offset=bass.IndirectOffsetOnAxis(ap=vgb[0:S, b, 1:2].bitcast(U32), axis=0),
                    in_=ysb[b].rearrange("p a n -> p (a n)"), in_offset=None, bounds_check=last_row,
                    oob_is_err=False).then_inc(s["sc"], 16)

            load_tidx(0, 0, 0)
            gather(0, 0)
            load_tidx(1, 1, NC)
            load_vg(0, 0, 0)
            for i in range(4):
                first_lo(pool, i, "lo_p")

            def step(n, n0, tail=False):
                b = n0 % 2
                moe_lo(pool, n, n0, 0, "lo_p")
                if not tail:
                    gather(n + 1, 1 - b)
                moe_lo(pool, n, n0, 1, "lo_p")
                scatter(n - 2, b)
                moe_lo(pool, n, n0, 2, "lo_p")
                moe_lo(pool, n, n0, 3, "lo_p")
                load_vg(n, b, NC * n)
                moe_lo(pool, n, n0, 4, "lo_p")
                if not tail:
                    load_tidx(n + 2, b, NC * (n + 2))
                moe_lo(pool, n, n0, 5, "lo_p")

            gather(1, 1)
            load_tidx(2, 0, 2 * NC)

            def step1():
                moe_lo(pool, 1, 1, 0, "lo_p")
                gather(2, 0)
                for i in (1, 2, 3):
                    moe_lo(pool, 1, 1, i, "lo_p")
                load_vg(1, 1, NC)
                moe_lo(pool, 1, 1, 4, "lo_p")
                load_tidx(3, 1, 3 * NC)
                moe_lo(pool, 1, 1, 5, "lo_p")

            step1()
            with pool.Fori(0, (NE - 4) // 2) as it:
                for j in range(2):
                    step(2 * it + 2 + j, 2 + j)
            moe_lo(pool, NE - 2, NE - 2, 0, "lo_p")
            gather(NE - 1, 1)
            moe_lo(pool, NE - 2, NE - 2, 1, "lo_p")
            scatter(NE - 4, 0)
            moe_lo(pool, NE - 2, NE - 2, 2, "lo_p")
            moe_lo(pool, NE - 2, NE - 2, 3, "lo_p")
            load_vg(NE - 2, 0, NC * (NE - 2))
            moe_lo(pool, NE - 2, NE - 2, 4, "lo_p")
            moe_lo(pool, NE - 2, NE - 2, 5, "lo_p")
            step(NE - 1, NE - 1, tail=True)
            last_lo(pool, 0, "lo_p")
            last_lo(pool, 1, "lo_p")
            scatter(NE - 2, 0)
            scatter(NE - 1, 1)

            n_over = over_count(pool)
            with pool.If(n_over > 0):
                with pool.Fori(0, n_over) as i:
                    n = NE + i
                    row = pool.value_load(over[0:1, bass.ds(i + 9, 1)].bitcast(I32), min_val=0, max_val=NE * NC - 1)
                    pool.wait_ge(s["sc"], 16 * n)
                    pool.dma_start(tidx[0:S, 0, :], list_rows(row)).then_inc(s["tidx"], 16)
                    pool.dma_start(vgb[0:S, 0, :], list_rows(row)).then_inc(s["vg"], 16)
                    pool.wait_ge(s["tidx"], 16 * (n + 1))
                    pool.nop(nofuse=True)
                    pool.indirect_dma_start(
                        out=xg[0], out_offset=None, in_=xn2_dram[:, :],
                        in_offset=bass.IndirectOffsetOnAxis(ap=tidx[0:S, 0, 0:1].bitcast(U32), axis=0),
                        bounds_check=last_token, oob_is_err=False).then_inc(s["xg"], 16)
                    for q in range(6):
                        over_lo(pool, i, q, "lo_p")
                    scatter(n, 0)

        @block.scalar
        def _(act):
            def vec_in(v, row, n):
                act.dma_start(rows[row:row + n, :], v).then_inc(s["vecs"], 16)

            vec_in(norm_mix_g.rearrange("a (n p) -> (a n) p", p=P), V_GMIX, KD)
            vec_in(mu_rkv[0].rearrange("a (n p) -> (a n) p", p=P), V_MRKV, 3 * CT)
            vec_in(mu_x[0].rearrange("a (n p) -> (a n) p", p=P), V_MX, 3 * KD)
            vec_in(r_k[0].rearrange("(n b) d -> n (b d)", b=2), V_RK, CT)
            for v, row in ((q_gain, V_QG), (k_gain, V_KG)):
                for i in range(2):
                    act.dma_start(rows[row:row + 1, 64 * i:64 * i + 64], v[:, :]).then_inc(s["vecs"], 16)

            junk = R(O_V, D)
            act.wait_ge(s["xin"], 16)
            for a in range(TT):
                act.activation(junk, xin[:, a, :], ACT.Square, accum_out=st_[:, a:a + 1]).then_inc(s["rms0"], 1)
                act.wait_ge(s["rms0"], a + 1)
            act.wait_ge(s["consts"], 16)
            act.activation(st_[:, 4:6], st_[:, 0:2], ACT.Sqrt, scale=1.0 / D, bias=eps).then_inc(s["rms0"], 1)
            act.dma_start(R(O_YR, CW, p1=64), w2[0]).then_inc(s["lora2"], 16)
            act.dma_start(R(O_YR, CW, p0=64), a2[0]).then_inc(s["lora2"], 16)
            act.dma_start(R(O_YR + CW, CW), g2[0]).then_inc(s["lora2"], 16)
            pre_hi(act, 0)
            act.wait_ge(s["xnT"], KD)
            act.activation(xh, xnT[:, :, 1:T + 1], ACT.Copy).then_inc(s["xsplit"], 1)
            pre_hi(act, 1)
            act.dma_start(JJ, bias_consts[:, 768:896]).then_inc(s["hank"], 16)
            act.dma_start(rowv.rearrange("p a k w -> p (a k w)").bitcast(I32), slot_rows[:, :]).then_inc(s["rte"], 16)

            def evac(g):
                act.wait_ge(s["half"], g + 1)
                src = banks[6 + g % 2][:, :].rearrange("p (a t) -> p a t", a=2)
                f = ACT.Copy
                if g < 6:
                    dst = pads[g // 2][:, 2 * (g % 2):2 * (g % 2) + 2, 1:T + 1]
                elif g < 10:
                    if g == 6:
                        act.wait_ge(s["lora"], 1)
                    dst = (qb, kb)[g // 2 - 3][:, 2 * (g % 2):2 * (g % 2) + 2, :]
                elif g < 12:
                    dst = ym[:, 2 * (g % 2):2 * (g % 2) + 2, :]
                else:
                    dst, f = Z[:, 2 * (g - 12):2 * (g - 12) + 2, :], ACT.Sigmoid
                act.activation(dst, src, f).then_inc(s["projev"], 1)

            def two(i):
                return banks[i][:, :].rearrange("p (a t) -> p a t", a=2)

            def lora_hidden():
                act.wait_ge(s["lora"], 1)
                lt = R(O_V, 2, T)
                act.activation(lt[0:64, 0, :], banks[2][0:64, 0:T], ACT.Tanh).then_inc(s["lt"], 1)
                act.activation(lt[64:128, 0, :], banks[2][64:128, 0:T], ACT.Copy).then_inc(s["lt"], 1)
                act.activation(lt[:, 1, :], banks[2][:, T:2 * T], ACT.Sigmoid).then_inc(s["lt"], 1)
                act.wait_ge(s["vec"], 1)
                act.dma_start(bias_rows[:, 0:NV], R(O_B, NV, p1=H)).then_inc(s["vecst"], 16)

            def lora_outputs():
                act.wait_ge(s["loraout"], 1)
                for ct in range(CT):
                    act.activation(Kc[:, ct, :], banks[3 + ct // 2][:, T * (ct % 2):T * (ct % 2) + T], ACT.Sigmoid,
                                   bias=VT[:, V_W0 + ct:V_W0 + ct + 1]).then_inc(s["sgm"], 1)
                act.wait_ge(s["vecst"], 16)
                for ct in range(CT):
                    act.activation(Bc[:, ct, :], banks[(5, 0)[ct // 2]][:, T * (ct % 2):T * (ct % 2) + T], ACT.Sigmoid,
                                   bias=VT[:, V_A0 + ct:V_A0 + ct + 1]).then_inc(s["sgm"], 1)
                for i in range(2):
                    act.activation(gg[:, 2 * i:2 * i + 2, :], two(1 + i), ACT.Copy).then_inc(s["gout"], 1)
                act.wait_ge(s["xsplit"], 2)
                act.dma_start(HK, bass.AP(bias_rows.tensor, 0, [[1, P], [384, H], [1, 2 * P]])).then_inc(s["hank"], 16)

            def decays(ct):
                for c in range(2):
                    act.activation(EP[:, ct, c, 1:P + 1], cs[:, ct, P * c:P * c + P], ACT.Exp, scale=-DECAY,
                                   bias=cb[:, ct, c:c + 1]).then_inc(s["expd"], 1)
                    act.activation(EN[:, ct, P * c:P * c + P], cs[:, ct, P * c:P * c + P], ACT.Exp, scale=DECAY,
                                   bias=ncb[:, ct, c:c + 1]).then_inc(s["expd"], 1)

            def root(i, b0, b1):
                act.wait_ge(s["ssum"], i + 1)
                for j, bank_i in enumerate((b0, b1)):
                    act.activation(sqb[:, i, 512 * j:512 * j + 512], banks[bank_i][:, :], ACT.Sqrt, scale=1.0 / HD,
                                   bias=eps).then_inc(s["qks"], 1)

            def tokens(i, dst, bank_i):
                act.wait_ge(s["tokT"], i + 1)
                act.activation(dst, banks[bank_i][:, :], ACT.Copy).then_inc(s["tok"], 1)

            for g in range(12):
                if g >= 1:
                    pre_hi(act, g + 1)
                evac(g)
                if g == 1:
                    lora_hidden()
                elif g == 3:
                    lora_outputs()
                elif g == 6:
                    act.wait_ge(s["cbias"], 2)
                    act.activation(EP[:, :, :, 0], cb, ACT.Exp).then_inc(s["ebc"], 1)
                    act.activation(st_[:, 8:12], ncb[:, :, 1], ACT.Exp).then_inc(s["ebc"], 1)
                    decays(0)
                    decays(1)
                elif g == 7:
                    decays(2)
                    decays(3)
                    act.wait_ge(s["rk_ss"], 1)
                    for i in range(2):
                        act.activation(nr[:, 2 * i:2 * i + 2, :], two(i), ACT.Sqrt).then_inc(s["rk_nr"], 1)
                elif g == 9:
                    act.wait_ge(s["v_ch"], 1)
                    tokens(0, Vtok[:, 0, :], 0)
                    tokens(1, Vtok[:, 1, :], 1)
                elif g == 10:
                    root(0, 4, 5)
                elif g == 11:
                    root(1, 0, 1)

            def exps(h):
                act.wait_ge(s["nmx"], h + 1)
                for q, (lo, hi) in enumerate(((0, 256), (256, 384))):
                    act.activation(PR[:, h % 3, lo:hi], banks[6 + h % 2][:, lo:hi], ACT.Exp, bias=mx[:, h, q:q + 1],
                                   accum_out=rs[:, h, q:q + 1]).then_inc(s["prob"], 1)

            def pt_copy(h):
                act.wait_ge(s["pT"], h + 1)
                act.activation(PT_[:, h % 2, :], banks[6 + h % 2][:, 0:384], ACT.Copy).then_inc(s["pTc"], 1)

            def head_out(h):
                hp = slice(HD * (h % 2), HD * (h % 2) + HD)
                act.wait_ge(s["av"], h + 1)
                act.activation(ym[hp, h // 2, :], banks[6 + h % 2][hp, 0:T], ACT.Copy).then_inc(s["avc"], 1)

            for c in range(2):
                for b in range(2):
                    for u in range(4):
                        act.wait_ge(s["gram"], 8 * c + 4 * b + u + 1)
                        if c == 1 and u == 0 and b == 0:
                            act.wait_ge(s["y"], 1)
                        act.activation(GRo[b][:, u].rearrange("p a i -> p (a i)"), banks[u][:, :], ACT.Copy)\
                           .then_inc(s["gcp"], 1)
                for lev in range(1, 7):
                    L = 6 * c + lev - 1
                    if L == 1:
                        act.wait_ge(s["vtT"], 2)
                        act.activation(vtm[:, 1, :], banks[7][:, :], ACT.Copy).then_inc(s["vtok"], 1)
                    if L >= 10:
                        evac(L + 2)
                    for b in range(2):
                        n = 2 * L + b
                        act.wait_ge(s["t1"], n + 1)
                        if n >= 2:
                            act.wait_ge(s["dx"], n - 1)
                        act.activation(T1o[b].rearrange("p u i -> p (u i)"), banks[3 * b][:, :], ACT.Copy)\
                           .then_inc(s["t1c"], 1)
                    if L == 0:
                        act.wait_ge(s["vtT"], 1)
                        act.activation(vtm[:, 0, :], banks[6][:, :], ACT.Copy).then_inc(s["vtok"], 1)
                    if L == 1:
                        tokens(2, Btok, 6)
                        tokens(3, Ktok, 7)
                    if 2 <= L < H + 2:
                        pt_copy(L - 2)
                    if 3 <= L < H + 3:
                        head_out(L - 3)
                    if L in LEVEL_LO:
                        pre_hi(act, LEVEL_LO[L])
                    if 1 <= L < H + 1:
                        exps(L - 1)
                if c == 1:
                    evac(14)
                    pre_hi(act, 17)
                act.wait_ge(s["z"], c + 1)
                for q in range(2):
                    act.activation(Zb.rearrange("p (v q n) -> p q v n", v=CT, q=2)[:, q],
                                   banks[3 * q][:, 0:CT * HD].rearrange("p (v n) -> p v n", v=CT), ACT.Copy)\
                       .then_inc(s["zc"], 1)
                if c == 1:
                    evac(15)
                    pre_hi(act, 18)
                act.wait_ge(s["u"], c + 1)
                act.activation(Ub, banks[1][:, :], ACT.Copy).then_inc(s["uc"], 1)
                act.wait_ge(s["y"], c + 1)
                act.activation(yraw[:, :, c, :], banks[2][:, :].rearrange("p (a i) -> p a i", a=CT), ACT.Copy)\
                   .then_inc(s["yc"], 1)

            def y_hi(b, src):
                act.activation(ysp[:, b, 0], src, ACT.Copy).then_inc(s["ysplit"], 1)

            pre_hi(act, 19)
            evac(16)
            act.wait_ge(s["lnv"], 1)
            for i in range(2):
                act.activation(Bc[:, 2 * i:2 * i + 2, :], two(2 + i), ACT.Sqrt, scale=1.0 / HD, bias=lnx_eps)\
                   .then_inc(s["lnsd"], 1)
            evac(17)
            pre_hi(act, 20)
            evac(18)
            pre_hi(act, 21)
            evac(19)
            y_hi(1, ym)
            pre_hi(act, 22)
            act.wait_ge(s["yr"], 1)
            y_hi(0, yr)
            act.dma_start(xrs, x[0].rearrange("(a p) d -> p a d", p=P)).then_inc(s["xre"], 16)
            pre_hi(act, 23)
            pre_hi(act, 24)
            pre_hi(act, 25)
            act.wait_ge(s["ylo"], 2)
            act.dma_start(gbc, bcast(norm_ffn_g[0], 0, P)).then_inc(s["gbc"], 16)
            act.dma_start(Wr[:, :, 0:NG], w_grp[0].rearrange("(k p) n -> p k n", p=P)).then_inc(s["wr"], 16)
            act.dma_start(Wr[:, :, NG:NG + NE], w_exp[0].rearrange("(k p) n -> p k n", p=P)).then_inc(s["wr"], 16)
            act.dma_start(brc[:, 0:NG], bcast(b_grp[0], 0, P)).then_inc(s["wr"], 16)
            act.dma_start(brc[:, NG:NG + NE], bcast(b_exp[0], 0, P)).then_inc(s["wr"], 16)
            act.wait_ge(s["hm"], 8)
            act.wait_ge(s["half"], 24)
            act.activation(xh, hTm, ACT.Copy).then_inc(s["hsplit"], 1)
            pre_hi(act, 26)
            pre_hi(act, 27)

            act.wait_ge(s["x2"], 4)
            junk2 = R(O_B, D)
            for a in range(TT):
                act.activation(junk2, xrs[:, a, :], ACT.Square, accum_out=st_[:, a:a + 1]).then_inc(s["r2"], 1)
                act.wait_ge(s["r2"], a + 1)
            act.activation(st_[:, 4:6], st_[:, 0:2], ACT.Sqrt, scale=1.0 / D, bias=eps).then_inc(s["r2q"], 1)
            act.wait_ge(s["xn2"], TT)
            act.dma_start(xn2_dram.rearrange("(a p) d -> p a d", p=P), R(O_XNT, TT, D)).then_inc(s["xn2st"], 16)
            for q in range(4):
                act.wait_ge(s["xn2T"], q + 1)
                act.activation(hTm[:, 2 * q:2 * q + 2, :], banks[q][:, :].rearrange("p (a t) -> p a t", a=2), ACT.Copy)\
                   .then_inc(s["xn2Tc"], 1)
            act.wait_ge(s["rt"], 1)
            act.activation(R(O_B + 80, 2, NG), R(O_B + 80, 2, NG), ACT.Exp).then_inc(s["gates"], 1)
            act.wait_ge(s["rt"], 2)
            act.activation(R(O_B + 100, 2), R(O_B + 100, 2), ACT.Exp).then_inc(s["gates"], 1)

            def t_gate(n, extra=False):
                act.wait_ge(s["half"], gate_done(n, extra))
                if not isinstance(n, int) or n >= 1:
                    act.wait_ge(s["gf"], n)
                act.activation(tg, banks[0][S:2 * S, :], ACT.Copy).then_inc(s["tg"], 1)

            def t_up(n):
                act.wait_ge(s["half"], up_done(n))
                if not isinstance(n, int) or n >= 1:
                    act.wait_ge(s["uf"], n)
                act.activation(tu, banks[1][S:2 * S, :], ACT.Copy).then_inc(s["tu"], 1)

            def sigm(n):
                act.wait_ge(s["gf"], n + 1)
                if not isinstance(n, int) or n >= 1:
                    act.wait_ge(s["m"], n)
                act.activation(sg, gf, ACT.Sigmoid).then_inc(s["sg"], 1)

            def t_down(n, j, late=False):
                act.wait_ge(s["half"], down_done(n, j, late))
                if not isinstance(n, int) or n >= 1 or j:
                    act.wait_ge(s["y_"], 2 * n + j)
                act.activation(ty, banks[2 + j][S:2 * S, :], ACT.Copy).then_inc(s["ty"], 1)

            for i in range(4):
                first_hi(act, i)
                if i == 3:
                    t_gate(0)
                    sigm(0)

            def step(n, n0):
                moe_hi(act, n, n0, 0)
                if not isinstance(n, int) or n >= 2:
                    t_down(n - 2, 1)
                moe_hi(act, n, n0, 1)
                moe_hi(act, n, n0, 2)
                t_up(n - 1)
                moe_hi(act, n, n0, 3)
                moe_hi(act, n, n0, 4)
                t_gate(n)
                moe_hi(act, n, n0, 5)
                sigm(n)
                t_down(n - 1, 0)

            step(1, 1)
            with act.Fori(0, (NE - 2) // 2) as it:
                for j in range(2):
                    step(2 * it + 2 + j, 2 + j)
            last_hi(act, 0)
            t_down(NE - 2, 1)
            last_hi(act, 1)
            t_up(NE - 1)
            t_down(NE - 1, 0, late=True)
            t_down(NE - 1, 1, late=True)

            n_over = over_count(act)
            with act.If(n_over > 0):
                with act.Fori(0, n_over) as i:
                    n = NE + i
                    for q in range(3):
                        over_hi(act, i, q)
                    t_gate(n, extra=True)
                    sigm(n)
                    for q in range(3, 6):
                        over_hi(act, i, q)
                    t_up(n)
                    t_down(n, 0, late=True)
                    t_down(n, 1, late=True)

        @block.vector
        def _(dve):
            chain = [0]

            def link(ins):
                chain[0] += 1
                ins.then_inc(s["ch_d"], 1)
                dve.wait_ge(s["ch_d"], chain[0])

            def flink(ins, name, count):
                ins.then_inc(s[name], 1)
                dve.wait_ge(s[name], count)

            dve.memset(xnT[:, :, 0:1], 0.0)
            dve.wait_ge(s["rms0"], 3)
            link(dve.reciprocal(st_[:, 6:8], st_[:, 4:6]))
            for a in range(TT):
                dve.tensor_scalar(xin[:, a, :], xin[:, a, :], st_[:, 6 + a:7 + a], None, ALU.mult).then_inc(s["xsn"], 1)
            dve.wait_ge(s["vecT"], 1)
            flink(dve.tensor_copy(VT, banks[6][:, 0:NVEC]), "PT", 1)
            link(dve.tensor_scalar(gqk[:, 0:1], VT[:, V_QG:V_QG + 1], HD ** -0.5, None, ALU.mult))
            dve.wait_ge(s["vecmm"], 1)
            dve.tensor_tensor(R(O_B, NV, p1=H), banks[7][0:H, 0:NV], R(O_G + 384, NV, p1=H), ALU.add).then_inc(s["vec"], 1)
            for k in range(KD):
                dve.wait_ge(s["xT"], k // 2 + 1)
                dve.tensor_scalar(xnT[:, k, 1:T + 1], banks[2 + k // 2][:, T * (k % 2):T * (k % 2) + T],
                                  VT[:, V_GMIX + k:V_GMIX + k + 1], None, ALU.mult).then_inc(s["xnT"], 1)
            dve.wait_ge(s["xsplit"], 1)
            dve.wait_ge(s["xnT"], KD)
            dve.tensor_tensor(xl, xnT[:, :, 1:T + 1], xh.bitcast(F32), ALU.subtract).then_inc(s["xsplit"], 1)
            for g in range(4):
                pre_lo(dve, g, "lo_d")

            for p_ in pads:
                link(dve.memset(p_[:, :, 0:1], 0.0))

            def shift_mix(i, mi, dst):
                p_ = pads[i]
                dve.wait_ge(s["projev"], 2 * i + 2)
                link(dve.tensor_tensor(df, p_[:, :, 0:T], p_[:, :, 1:T + 1], ALU.subtract))
                for ct in range(CT):
                    ins = dve.scalar_tensor_tensor(out=dst[:, ct, :], in0=df[:, ct, :],
                                                   scalar=VT[:, V_MRKV + CT * mi + ct:V_MRKV + CT * mi + ct + 1],
                                                   in1=p_[:, ct, 1:T + 1], op0=ALU.mult, op1=ALU.add)
                link(ins)

            shift_mix(0, 1, kk)
            pre_lo(dve, 4, "lo_d")
            for ct in range(CT):
                ins = dve.tensor_scalar(kn[:, ct, :], kk[:, ct, :], VT[:, V_KK + ct:V_KK + ct + 1], None, ALU.mult)
            link(ins)
            dve.tensor_tensor(nr, kn, kn, ALU.mult).then_inc(s["rk_sq"], 1)
            pre_lo(dve, 5, "lo_d")
            dve.wait_ge(s["sgm"], 4)
            for ct in range(CT):
                for c in range(2):
                    ins = dve.tensor_tensor_scan(cs[:, ct, P * c:P * c + P], ones,
                                                 Kc[:, ct, P * c:P * c + P], 0.0, ALU.mult, ALU.add)
            link(ins)
            mid = cs.rearrange("p c (b t) -> p c b t", b=2)[:, :, :, P // 2 - 1]
            dve.tensor_scalar(cb, mid, DECAY, None, ALU.mult).then_inc(s["cbias"], 1)
            dve.tensor_scalar(ncb, mid, -DECAY, None, ALU.mult).then_inc(s["cbias"], 1)
            pre_lo(dve, 6, "lo_d")
            shift_mix(1, 0, rr)
            pre_lo(dve, 7, "lo_d")
            dve.wait_ge(s["loraout"], 1)
            shift_mix(2, 2, vc)
            dve.sem_inc(s["v_ch"], 1)
            pre_lo(dve, 8, "lo_d")
            dve.wait_ge(s["sgm"], 8)
            for ct in range(CT):
                ins = dve.tensor_scalar(df[:, ct, :], Bc[:, ct, :], 1.0, VT[:, V_KA + ct:V_KA + ct + 1],
                                        ALU.subtract, ALU.mult)
            link(ins)
            link(dve.scalar_tensor_tensor(out=kk, in0=df, scalar=1.0, in1=kk, op0=ALU.add, op1=ALU.mult))
            for ct in range(CT):
                ins = dve.scalar_tensor_tensor(out=df[:, ct, :], in0=rr[:, ct, :], scalar=VT[:, V_RK + ct:V_RK + ct + 1],
                                               in1=kk[:, ct, :], op0=ALU.mult, op1=ALU.mult)
            flink(ins, "bonus", 1)
            pre_lo(dve, 9, "lo_d")
            dve.wait_ge(s["rk_nr"], 2)
            link(dve.tensor_scalar(nr, nr, 1e-12, None, ALU.max))
            link(dve.reciprocal(nr, nr))
            link(dve.tensor_tensor(kn, kn, nr, ALU.mult))
            link(dve.tensor_tensor(Bc, Bc, kn, ALU.mult))
            pre_lo(dve, 10, "lo_d")
            dve.wait_ge(s["expd"], 16)
            dve.wait_ge(s["ebc"], 2)

            def c4(t):
                return t.rearrange("p c (b t) -> p c b t", b=2)

            link(dve.tensor_tensor(sc1, st_[:, 8:12], EP[:, :, 0, P], ALU.mult))
            dve.tensor_tensor(Bc, Bc, EN, ALU.mult).then_inc(s["bk"], 1)
            dve.tensor_tensor(Kc, kk, EN, ALU.mult).then_inc(s["bk"], 1)
            pre_lo(dve, 11, "lo_d")
            for ct in range(CT):
                dve.tensor_tensor(AR[:, ct, :, 1, :], c4(rr)[:, ct], EP[:, ct, :, 1:P + 1], ALU.mult)
                ins = dve.scalar_tensor_tensor(out=AR[:, ct, :, 0, :], in0=c4(kn)[:, ct], scalar=-1.0,
                                               in1=EP[:, ct, :, 0:P], op0=ALU.mult, op1=ALU.mult)
            ins.then_inc(s["ar"], 1)
            dve.wait_ge(s["bons"], 1)
            dve.wait_ge(s["tokT"], 2)
            for i in range(2):
                ins = dve.tensor_tensor(vc[:, 2 * i:2 * i + 2, :], vc[:, 2 * i:2 * i + 2, :],
                                        banks[2 + i][:, :].rearrange("p (a t) -> p a t", a=2), ALU.mult)
            ins.then_inc(s["bonv"], 1)
            pre_lo(dve, 12, "lo_d")

            def hmax(h):
                dve.wait_ge(s["score"], h + 1)
                bk_ = banks[6 + h % 2]
                dve.reduce_max(mx[:, h, 0:1], bk_[:, 0:256], AX.X)
                link(dve.reduce_max(mx[:, h, 1:2], bk_[:, 256:384], AX.X))
                dve.tensor_scalar(mx[:, h, :], mx[:, h, :], -1.0, None, ALU.mult).then_inc(s["nmx"], 1)

            def hnorm(h):
                dve.wait_ge(s["prob"], 2 * h + 2)
                link(dve.reciprocal(rs[:, h, :], rs[:, h, :]))
                for q, (lo, hi) in enumerate(((0, 256), (256, 384))):
                    ins = dve.tensor_scalar(PR[:, h % 3, lo:hi], PR[:, h % 3, lo:hi], rs[:, h, q:q + 1], None, ALU.mult)
                ins.then_inc(s["pnorm"], 1)

            def qk_norm(i, t, gain):
                dve.wait_ge(s["qks"], 2 * i + 2)
                link(dve.reciprocal(sqb[:, i, :], sqb[:, i, :]))
                tf = t.rearrange("p c t -> p (c t)")
                dve.scalar_tensor_tensor(out=tf, in0=tf, scalar=gain, in1=sqb[:, i, :], op0=ALU.mult, op1=ALU.mult)                   .then_inc(s["qkn"], 1)

            qk_norm(0, qb, gqk[:, 0:1])

            for c in range(2):
                for b in range(2):
                    n = 2 * c + b
                    dve.wait_ge(s["gl"], n + 1)
                    dve.wait_ge(s["gsel"], 4 * n + 4)
                    for q in range(2):
                        v = XXo[b].rearrange("p (v q) x i -> p q v x i", q=2)[:, q, :, 0, :]
                        link(dve.tensor_tensor(v, banks[4 + q][:, 0:2 * P].rearrange("p (u i) -> p u i", u=2),
                                               bcast(cst[:, C_M0T:C_M0T + P], 1, 2), ALU.mult))
                    link(dve.tensor_tensor(XXo[b][:, :, 1, :], GRo[b][:, :, 0, :], bcast(masks[:, 0, :], 1, 4), ALU.mult))
                    for q in range(2):
                        ins = dve.tensor_tensor(XXo[b][:, :, q, :], XXo[b][:, :, q, :], bcast(ident, 1, 4), ALU.add)
                    ins.then_inc(s["x0"], 1)
                for lev in range(1, 7):
                    L = 6 * c + lev - 1
                    for b in range(2):
                        n = 2 * L + b
                        dve.wait_ge(s["dx"], n + 1)
                        dve.wait_ge(s["x0"], 2 * c + 2)
                        if n >= 2:
                            dve.wait_ge(s["xx"], n - 1)
                        for i in range(2):
                            v = XXo[b][:, 2 * i:2 * i + 2]
                            ins = dve.tensor_tensor(v, v, banks[3 * b + 1 + i][:, :].rearrange("p (u q i) -> p u q i", u=2, q=2),
                                                    ALU.add)
                        ins.then_inc(s["xx"], 1)
                    if L == 0:
                        qk_norm(1, kb, VT[:, V_KG:V_KG + 1])
                    if 1 <= L < H + 1:
                        hmax(L - 1)
                        hnorm(L - 1)
                    if L in LEVEL_LO:
                        pre_lo(dve, LEVEL_LO[L], "lo_d")
                if c == 0:
                    dve.wait_ge(s["st"], 1)
                    for ct in range(CT):
                        ins = dve.tensor_scalar(St[:, ct, :], banks[3][:, HD * ct:HD * ct + HD], sc1[:, ct:ct + 1], None,
                                                ALU.mult)
                    ins.then_inc(s["stc"], 1)
            pre_lo(dve, 17, "lo_d")
            pre_lo(dve, 18, "lo_d")

            dve.wait_ge(s["lnm"], 1)

            def two(i):
                return banks[i][:, :].rearrange("p (a t) -> p a t", a=2)

            dve.wait_ge(s["avc"], H)
            for i in range(2):
                ins = dve.scalar_tensor_tensor(out=c4(yr)[:, 2 * i:2 * i + 2], in0=c4(two(i)), scalar=-1.0 / HD,
                                               in1=yraw[:, 2 * i:2 * i + 2], op0=ALU.mult, op1=ALU.add)
            link(ins)
            dve.tensor_tensor(Kc, yr, yr, ALU.mult).then_inc(s["lnsq"], 1)
            pre_lo(dve, 19, "lo_d")
            dve.wait_ge(s["lnsd"], 2)
            link(dve.reciprocal(Bc, Bc))
            link(dve.tensor_tensor(yr, yr, Bc, ALU.mult))
            for ct in range(CT):
                ins = dve.tensor_scalar(yr[:, ct, :], yr[:, ct, :], VT[:, V_LG + ct:V_LG + ct + 1],
                                        VT[:, V_LB + ct:V_LB + ct + 1], ALU.mult, ALU.add)
            link(ins)
            link(dve.tensor_tensor(yr, yr, vc, ALU.add))
            dve.wait_ge(s["gout"], 2)
            flink(dve.tensor_tensor(yr, yr, gg, ALU.mult), "yr", 1)
            pre_lo(dve, 20, "lo_d")
            pre_lo(dve, 21, "lo_d")
            dve.wait_ge(s["ysplit"], 1)
            dve.tensor_tensor(ysp[:, 1, 1], ym, ysp[:, 1, 0].bitcast(F32), ALU.subtract).then_inc(s["ylo"], 1)
            dve.wait_ge(s["ysplit"], 2)
            dve.tensor_tensor(ysp[:, 0, 1], yr, ysp[:, 0, 0].bitcast(F32), ALU.subtract).then_inc(s["ylo"], 1)

            def mix(g):
                j, br = (g - 20) % 2, 1 - (g - 20) // 2
                for i in range(2):
                    q = 4 * j + 2 * i
                    dve.wait_ge(s["half"], g + 1)
                    src = two(2 * (g % 2) + i)
                    sig = Z[:, 8 * br + q:8 * br + q + 2, :]
                    if g < 22:
                        dve.tensor_tensor(hTm[:, q:q + 2, :], src, sig, ALU.mult).then_inc(s["hm"], 1)
                    else:
                        link(dve.tensor_tensor(Bc[:, 2 * i:2 * i + 2, :], src, sig, ALU.mult))
                        dve.wait_ge(s["hm"], 4)
                        dve.tensor_tensor(hTm[:, q:q + 2, :], hTm[:, q:q + 2, :], Bc[:, 2 * i:2 * i + 2, :], ALU.add)\
                           .then_inc(s["hm"], 1)

            mix(20)
            pre_lo(dve, 22, "lo_d")
            mix(21)
            pre_lo(dve, 23, "lo_d")
            mix(22)
            pre_lo(dve, 24, "lo_d")
            mix(23)
            pre_lo(dve, 25, "lo_d")
            dve.wait_ge(s["hsplit"], 1)
            dve.tensor_tensor(xl, hTm, xh.bitcast(F32), ALU.subtract).then_inc(s["hsplit"], 1)
            dve.wait_ge(s["xre"], 16)
            for g in range(24, 28):
                if g < 26:
                    pre_lo(dve, g + 2, "lo_d")
                dve.wait_ge(s["half"], g + 1)
                v = xrs[:, :, 256 * (g - 24):256 * (g - 23)]
                dve.tensor_tensor(v, v, two(4 + g % 2), ALU.add).then_inc(s["x2"], 1)
            dve.wait_ge(s["r2q"], 1)
            link(dve.reciprocal(st_[:, 6:8], st_[:, 4:6]))
            dve.wait_ge(s["gbc"], 16)
            dve.wait_ge(s["x2"], 4)
            xn2 = R(O_XNT, TT, D)
            for a in range(TT):
                dve.scalar_tensor_tensor(out=xn2[:, a, :], in0=xrs[:, a, :], scalar=st_[:, 6 + a:7 + a], in1=gbc,
                                         op0=ALU.mult, op1=ALU.mult).then_inc(s["xn2"], 1)

            lg = R(O_B, 2, NG + NE)
            eg = R(O_B + 80, 2, NG)
            d21 = R(O_B + 100, 2)
            one1, one2, sel, key = (R(O_B + 128 + 64 * i, 2, NE) for i in range(4))
            lem = R(O_B + 384, 2, NE)
            cum = R(O_B + 448, 2, NE)
            sm = R(O_B + 520, 8, 2)
            ggrp = R(O_B + 540, 2, NG)
            gk = R(O_B + 550, 2, NG)
            cnt = R(O_B + 560, NE)
            descg, desce = cst[:, C_DESC:C_DESC + NG], cst[:, C_DESC + NG:C_DESC + NG + NE]
            dve.wait_ge(s["wr"], 64)
            dve.wait_ge(s["logit"], 1)
            link(dve.tensor_tensor(lg, banks[4][:, 0:2 * (NG + NE)].rearrange("p (a n) -> p a n", a=2), bcast(brc, 1, 2), ALU.add))

            def first_max(onehot, tmp, val, m_, desc, n, km):
                link(dve.tensor_reduce(m_, val, AX.X, ALU.max))
                link(dve.tensor_tensor(tmp, val, bcast(m_, 2, n), ALU.is_equal))
                link(dve.tensor_tensor(tmp, tmp, bcast(desc, 1, 2), ALU.mult))
                link(dve.tensor_reduce(km, tmp, AX.X, ALU.max))
                link(dve.tensor_tensor(onehot, tmp, bcast(km, 2, n), ALU.is_equal))

            first_max(ggrp, gk, lg[:, :, 0:NG], sm[:, 0, :], descg, NG, sm[:, 1, :])
            flink(dve.tensor_tensor(eg, lg[:, :, 0:NG], bcast(sm[:, 0, :], 2, NG), ALU.subtract), "rt", 1)
            link(dve.tensor_scalar(gk, ggrp, 1.0, BIG, ALU.subtract, ALU.mult))
            for a in range(2):
                ins = dve.tensor_tensor(lem[:, a, :].rearrange("p (g e) -> p g e", g=NG),
                                        lg[:, a, NG:NG + NE].rearrange("p (g e) -> p g e", g=NG),
                                        bcast(gk[:, a, :], 2, EG), ALU.add)
            link(ins)
            first_max(one1, key, lem, sm[:, 2, :], desce, NE, sm[:, 3, :])
            link(dve.scalar_tensor_tensor(out=lem, in0=one1, scalar=-3.0 * BIG, in1=lem, op0=ALU.mult, op1=ALU.add))
            first_max(one2, key, lem, sm[:, 4, :], desce, NE, sm[:, 5, :])
            flink(dve.tensor_tensor(d21, sm[:, 4, :], sm[:, 2, :], ALU.subtract), "rt", 2)
            flink(dve.tensor_tensor(sel, one1, one2, ALU.add), "cum", 1)
            dve.wait_ge(s["gates"], 2)
            link(dve.tensor_reduce(sm[:, 6, :], eg, AX.X, ALU.add))
            link(dve.tensor_scalar(sm[:, 7, :], d21, 1.0, None, ALU.add))
            link(dve.tensor_tensor(sm[:, 6, :], sm[:, 6, :], sm[:, 7, :], ALU.mult))
            link(dve.reciprocal(sm[:, 6, :], sm[:, 6, :]))
            dve.wait_ge(s["rte"], 16)
            dve.tensor_copy(rowv[:, :, 0, 2], sm[:, 6, :])
            dve.tensor_tensor(rowv[:, :, 1, 2], sm[:, 6, :], d21, ALU.mult)
            dve.wait_ge(s["cumd"], 1)
            link(dve.tensor_tensor(cum, banks[5][:, 0:2 * NE].rearrange("p (a n) -> p a n", a=2),
                                   bcast(cst[:, C_EB:C_EB + NE], 1, 2), ALU.add))
            for k, oh in enumerate((one1, one2)):
                link(dve.tensor_tensor(key, oh, cum, ALU.mult))
                link(dve.tensor_reduce(sm[:, k, :], key, AX.X, ALU.add))
                ins = dve.tensor_copy(addr[:, :, k].bitcast(U32), sm[:, k, :])
            ins.then_inc(s["addr"], 1)
            fl = R(O_B + 600, 3, NE, p1=1)
            fl96 = R(O_B + 600, 3 * NE, p1=1)
            inc = R(O_B + 700, 3 * NE, p1=1)
            of = R(O_B + 100 + 4, 20, p1=1)
            link(dve.tensor_copy(cnt[0:1, :], banks[5][0:1, 2 * NE:3 * NE]))
            for c in range(3):
                ins = dve.tensor_scalar(fl[:, c, :], cnt[0:1, :], S * (c + 1) + 0.5, None, ALU.is_gt)
            link(ins)
            link(dve.tensor_tensor_scan(inc, ones[0:1, 0:3 * NE], fl96, 0.0, ALU.mult, ALU.add))
            link(dve.tensor_copy(over[0:1, 0:1].bitcast(I32), inc[:, 3 * NE - 1:3 * NE]))
            link(dve.tensor_tensor(inc, inc, fl96, ALU.mult))
            for w_, (o, col) in enumerate(((1, C_UE), (9, C_UB))):
                for i in range(MAXO):
                    link(dve.tensor_scalar(fl96, inc, float(i + 1), None, ALU.is_equal))
                    link(dve.tensor_tensor(fl96, fl96, cst[0:1, col:col + 3 * NE], ALU.mult))
                    link(dve.tensor_reduce(of[:, 0:1], fl96, AX.X, ALU.add))
                    link(dve.tensor_copy(over[0:1, o + i:o + i + 1].bitcast(I32), of[:, 0:1]))
            dve.sem_inc(s["ovf"], 1)

            def xsplit(n, b):
                dve.wait_ge(s["xgT"], n + 1)
                if not isinstance(n, int) or n >= 2:
                    dve.wait_ge(s["half"], up_done(n - 2))
                src = banks[6][:, :].rearrange("p (k t) -> p k t", k=KD)
                flink(dve.tensor_copy(xsx[b][:, :, 0:S], src), "xsx", 2 * n + 1)
                dve.tensor_tensor(xsx[b][:, :, S:2 * S], src, xsx[b][:, :, 0:S].bitcast(F32), ALU.subtract)\
                   .then_inc(s["xsx"], 1)

            def fold_gate(n):
                dve.wait_ge(s["tg"], n + 1)
                dve.tensor_tensor(gf, banks[0][0:S, :], tg, ALU.add).then_inc(s["gf"], 1)

            def gated(n, b):
                dve.wait_ge(s["sg"], n + 1)
                dve.wait_ge(s["vg"], 16 * (n + 1))
                dve.scalar_tensor_tensor(out=gf, in0=gf, scalar=vgb[0:S, b, 2:3], in1=sg, op0=ALU.mult, op1=ALU.mult)\
                   .then_inc(s["m"], 1)

            def hidden(n):
                dve.wait_ge(s["tu"], n + 1)
                flink(dve.tensor_tensor(ub, banks[1][0:S, :], tu, ALU.add), "uf", n + 1)
                if not isinstance(n, int) or n >= 1:
                    dve.wait_ge(s["hT"], n)
                dve.wait_ge(s["m"], n + 1)
                dve.tensor_tensor(hb, ub, gf, ALU.mult).then_inc(s["h"], 1)

            def hsplit(n, late=False):
                dve.wait_ge(s["hT"], n + 1)
                if not isinstance(n, int) or n >= 1:
                    dve.wait_ge(s["half"], down_done(n - 1, 1, late))
                src = banks[7][:, 0:256].rearrange("p (k t) -> p k t", k=4)
                flink(dve.tensor_copy(xsh[:, :, 0:S], src), "hs", 2 * n + 1)
                dve.tensor_tensor(xsh[:, :, S:2 * S], src, xsh[:, :, 0:S].bitcast(F32), ALU.subtract)\
                   .then_inc(s["hs"], 1)

            def fold_down(n, b, j):
                dve.wait_ge(s["ty"], 2 * n + j + 1)
                if j == 0 and (not isinstance(n, int) or n >= 2):
                    dve.wait_ge(s["sc"], 16 * (n - 1))
                dve.tensor_tensor(ysb[b][:, j, :], banks[2 + j][0:S, :], ty, ALU.add).then_inc(s["y_"], 1)

            dve.wait_ge(s["half"], 2 * PRE)
            xsplit(0, 0)
            for i in range(4):
                first_lo(dve, i, "lo_d")
            fold_gate(0)

            def step(n, n0, head=False, tail=False):
                b = n0 % 2
                moe_lo(dve, n, n0, 0, "lo_d")
                gated(n - 1, 1 - b)
                if not head:
                    fold_down(n - 2, b, 1)
                moe_lo(dve, n, n0, 1, "lo_d")
                moe_lo(dve, n, n0, 2, "lo_d")
                hidden(n - 1)
                moe_lo(dve, n, n0, 3, "lo_d")
                hsplit(n - 1)
                if not tail:
                    xsplit(n + 1, 1 - b)
                moe_lo(dve, n, n0, 4, "lo_d")
                fold_gate(n)
                moe_lo(dve, n, n0, 5, "lo_d")
                fold_down(n - 1, 1 - b, 0)

            xsplit(1, 1)
            step(1, 1, head=True)
            with dve.Fori(0, (NE - 4) // 2) as it:
                for j in range(2):
                    step(2 * it + 2 + j, 2 + j)
            step(NE - 2, NE - 2)
            step(NE - 1, NE - 1, tail=True)
            last_lo(dve, 0, "lo_d")
            gated(NE - 1, 1)
            fold_down(NE - 2, 0, 1)
            last_lo(dve, 1, "lo_d")
            hidden(NE - 1)
            hsplit(NE - 1)
            fold_down(NE - 1, 1, 0)
            fold_down(NE - 1, 1, 1)

            n_over = over_count(dve)
            with dve.If(n_over > 0):
                with dve.Fori(0, n_over) as i:
                    n = NE + i
                    xsplit(n, 0)
                    for q in range(3):
                        over_lo(dve, i, q, "lo_d")
                    fold_gate(n)
                    gated(n, 0)
                    for q in range(3, 6):
                        over_lo(dve, i, q, "lo_d")
                    hidden(n)
                    hsplit(n, late=True)
                    dve.wait_ge(s["sc"], 16 * n)
                    for j in range(2):
                        dve.wait_ge(s["ty"], 2 * n + j + 1)
                        dve.tensor_tensor(ysb[0][:, j, :], banks[2 + j][0:S, :], ty, ALU.add).then_inc(s["y_"], 1)

            dve.wait_ge(s["ychunk"], 32)
            link(dve.tensor_tensor(xrs, xrs, yall[:, :, 0:D], ALU.add))
            dve.tensor_tensor(xrs, xrs, yall[:, :, D:2 * D], ALU.add).then_inc(s["fin"], 1)

        @block.tensor
        def _(pe):
            pe.wait_ge(s["consts"], 16)
            pe.wait_ge(s["vecs"], 16 * 14)
            pe.transpose(banks[6][:, 0:NVEC], R(O_K, P, p1=NVEC), ident[0:NVEC, 0:NVEC]).then_inc(s["vecT"], 1)
            pe.wait_ge(s["biasc"], 32)
            pe.matmul(banks[7][0:H, 0:NV], R(O_G + 768, H, p1=32), R(O_G, NV, p1=32), start=True, stop=True)\
              .then_inc(s["vecmm"], 1)
            pe.wait_ge(s["xsn"], TT)
            for q in range(4):
                for k in (2 * q, 2 * q + 1):
                    for a in range(TT):
                        o = T * (k % 2) + P * a
                        ins = pe.transpose(banks[2 + q][:, o:o + P], xin[:, a, P * k:P * k + P], ident)
                ins.then_inc(s["xT"], 1)

            def passes(bank_ap, stat, mov, first, last, fresh):
                for i, (a, b) in enumerate(((0, 0), (0, 1), (1, 0))):
                    ins = pe.matmul(bank_ap, stat[a], mov[b], start=(first and i == 0 and fresh),
                                    stop=(last and i == 2), skip_group_check=True)
                return ins

            def ready(g):
                pe.wait_ge(s["lo_d"], g + 1)
                pe.wait_ge(s["lo_p"], g + 1)

            def project(g):
                ready(g)
                if g == 0:
                    pe.wait_ge(s["xsplit"], 2)
                if g >= 2:
                    pe.wait_ge(s["projev"], g - 1)
                h_, l_ = part_view(wh, g % NB, "cols"), part_view(wl, g % NB, "cols")
                for a in range(2):
                    for k in range(KD):
                        ins = passes(banks[6 + g % 2][:, T * a:T * a + T],
                                     (h_[:, k, P * a:P * a + P], l_[:, k, P * a:P * a + P]),
                                     (xh[:, k, :], xl[:, k, :]), k == 0, k == KD - 1, True)
                ins.then_inc(s["half"], 1)

            def lora_in():
                pe.wait_ge(s["musplit"], 1)
                for a in range(2):
                    for k in range(KD):
                        pe.matmul(banks[2][:, T * a:T * a + T], WL[:, k, P * a:P * a + P], xnT[:, k, 1:T + 1],
                                  start=(k == 0), stop=False)
                        ins = pe.matmul(banks[2][:, T * a:T * a + T], WM[:, k, P * a:P * a + P], xnT[:, k, 0:T],
                                        start=False, stop=(k == KD - 1))
                ins.then_inc(s["lora"], 1)

            def lora_out():
                pe.wait_ge(s["lt"], 3)
                pe.wait_ge(s["lora2"], 48)
                pe.wait_ge(s["vec"], 1)
                lt = R(O_V, 2, T)
                w2s = R(O_YR, CW)
                g2s = R(O_YR + CW, CW)
                for ct in range(CT):
                    o = T * (ct % 2)
                    pe.matmul(banks[3 + ct // 2][:, o:o + T], w2s[0:64, P * ct:P * ct + P], lt[0:64, 0, :], start=True, stop=True)
                    pe.matmul(banks[(5, 0)[ct // 2]][:, o:o + T], w2s[64:128, P * ct:P * ct + P], lt[64:128, 0, :],
                              start=True, stop=True)
                    ins = pe.matmul(banks[1 + ct // 2][:, o:o + T], g2s[:, P * ct:P * ct + P], lt[:, 1, :], start=True, stop=True)
                ins.then_inc(s["loraout"], 1)

            def head_sums(src, bank_0, bank_1):
                for j, bank_i in enumerate((bank_0, bank_1)):
                    ins = pe.matmul(banks[bank_i][:, :], bones, src[:, 512 * j:512 * j + 512], start=True, stop=True)
                return ins

            def flat_ct(t):
                return t.rearrange("p c t -> p (c t)")

            def to_tokens(src, a, bank_i):
                for ct in range(CT):
                    ins = pe.transpose(banks[bank_i][:, P * ct:P * ct + P], src[:, ct, P * a:P * a + P], ident)
                return ins

            for g in range(12):
                project(g)
                if g == 1:
                    lora_in()
                elif g == 3:
                    lora_out()
                elif g == 7:
                    pe.wait_ge(s["rk_sq"], 1)
                    pe.wait_ge(s["sgm"], 8)
                    pe.wait_ge(s["gout"], 2)
                    head_sums(flat_ct(nr), 0, 1).then_inc(s["rk_ss"], 1)
                elif g == 8:
                    pe.wait_ge(s["v_ch"], 1)
                    pe.wait_ge(s["rk_nr"], 2)
                    for a in range(2):
                        to_tokens(vc, a, a).then_inc(s["tokT"], 1)
                elif g == 9:
                    pe.wait_ge(s["bonus"], 1)
                    head_sums(flat_ct(df), 2, 3).then_inc(s["bons"], 1)
                    pe.wait_ge(s["sq"], 1)
                    head_sums(sqb[:, 0, :], 4, 5).then_inc(s["ssum"], 1)
                elif g == 10:
                    pe.wait_ge(s["sq"], 2)
                    pe.wait_ge(s["tok"], 2)
                    head_sums(sqb[:, 1, :], 0, 1).then_inc(s["ssum"], 1)

            def heads_of(h):
                return slice(HD * (h % 2), HD * (h % 2) + HD), h // 2

            def scores(h):
                hp, ct = heads_of(h)
                if h == 0:
                    pe.wait_ge(s["qkn"], 2)
                    pe.wait_ge(s["hank"], 32)
                if h < 2:
                    pe.wait_ge(s["tok"], 3 + h)
                else:
                    pe.wait_ge(s["avc"], h - 1)
                bk_ = banks[6 + h % 2]
                pe.matmul(bk_[:, 0:256], JJ, HK[:, h, :], start=True, stop=False)
                pe.matmul(bk_[:, 0:256], qb[hp, ct, P:T], kb[hp, ct, :], start=False, stop=True)
                pe.matmul(bk_[:, 256:384], JJ, HK[:, h, P:2 * P], start=True, stop=False)
                pe.matmul(bk_[:, 256:384], qb[hp, ct, 0:P], kb[hp, ct, 0:P], start=False, stop=True)\
                  .then_inc(s["score"], 1)

            def turn(h):
                pe.wait_ge(s["pnorm"], h + 1)
                for a in range(3):
                    ins = pe.transpose(banks[6 + h % 2][:, P * a:P * a + P], PR[:, h % 3, P * a:P * a + P], ident)
                ins.then_inc(s["pT"], 1)

            def values(h):
                hp, ct = heads_of(h)
                pe.wait_ge(s["pTc"], h + 1)
                if h == 0:
                    pe.wait_ge(s["vtok"], 2)
                o, pt = banks[6 + h % 2], PT_[:, h % 2, :].rearrange("p (a t) -> p a t", a=3)
                pe.matmul(o[hp, 0:P], vtm[:, 0, HD * h:HD * h + HD], pt[:, 2, :], start=True, stop=True)
                pe.matmul(o[hp, P:T], vtm[:, 0, HD * h:HD * h + HD], pt[:, 0, :], start=True, stop=False)
                pe.matmul(o[hp, P:T], vtm[:, 1, HD * h:HD * h + HD], pt[:, 1, :], start=False, stop=True)\
                  .then_inc(s["av"], 1)

            def early_gap(L):
                if L == 0:
                    pe.wait_ge(s["projev"], 12)
                    to_tokens(ym, 0, 6).then_inc(s["vtT"], 1)
                if L == 1:
                    pe.wait_ge(s["vtok"], 2)
                    to_tokens(Bc, 0, 6).then_inc(s["tokT"], 1)
                    to_tokens(Kc, 0, 7).then_inc(s["tokT"], 1)
                if 2 <= L < H + 2:
                    turn(L - 2)
                if 3 <= L < H + 3:
                    values(L - 3)
                if L == 11:
                    project(14)

            def late_gap(L):
                if L == 0:
                    to_tokens(ym, 1, 7).then_inc(s["vtT"], 1)
                if 1 <= L < H + 1:
                    scores(L - 1)
                if 9 <= L < 11:
                    pe.wait_ge(s["avc"], L - 2)
                    project(L + 3)

            pe.wait_ge(s["ar"], 1)
            pe.wait_ge(s["qks"], 4)
            pe.wait_ge(s["bonv"], 1)
            for c in range(2):
                tok = slice(P * c, P * c + P)
                if c == 1:
                    pe.wait_ge(s["yc"], 1)
                    pe.wait_ge(s["stc"], 1)
                for b in range(2):
                    if b == 1:
                        pe.wait_ge(s["x0"], 2 * c + 1)
                    for u in range(4):
                        hp, ct = heads_of(4 * b + u)
                        if b == 1:
                            pe.wait_ge(s["gcp"], 8 * c + u + 1)
                        ar = AR[hp, ct, c].rearrange("p a i -> p (a i)")
                        pe.matmul(banks[u][:, 0:256], Bc[hp, ct, tok], ar, start=True, stop=True)
                        pe.matmul(banks[u][:, 256:512], Kc[hp, ct, tok], ar, start=True, stop=True).then_inc(s["gram"], 1)
                        ins = pe.matmul(banks[4 + u % 2][:, P * (u // 2):P * (u // 2) + P], AR[hp, ct, c, 0, :], Bc[hp, ct, tok],
                                        start=True, stop=True)
                    ins.then_inc(s["gl"], 1)
                for lev in range(1, 7):
                    L = 6 * c + lev - 1
                    for b in range(2):
                        n = 2 * L + b
                        pe.wait_ge(s["nt"], n + 1)
                        pe.wait_ge(s["x0"], 2 * c + 2)
                        if n >= 2:
                            pe.wait_ge(s["xx"], n - 1)
                            pe.wait_ge(s["t1c"], n - 1)
                        if lev == 1:
                            pe.wait_ge(s["gcp"], 8 * c + 8)
                        for u in range(4):
                            ins = pe.matmul(banks[3 * b][:, P * u:P * u + P], NTo[b][:, u, :], XXo[b][:, u, 0, :],
                                            start=True, stop=True)
                        ins.then_inc(s["t1"], 1)
                    early_gap(L)
                    for b in range(2):
                        n = 2 * L + b
                        pe.wait_ge(s["t1c"], n + 1)
                        for u in range(4):
                            o = banks[3 * b + 1 + u // 2]
                            c0 = 256 * (u % 2)
                            pe.matmul(o[:, c0:c0 + P], XXo[b][:, u, 1, :], T1o[b][:, u, :], start=True, stop=True)
                            ins = pe.matmul(o[:, c0 + P:c0 + 2 * P], T1o[b][:, u, :], XXo[b][:, u, 1, :],
                                            start=True, stop=True)
                        ins.then_inc(s["dx"], 1)
                    late_gap(L)
                pe.wait_ge(s["xx"], 12 * c + 12)
                if c == 0:
                    pe.wait_ge(s["tok"], 4)
                for h in range(H):
                    hp, ct = heads_of(h)
                    v_ = Vtok[:, c, HD * h:HD * h + HD]
                    zo = banks[3 * (h % 2)][:, HD * ct:HD * ct + HD]
                    ins = pe.matmul(zo, GRo[h // 4][:, h % 4, 2, :], v_, start=True, stop=(c == 0))
                    if c == 1:
                        ins = pe.matmul(zo, AR[hp, ct, 1, 0, :], St[hp, ct, :], start=False, stop=True)
                ins.then_inc(s["z"], 1)
                if c == 1:
                    project(15)
                pe.wait_ge(s["zc"], 2 * c + 2)
                for h in range(H):
                    ins = pe.matmul(banks[1][:, HD * h:HD * h + HD], XXo[h // 4][:, h % 4, 1, :],
                                    Zb[:, HD * h:HD * h + HD], start=True, stop=True)
                ins.then_inc(s["u"], 1)
                pe.wait_ge(s["uc"], c + 1)
                if c == 0:
                    for h in range(H):
                        hp, ct = heads_of(h)
                        so = banks[3][hp, HD * ct:HD * ct + HD]
                        pe.matmul(so, Btok[:, HD * h:HD * h + HD], Ub[:, HD * h:HD * h + HD], start=True, stop=False)
                        ins = pe.matmul(so, Ktok[:, HD * h:HD * h + HD], Vtok[:, 0, HD * h:HD * h + HD],
                                        start=False, stop=True)
                    ins.then_inc(s["st"], 1)
                for h in range(H):
                    hp, ct = heads_of(h)
                    yo = banks[2][hp, P * ct:P * ct + P]
                    G_ = GRo[h // 4][:, h % 4]
                    pe.matmul(yo, Vtok[:, c, HD * h:HD * h + HD], G_[:, 3, :], start=True, stop=False)
                    ins = pe.matmul(yo, Ub[:, HD * h:HD * h + HD], G_[:, 1, :], start=False, stop=(c == 0))
                    if c == 1:
                        ins = pe.matmul(yo, St[hp, ct, :], AR[hp, ct, 1, 1, :], start=False, stop=True)
                ins.then_inc(s["y"], 1)

            pe.wait_ge(s["yc"], 2)
            for i in range(2):
                ins = pe.matmul(banks[i][:, :].rearrange("p (a c i) -> p a c i", a=2, c=2), bones,
                                yraw[:, 2 * i:2 * i + 2], start=True, stop=True)
            ins.then_inc(s["lnm"], 1)
            project(16)
            pe.wait_ge(s["lnsq"], 1)
            head_sums(flat_ct(Kc), 2, 3).then_inc(s["lnv"], 1)
            for g in range(17, 20):
                project(g)

            pe.wait_ge(s["lnsd"], 2)
            for g in range(20, 24):
                ready(g)
                pe.wait_ge(s["ysplit"], 1 if g < 22 else 2)
                pe.wait_ge(s["ylo"], 1 if g < 22 else 2)
                if g >= 22:
                    pe.wait_ge(s["hm"], 2 * (g - 21))
                br = 1 - (g - 20) // 2
                h_, l_ = part_view(wh, g % NB, "br"), part_view(wl, g % NB, "br")
                for q in range(4):
                    for k in range(CT):
                        ins = passes(banks[2 * (g % 2) + q // 2][:, T * (q % 2):T * (q % 2) + T],
                                     (h_[:, k, P * q:P * q + P], l_[:, k, P * q:P * q + P]),
                                     (ysp[:, br, 0, k, :], ysp[:, br, 1, k, :]), k == 0, k == CT - 1, True)
                ins.then_inc(s["half"], 1)
            pe.wait_ge(s["hsplit"], 2)
            for g in range(24, 28):
                ready(g)
                if g >= 26:
                    pe.wait_ge(s["x2"], g - 25)
                h_, l_ = part_view(wh, g % NB, "cols"), part_view(wl, g % NB, "cols")
                for a in range(TT):
                    tk = slice(P * a, P * a + P)
                    for k in range(KD):
                        ins = passes(banks[4 + g % 2][:, T * a:T * a + T], (xh[:, k, tk], xl[:, k, tk]),
                                     (h_[:, k, :], l_[:, k, :]), k == 0, k == KD - 1, True)
                ins.then_inc(s["half"], 1)

            pe.wait_ge(s["xn2"], TT)
            xn2 = R(O_XNT, TT, D)
            for q in range(4):
                for k in (2 * q, 2 * q + 1):
                    for a in range(TT):
                        o = T * (k % 2) + P * a
                        ins = pe.transpose(banks[q][:, o:o + P], xn2[:, a, P * k:P * k + P], ident)
                ins.then_inc(s["xn2T"], 1)
            pe.wait_ge(s["xn2Tc"], 4)
            pe.wait_ge(s["wr"], 64)
            pe.wait_ge(s["x2"], 4)
            NR_ = NG + NE
            for a in range(TT):
                for k in range(KD):
                    ins = pe.matmul(banks[4][:, NR_ * a:NR_ * a + NR_], hTm[:, k, P * a:P * a + P], Wr[:, k, :],
                                    start=(k == 0), stop=(k == KD - 1))
            ins.then_inc(s["logit"], 1)
            pe.wait_ge(s["cum"], 1)
            sel = R(O_B + 256, 2, NE)
            pe.matmul(banks[5][:, 0:NE], tri, sel[:, 0, :], start=True, stop=True)
            pe.matmul(banks[5][:, NE:2 * NE], tri, sel[:, 1, :], start=True, stop=False)
            pe.matmul(banks[5][:, NE:2 * NE], ones, sel[:, 0, :], start=False, stop=True)
            pe.matmul(banks[5][:, 2 * NE:3 * NE], ones, sel[:, 0, :], start=True, stop=False)
            pe.matmul(banks[5][:, 2 * NE:3 * NE], ones, sel[:, 1, :], start=False, stop=True).then_inc(s["cumd"], 1)

            def turn_x(n, b):
                pe.wait_ge(s["xg"], 16 * (n + 1))
                if not isinstance(n, int) or n >= 1:
                    pe.wait_ge(s["xsx"], 2 * n)
                pe.nop(nofuse=True)
                v = xg[b].rearrange("p (q k) -> p q k", k=KD)
                for k in range(KD):
                    ins = pe.transpose(banks[6][:, S * k:S * k + S], v[:, :, k], ident[0:S, 0:S])
                ins.then_inc(s["xgT"], 1)

            def wide(bank_i, stat, buf, k0, first, last):
                h_, l_ = part_view(wh, buf, "rows"), part_view(wl, buf, "rows")
                for k in range(4):
                    pe.matmul(banks[bank_i][:, :], stat[:, k0 + k, :], h_[:, k, :], start=(first and k == 0), stop=False)
                    ins = pe.matmul(banks[bank_i][:, :], stat[:, k0 + k, :], l_[:, k, :], start=False,
                                    stop=(last and k == 3))
                return ins

            def gate_half(n, b, g, buf, j):
                ready(g)
                if j == 0:
                    pe.wait_ge(s["xsx"], 2 * n + 2)
                    if not isinstance(n, int) or n >= 1:
                        pe.wait_ge(s["gf"], n)
                ins = wide(0, xsx[b], buf, 4 * j, j == 0, j == 1)
                ins.then_inc(s["half"], 1)

            def up_half(n, b, g, buf, j):
                ready(g)
                if j == 0 and (not isinstance(n, int) or n >= 1):
                    pe.wait_ge(s["uf"], n)
                ins = wide(1, xsx[b], buf, 4 * j, j == 0, j == 1)
                ins.then_inc(s["half"], 1)

            def turn_h(n):
                pe.wait_ge(s["h"], n + 1)
                if not isinstance(n, int) or n >= 1:
                    pe.wait_ge(s["hs"], 2 * n)
                pe.nop(nofuse=True)
                v = hb.rearrange("p (q k) -> p q k", k=4)
                for k in range(4):
                    ins = pe.transpose(banks[7][:, S * k:S * k + S], v[:, :, k], ident[0:S, 0:S])
                ins.then_inc(s["hT"], 1)

            def down_half(n, g, buf, j):
                ready(g)
                if j == 0:
                    pe.wait_ge(s["hs"], 2 * n + 2)
                if not isinstance(n, int) or n >= 1:
                    pe.wait_ge(s["y_"], 2 * n - 1 + j)
                ins = wide(2 + j, xsh, buf, 0, True, True)
                ins.then_inc(s["half"], 1)

            turn_x(0, 0)
            for j in range(2):
                gate_half(0, 0, 2 * PRE + j, (2 * PRE + j) % NB, j)
            turn_x(1, 1)
            for j in range(2):
                up_half(0, 0, 2 * PRE + 2 + j, (2 * PRE + 2 + j) % NB, j)

            def step(n, n0, tail=False):
                b = n0 % 2
                place = [moe_place(n0, i)[0] for i in range(6)]
                for j in range(2):
                    gate_half(n, b, moe_half(n, j), place[j], j)
                turn_h(n - 1)
                if not tail:
                    turn_x(n + 1, 1 - b)
                for j in range(2):
                    down_half(n - 1, moe_half(n, 2 + j), place[2 + j], j)
                for j in range(2):
                    up_half(n, b, moe_half(n, 4 + j), place[4 + j], j)

            step(1, 1)
            with pe.Fori(0, (NE - 4) // 2) as it:
                for j in range(2):
                    step(2 * it + 2 + j, 2 + j)
            step(NE - 2, NE - 2)
            step(NE - 1, NE - 1, tail=True)
            turn_h(NE - 1)
            for j in range(2):
                g = 2 * PRE + 2 * LAST + j
                down_half(NE - 1, g, g % NB, j)

            n_over = over_count(pe)
            with pe.If(n_over > 0):
                with pe.Fori(0, n_over) as i:
                    n = NE + i
                    turn_x(n, 0)
                    for j in range(2):
                        gate_half(n, 0, over_half(i, j), (2 * PRE + j) % NB, j)
                    for j in range(2):
                        up_half(n, 0, over_half(i, 2 + j), (2 * PRE + 2 + j) % NB, j)
                    turn_h(n)
                    for j in range(2):
                        down_half(n, over_half(i, 4 + j), (2 * PRE + 4 + j) % NB, j)


_INS = ['x', 'norm_mix_g', 'norm_ffn_g', 'w_in', 'mu_rkv', 'mu_x', 'w0', 'w1', 'w2', 'a0', 'a1', 'a2', 'g1', 'g2',
        'k_k', 'k_a', 'r_k', 'lnx_g', 'lnx_b', 'q_gain', 'k_gain', 'rel_bias', 'w_br_rwkv', 'w_br_moba', 'w_out',
        'w_grp', 'b_grp', 'w_exp', 'b_exp', 'w_gate', 'w_up', 'w_down']


def shape_constants():
    import math

    import numpy as np
    i = np.arange(P)
    c = np.zeros((P, NCONST), np.float32)
    c[:, C_ID:C_ID + P] = np.eye(P)
    c[:, C_BO:C_BO + P] = (i[:, None] // HD == i[None, :] // HD)
    for lev in range(7):
        half = 1 << lev
        m = (i[:, None] // (2 * half) == i[None, :] // (2 * half)) & (i[:, None] % (2 * half) < half) \
            & (i[None, :] % (2 * half) >= half)
        c[:, C_MK + lev * P:C_MK + (lev + 1) * P] = m
    c[:, C_TRI:C_TRI + P] = i[:, None] < i[None, :]
    c[:, C_ONE:C_ONE + P] = 1
    c[:, C_DESC:C_DESC + NG] = np.arange(NG, 0, -1)
    c[:, C_DESC + NG:C_DESC + NG + NE] = np.arange(NE, 0, -1)
    c[:, C_EB:C_EB + NE] = T * np.arange(NE)
    e = np.tile(np.arange(NE), 3)
    c[:, C_UE:C_UE + 3 * NE] = e
    c[:, C_UB:C_UB + 3 * NE] = e * NC + 1 + np.arange(3 * NE) // NE
    c[:, C_M0T:C_M0T + P] = c[:, C_MK:C_MK + P].T
    c[:, C_EPS:C_EPS + 2] = NORM_EPS, LNX_EPS
    bc_ = np.zeros((P, 896), np.float32)
    for m in range(NV):
        n = T - 1 - m
        if n < 0:
            bc_[:, 384 + m] = -BIG
            continue
        if n < 16:
            b = n
        else:
            b = min(31, 16 + int(np.float32(np.log(np.float32(n) / np.float32(16))) / np.float32(math.log(8)) * np.float32(16)))
        bc_[b, m] = 1
    bc_[:, 768:896] = np.eye(P)[::-1]
    rows = np.zeros((P, 2, 2, 4), np.int32)
    for a in range(2):
        for k in range(2):
            rows[:, a, k, 0] = P * a + i
            rows[:, a, k, 1] = 2 * (P * a + i) + k
    return c, bc_, rows.reshape(P, 16)


def kernel(**inputs):
    import numpy as _np
    import concourse.bacc as _bacc
    from concourse import mybir as _mybir
    from concourse.bass_utils import run_bass_kernel_spmd as _run

    nc = _bacc.Bacc("TRN2", target_bir_lowering=False, num_devices=1)
    arrays, args = {}, []

    def give(name, a):
        arrays[f"in_{name}_dram"] = a
        args.append(nc.dram_tensor(f"in_{name}_dram", a.shape, _mybir.dt.from_np(a.dtype), kind="ExternalInput").ap())

    for name in _INS:
        give(name, _np.ascontiguousarray(inputs[name]))
    for name, a in zip(("consts", "bias_consts", "slot_rows"), shape_constants()):
        give(name, a)
    args.append(nc.dram_tensor("out_0_dram", (1, T, D), _mybir.dt.float32, kind="ExternalOutput").ap())
    build(nc, *args)
    r = _run(nc, [arrays], core_ids=[0])
    return r.results[0]["out_0_dram"]
```

```python
from contextlib import ExitStack

import concourse.bass as bass
from concourse import mybir

F32 = mybir.dt.float32
F32R = mybir.dt.float32r
I32 = mybir.dt.int32
U32 = mybir.dt.uint32
ALU = mybir.AluOpType
ACT = mybir.ActivationFunctionType
AX = mybir.AxisListType

P = 128
T, D = 256, 1024
TT, KD = T // P, D // P
CW = 512
CT = CW // P
H, HD = 8, 64
NG, EG = 4, 8
NE = NG * EG
FE = 512
S = 32
NC = T // S
MAXO = 2 * T // (S + 1)
MAXP = 16
NV = 2 * T - 129
DECAY = 0.6065306597126334
NORM_EPS, LNX_EPS = 1e-6, 64e-5
BIG = 1e30

CHUNK = 4096
HALF = CHUNK // 2
LO_D = 11
NB = 3
NS = 6
PRE = 14
PCH = [CW, 0, 2 * CW, 3 * CW, 4 * CW, 5 * CW] + [6 * CW + CW * i for i in range(4)]

C_ID, C_BO, C_MK, C_TRI, C_ONE = 0, 128, 256, 256 + 7 * 128, 256 + 8 * 128
C_DESC = C_ONE + 128
C_EB = C_DESC + NG + NE
C_IP = C_EB + NE
C_PI = C_IP + 8
C_M0T = C_PI + 1
C_EPS = C_M0T + P
NCONST = C_EPS + 2
V_GMIX, V_MRKV, V_MX, V_W0, V_A0, V_KK, V_KA, V_RK, V_LG, V_LB, V_QG, V_KG = 0, 8, 20, 44, 48, 52, 56, 60, 64, 68, 72, 73
NVEC = 74


def bcast(ap, axis, n):
    dims = [list(d) for d in ap.ap]
    dims.insert(axis, [0, n])
    return bass.AP(ap.tensor, ap.offset, dims)


def build(nc, x, norm_mix_g, norm_ffn_g, w_in, mu_rkv, mu_x, w0, w1, w2, a0, a1, a2, g1, g2, k_k, k_a, r_k,
          lnx_g, lnx_b, q_gain, k_gain, rel_bias, w_br_rwkv, w_br_moba, w_out, w_grp, b_grp, w_exp, b_exp,
          w_gate, w_up, w_down, consts, bias_consts, slot_rows, out):
    with ExitStack() as ctx:
        def sb(name, shape, dt=F32):
            return ctx.enter_context(nc.sbuf_tensor(name, shape, dt))

        ring = sb("ring", [P, NS, CHUNK])
        wh = sb("wh", [P, NB, HALF], F32R)
        wl = sb("wl", [P, NB, HALF], F32R)
        xs = sb("xs", [P, 4096], F32R)
        reg = sb("reg", [P, 12248])
        banks = [ctx.enter_context(nc.psum_tensor(f"bank{i}", [P, 512], F32)) for i in range(8)]

        sem_names = (
            "consts gain vecs vecs2 lora_w lora2 biasc xre "
            "rms0 xsn vecT gmixT gmix PT xT xnT xhi xlo musplit "
            "hi lo_d lo_p half projev "
            "prefill prefset vecmm vec vecst hank lora lt sgm loraout gout "
            "sq ssum qks qkn vtT vtok score nmx prob pnorm pT pTc av avc "
            "rk_sq rk_ss rk_nr cbias ebc expd ar bk bonus bons bonv tokT tok v_ch "
            "gram gcp gsel gl x0 nt t1 t1c dx xx z zc u uc y yc st stc "
            "lnm lnsq lnv lnsd yr ysplit ylo "
            "hm hhi hlo r2s x2 x2T x2Tc r2 r2q rn xn2r xn2 gbc xn2st wr wrg logit rt rte cum cumd gates addr lists ovf zero "
            "found foundT "
            "tidx vg xgT xsx tix rows tg gf sg tu uf h hT hs ty y_ "
            "fin out ch_d ch_p"
        ).split()
        s = {n: ctx.enter_context(nc.semaphore("s_" + n)) for n in sem_names}
        pre_in = [ctx.enter_context(nc.semaphore(f"s_pre{i}")) for i in range(2)]
        slot_in = [ctx.enter_context(nc.semaphore(f"s_slot{i}")) for i in range(NS)]

        xgs, sc = ([ctx.enter_context(nc.semaphore(f"s_{q}{i}")) for i in range(2)] for q in ("gathered", "scattered"))
        x_in = [ctx.enter_context(nc.semaphore(f"s_xin{i}")) for i in range(TT)]
        y_in = [ctx.enter_context(nc.semaphore(f"s_y{i}")) for i in range(4)]

        bias_rows = nc.dram_tensor("bias_rows", [H, 384], F32).ap()
        xn2_dram = nc.dram_tensor("xn2_rows", [T, D], F32).ap()
        lists = nc.dram_tensor("slot_lists", [NE * T, 4], F32).ap()
        y_dram = nc.dram_tensor("expert_rows", [2 * T, D], F32).ap()

        def R(off, *dims, p0=0, p1=P):
            n = 1
            for d in dims:
                n *= d
            v = reg[p0:p1, off:off + n]
            if len(dims) == 2:
                return v.rearrange("p (a b) -> p a b", a=dims[0])
            if len(dims) == 3:
                return v.rearrange("p (a b c) -> p a b c", a=dims[0], b=dims[1])
            if len(dims) == 4:
                return v.rearrange("p (a b c d) -> p a b c d", a=dims[0], b=dims[1], c=dims[2])
            return v

        flat = ring[:, :, :].rearrange("p s n -> p (s n)")

        def A(off, *dims, p0=0, p1=P):
            n = 1
            for d in dims:
                n *= d
            o = 2 * CHUNK + off
            v = flat[p0:p1, o:o + n]
            if len(dims) == 2:
                return v.rearrange("p (a b) -> p a b", a=dims[0])
            if len(dims) == 3:
                return v.rearrange("p (a b c) -> p a b c", a=dims[0], b=dims[1])
            if len(dims) == 4:
                return v.rearrange("p (a b c d) -> p a b c d", a=dims[0], b=dims[1], c=dims[2])
            return v

        cst = R(0, NCONST)
        ident, bones, tri, ones = (cst[:, o:o + P] for o in (C_ID, C_BO, C_TRI, C_ONE))
        masks = cst[:, C_MK:C_MK + 7 * P].rearrange("p (l n) -> p l n", l=7)
        VT = R(NCONST, NVEC)
        SM = NCONST + NVEC
        st_ = R(SM, 16)
        mx = R(SM + 16, H, 2)
        rs = R(SM + 32, H, 2)
        cb = R(SM + 48, CT, 2)
        ncb = R(SM + 56, CT, 2)
        sc1 = R(SM + 64, CT)
        gqk = R(SM + 68, 2)
        gcol0 = R(SM + 80, KD)
        tidx = R(SM + 72, 2, 4)
        vgb = R(SM + 16, 2, 4)
        over = R(SM + 120, 1 + 2 * MAXP)
        rowv = R(SM + 100, 2, 2, 4)
        addr = R(SM + 116, 2, 2)
        assert SM + 121 + 2 * MAXP <= 2000 and MAXO <= MAXP and NC == 8
        eps, lnx_eps = (cst[:, C_EPS + i:C_EPS + i + 1] for i in range(2))
        O_XNT, O_AR, O_B, O_K, O_V, O_G, O_YR, O_YM = 2000, 4056, 6104, 7128, 8152, 9176, 10200, 11224
        xnT = R(O_XNT, KD, T + 1)
        xin = R(O_AR, TT, D)
        xrs = R(O_V, TT, D)
        AR = R(O_AR, CT, 2, 2, P)
        Bc = R(O_B, CT, T)
        Kc = R(O_K, CT, T)
        vc = R(O_V, CT, T)
        gg = R(O_G, CT, T)
        yr = R(O_YR, CT, T)
        ym = R(O_YM, CT, T)
        assert O_YM + 1024 <= 12248
        HK = R(O_XNT, H, 256)

        df, rr, kk, kn, nr = (A(1024 * i, CT, T) for i in range(5))
        EP = A(5120, CT, 2, P + 1)
        EN, cs = A(6160, CT, T), A(7184, CT, T)
        pads = [A(8208 + i * CT * (T + 1), CT, T + 1) for i in range(3)]
        sent = A(11296, NE * T * 4 // P).bitcast(I32)
        JJ = A(11552, P)
        GRo = [A(4608 * b, 4, 4, P) for b in range(2)]
        XXo = [A(4608 * b + 2048, 4, 2, P) for b in range(2)]
        NTo = [A(4608 * b + 3072, 4, P) for b in range(2)]
        T1o = [A(4608 * b + 3584, 4, P) for b in range(2)]
        Zb, Ub = A(4096, CW), A(8704, CW)
        Btok, Ktok, Vtok = A(9216, CW), A(9728, CW), A(10240, 2, CW)
        yraw = AR[:, :, :, 0, :]
        St = AR[:, :, 0, 1, 0:HD]

        WL, WM = A(3 * CHUNK, KD, 256), A(3 * CHUNK + 2048, KD, 256)
        qb, kb = A(3 * CHUNK, CT, T), A(3 * CHUNK + 1024, CT, T)
        sqb = A(3 * CHUNK + 2048, 2, CT * T)
        PR = A(3 * CHUNK + 2048, 3, 384)
        PT_ = A(3 * CHUNK + 3200, 2, 384)
        Z = A(3 * CHUNK, 16, T)
        vtm = R(O_YR, TT, CW)

        xh, xl = (xs[:, i * 2048:(i + 1) * 2048].rearrange("p (k t) -> p k t", k=KD) for i in range(2))
        ysp = xs[:, :].rearrange("p (b q c t) -> p b q c t", b=2, q=2, c=CT)
        xsx = [xs[:, b * 2 * S * KD:(b + 1) * 2 * S * KD].rearrange("p (k m) -> p k m", k=KD) for b in range(2)]
        xsh = xs[:, 2048:2048 + 2 * S * (FE // P)].rearrange("p (k m) -> p k m", k=FE // P)
        hTm = R(O_AR, KD, T)
        hh, hl = xl, xh

        LEVEL_LO = {0: 13, 1: 14, 10: 15, 11: 16}

        xg = [R(O_AR + 1024 * b, D, p1=S) for b in range(2)]
        tg, tu, gf, sg = (R(O_XNT + 512 * i, FE, p1=S) for i in range(4))
        ysb = [R(O_B + 1024 * b, 2, 512, p1=S) for b in range(2)]
        ty = R(O_YR, 512, p1=S)
        ub = R(O_YR + 512, 512, p1=S)
        hb = R(O_YM, 512, p1=S)
        slots = R(O_YM + 512, NE, 4, p1=S)
        Wr = R(O_YM, KD, NG + NE)
        brc = R(O_YM + KD * (NG + NE), NG + NE)
        gcol = R(O_YM + 324, 4, 2)
        sq2 = R(O_YM + 332, 2, 4)
        gbc = R(O_YR, D)
        yall = A(CHUNK, 4, 2, 512)

        def chunk_view(slot, kind):
            k = 8 if kind in ("cols", "rows") else 4
            return ring[:, slot, :].rearrange("p (k n) -> p k n", k=k)

        def half_view(slot, kind, j):
            v = chunk_view(slot, kind)
            if kind == "cols":
                return v[:, :, 256 * j:256 * j + 256]
            if kind == "rows":
                return v[:, 4 * j:4 * j + 4, :]
            return v[:, :, 512 * j:512 * j + 512]

        def part_view(w, b, kind):
            k = 8 if kind == "cols" else 4
            return w[:, b, :].rearrange("p (k n) -> p k n", k=k)

        def split_hi(eng, g, b, slot, kind, j, landed):
            landed()
            if not isinstance(g, int) or g >= NB:
                eng.wait_ge(s["half"], g - NB + 1)
            eng.activation(part_view(wh, b, kind), half_view(slot, kind, j), ACT.Copy).then_inc(s["hi"], 1)

        def split_lo(eng, g, b, slot, kind, j, which):
            n = 256 if kind == "cols" else 512
            q = slice(0, LO_D * n // 16) if which == "lo_d" else slice(LO_D * n // 16, n)
            eng.wait_ge(s["hi"], g + 1)
            eng.tensor_tensor(part_view(wl, b, kind)[:, :, q], half_view(slot, kind, j)[:, :, q],
                              part_view(wh, b, kind)[:, :, q].bitcast(F32), ALU.subtract).then_inc(s[which], 1)

        def pre_kind(c):
            return "br" if c in (10, 11) else "cols"

        def pre_hi(eng, g):
            c = g // 2
            split_hi(eng, g, g % NB, c % 2, pre_kind(c), g % 2, lambda: eng.wait_ge(pre_in[c % 2], 16 * (c // 2 + 1)))

        def pre_lo(eng, g, which):
            c = g // 2
            split_lo(eng, g, g % NB, c % 2, pre_kind(c), g % 2, which)

        def moe_half(n, i):
            idx = 3 * n - 1 + i // 2
            return 2 * PRE + 2 * idx + i % 2

        KINDS = ("rows", "rows", "down", "down", "rows", "rows")

        def moe_place(n0, i):
            idx = 3 * n0 - 1 + i // 2
            return (2 * PRE + 2 * idx + i % 2) % NB, idx % NS

        def moe_hi(eng, n, n0, i):
            b, slot = moe_place(n0, i)
            use = (n - n0) // 2 if isinstance(n, int) else None
            base = (3 * n0 - 1 + i // 2) // NS + 1
            count = 16 * (base + use) if use is not None else 8 * (n - n0) + 16 * base
            split_hi(eng, moe_half(n, i), b, slot, KINDS[i], i % 2, lambda: eng.wait_ge(slot_in[slot], count))

        def moe_lo(eng, n, n0, i, which):
            b, slot = moe_place(n0, i)
            split_lo(eng, moe_half(n, i), b, slot, KINDS[i], i % 2, which)

        FIRST = [(0, 0, "rows", 0), (0, 1, "rows", 1), (1, 0, "rows", 2), (1, 1, "rows", 3)]
        LAST = 3 * NE - 1

        def first_hi(eng, i):
            c, j, kind, o = FIRST[i]
            split_hi(eng, 2 * PRE + o, (2 * PRE + o) % NB, c, kind, j, lambda: eng.wait_ge(slot_in[c], 16))

        def first_lo(eng, i, which):
            c, j, kind, o = FIRST[i]
            split_lo(eng, 2 * PRE + o, (2 * PRE + o) % NB, c, kind, j, which)

        def last_hi(eng, j):
            g = 2 * PRE + 2 * LAST + j
            split_hi(eng, g, g % NB, LAST % NS, "down", j,
                     lambda: eng.wait_ge(slot_in[LAST % NS], 16 * (LAST // NS + 1)))

        def last_lo(eng, j, which):
            g = 2 * PRE + 2 * LAST + j
            split_lo(eng, g, g % NB, LAST % NS, "down", j, which)

        def moved(n, n0):
            return 16 * (n // 2 + 1) if isinstance(n, int) else 8 * (n - n0) + 16 * (n0 // 2 + 1)

        def moved_extra(i):
            return 16 * (NE // 2) + 16 * i + 16

        OKIND = ("rows", "rows", "rows", "rows", "down", "down")

        def over_half(i, q):
            return 2 * PRE + 6 * NE + 6 * i + q

        def over_hi(eng, i, q):
            split_hi(eng, over_half(i, q), (2 * PRE + q) % NB, q // 2, OKIND[q], q % 2,
                     lambda: eng.wait_ge(slot_in[q // 2], 16 * (3 * NE // NS) + 16 + 16 * i))

        def over_lo(eng, i, q, which):
            split_lo(eng, over_half(i, q), (2 * PRE + q) % NB, q // 2, OKIND[q], q % 2, which)

        def gate_done(n, extra=False):
            return 6 * n + 2 * PRE + (2 if extra or (isinstance(n, int) and n == 0) else 0)

        def up_done(n):
            return 6 * n + 2 * PRE + 4

        def down_done(n, j, late=False):
            return 6 * n + 2 * PRE + 7 + j - (2 if late else 0)

        def over_count(eng):
            eng.wait_ge(s["ovf"], 1)
            return eng.value_load(over[0:1, 0:1].bitcast(I32), min_val=0, max_val=MAXO)

        wg_v = w_gate[0].rearrange("e (p k) n -> e p (k n)", p=P)
        wu_v = w_up[0].rearrange("e (p k) n -> e p (k n)", p=P)
        wd_v = w_down[0].rearrange("e (p k) n -> e p (k n)", p=P)

        rows = R(O_K, P, p1=NVEC)

        block = ctx.enter_context(nc.Block())

        @block.sync
        def _(sp):
            for a in range(TT):
                sp.dma_start(xin[:, a, :], x[0, P * a:P * a + P, :]).then_inc(x_in[a], 16)
            sp.dma_start(cst, consts[:, :]).then_inc(s["consts"], 16)

            def vec_in(v, row):
                sp.dma_start(rows[row:row + CT, :], v.rearrange("a (n p) -> (a n) p", p=P)).then_inc(s["vecs"], 16)

            for v, row in ((w0, V_W0), (a0, V_A0), (k_k, V_KK)):
                vec_in(v, row)

            def freed(c):
                sp.wait_ge(s["lo_d"], 2 * c + 2)
                sp.wait_ge(s["lo_p"], 2 * c + 2)

            def pre_load(c):
                if c >= 2:
                    freed(c - 2)
                dst = ring[:, c % 2, :]
                if c < 10:
                    src = w_in[0].rearrange("(k p) n -> p k n", p=P)[:, :, PCH[c]:PCH[c] + 512]
                    dst = dst.rearrange("p (k n) -> p k n", k=8)
                elif c < 12:
                    src = (w_br_moba if c == 10 else w_br_rwkv)[0].rearrange("(k p) n -> p k n", p=P)
                    dst = dst.rearrange("p (k n) -> p k n", k=4)
                else:
                    src = w_out[0].rearrange("(k p) n -> p k n", p=P)[:, :, 512 * (c - 12):512 * (c - 11)]
                    dst = dst.rearrange("p (k n) -> p k n", k=8)
                sp.dma_start(dst, src).then_inc(pre_in[c % 2], 16)

            for c in range(11):
                pre_load(c)

            def moe_load(slot, view, e):
                src = view[e] if isinstance(e, int) else view[bass.ds(e, 1)].rearrange("o p n -> (o p) n")
                sp.dma_start(ring[:, slot, :], src).then_inc(slot_in[slot], 16)

            sp.wait_ge(s["prefill"], 16)
            sp.wait_ge(s["y"], 2)
            moe_load(2, wg_v, 1)
            moe_load(3, wd_v, 0)
            moe_load(4, wu_v, 1)
            for c in range(11, PRE):
                pre_load(c)
            sp.wait_ge(s["hm"], 8)
            moe_load(5, wg_v, 2)
            freed(PRE - 2)
            moe_load(0, wg_v, 0)
            freed(PRE - 1)
            moe_load(1, wu_v, 0)

            def step_loads(n, parity, first=True):
                for q, (view, e) in enumerate(((wg_v, n), (wd_v, n - 1), (wu_v, n))):
                    if q == 0 and not first:
                        continue
                    g = 2 * PRE + 2 * (3 * n - 1 + q - NS) + 2
                    sp.wait_ge(s["lo_d"], g)
                    sp.wait_ge(s["lo_p"], g)
                    moe_load((3 * parity - 1 + q) % NS, view, e)

            step_loads(2, 2, first=False)
            step_loads(3, 3)
            with sp.Fori(0, (NE - 4) // 2) as it:
                for j in range(2):
                    step_loads(2 * it + 4 + j, 4 + j)
            g = 2 * PRE + 2 * (LAST - NS) + 2
            sp.wait_ge(s["lo_d"], g)
            sp.wait_ge(s["lo_p"], g)
            moe_load(LAST % NS, wd_v, NE - 1)

            n_over = over_count(sp)
            with sp.If(n_over > 0):
                with sp.Fori(0, n_over) as i:
                    e = sp.value_load(over[0:1, bass.ds(i + 1, 1)].bitcast(I32), min_val=0, max_val=NE - 1)
                    g = 2 * PRE + 6 * NE + 6 * i
                    sp.wait_ge(s["lo_d"], g)
                    sp.wait_ge(s["lo_p"], g)
                    for q, view in enumerate((wg_v, wu_v, wd_v)):
                        moe_load(q, view, e)
            sp.wait_ge(s["lo_d"], 2 * PRE + 6 * NE)
            sp.wait_ge(s["lo_p"], 2 * PRE + 6 * NE)
            sp.wait_ge(sc[0], 8 * NE + 16 * n_over)
            sp.wait_ge(sc[1], 8 * NE)
            for i in range(4):
                a, cols = i // 2, slice(512 * (i % 2), 512 * (i % 2) + 512)
                sp.dma_start(yall[:, i], y_dram[2 * P * a:2 * P * (a + 1), cols].rearrange("(p k) d -> p k d", k=2))\
                  .then_inc(y_in[i], 16)
            for i in range(4):
                a, cols = i // 2, slice(512 * (i % 2), 512 * (i % 2) + 512)
                sp.wait_ge(s["fin"], i + 1)
                sp.dma_start(out[0, P * a:P * a + P, cols], xrs[:, a, cols]).then_inc(s["out"], 16)
            sp.wait_ge(s["out"], 64)

        @block.gpsimd
        def _(pool):
            chain = [0]

            def link(ins):
                chain[0] += 1
                ins.then_inc(s["ch_p"], 1)
                pool.wait_ge(s["ch_p"], chain[0])

            last_slot, last_token, last_row = (pool.to_reg(v) for v in (NE * T - 1, T - 1, 2 * T - 1))
            for v, row in ((q_gain, V_QG), (k_gain, V_KG)):
                for i in range(2):
                    pool.dma_start(rows[row:row + 1, 64 * i:64 * i + 64], v[:, :]).then_inc(s["vecs2"], 16)
            for v, row in ((k_a, V_KA), (lnx_g, V_LG), (lnx_b, V_LB)):
                pool.dma_start(rows[row:row + CT, :], v.rearrange("a (n p) -> (a n) p", p=P)).then_inc(s["vecs2"], 16)
            pool.dma_start(R(O_G, 768, p1=32), bias_consts[0:32, 0:768]).then_inc(s["biasc"], 16)
            pool.dma_start(R(O_G + 768, 8, p1=32), rel_bias[:, :]).then_inc(s["biasc"], 16)
            for w, lo, hi in ((w1, 0, 64), (a1, 64, 128), (g1, 128, 256)):
                pool.dma_start(WL[:, :, lo:hi], w[0].rearrange("(k p) n -> p k n", p=P)).then_inc(s["lora_w"], 16)
            pool.memset(sent, 1 << 20).then_inc(s["prefset"], 1)
            pool.wait_ge(s["prefset"], 1)
            pool.dma_start(lists.rearrange("(p a) w -> p (a w)", p=P).bitcast(I32), sent).then_inc(s["prefill"], 16)
            pre_lo(pool, 0, "lo_p")
            pre_lo(pool, 1, "lo_p")
            pool.wait_ge(s["lora_w"], 48)
            pool.wait_ge(s["PT"], 1)
            for i, (lo, hi) in enumerate(((0, 64), (64, 128), (128, 256))):
                mu = VT[:, V_MX + KD * i:V_MX + KD * (i + 1)]
                link(pool.tensor_tensor(WM[:, :, lo:hi], WL[:, :, lo:hi], bcast(mu, 2, hi - lo), ALU.mult))
            pool.tensor_tensor(WL, WL, WM, ALU.subtract).then_inc(s["musplit"], 1)

            def square(i):
                pool.wait_ge(s["projev"], 8 + 2 * i)
                tf = (qb, kb)[i].rearrange("p c t -> p (c t)")
                pool.tensor_tensor(sqb[:, i, :], tf, tf, ALU.mult).then_inc(s["sq"], 1)

            for g in range(2, 13):
                pre_lo(pool, g, "lo_p")
                if g == 9:
                    square(0)
                if g == 11:
                    square(1)

            for c in range(2):
                for b in range(2):
                    for u in range(4):
                        pool.wait_ge(s["gcp"], 8 * c + 4 * b + u + 1)
                        v = GRo[b][:, u].rearrange("p (a s) i -> p a s i", a=2)
                        pool.affine_select(out=v, in_=v, pattern=[[0, 2], [1, 2], [1, P]], compare_op=ALU.is_gt,
                                           fill=0.0, base=0, channel_multiplier=-1).then_inc(s["gsel"], 1)
                for lev in range(1, 7):
                    L = 6 * c + lev - 1
                    for b in range(2):
                        n = 2 * L + b
                        pool.wait_ge(s["gsel"], 8 * c + 4 * b + 4)
                        if n >= 2:
                            pool.wait_ge(s["t1"], n - 1)
                        pool.tensor_tensor(NTo[b], GRo[b][:, :, 0, :], bcast(masks[:, lev, :], 1, 4), ALU.mult)\
                            .then_inc(s["nt"], 1)
                    if L in LEVEL_LO:
                        pre_lo(pool, LEVEL_LO[L], "lo_p")
            for g in range(17, 28):
                pre_lo(pool, g, "lo_p")
            for i in range(3):
                first_lo(pool, i, "lo_p")

            pool.wait_ge(s["gbc"], 16)
            xn2 = R(O_XNT, TT, D)
            for a in range(TT):
                pool.wait_ge(s["xn2r"], a + 1)
                pool.tensor_tensor(xn2[:, a, :], xn2[:, a, :], gbc, ALU.mult).then_inc(s["xn2"], 1)
            pool.wait_ge(s["logit"], 1)
            for b in range(2):
                pool.memset(xg[b], 0.0).then_inc(s["zero"], 1)
            pool.wait_ge(s["prefill"], 16)
            pool.wait_ge(s["addr"], 1)
            for a in range(TT):
                for k in range(2):
                    pool.indirect_dma_start(
                        out=lists[:, :], out_offset=bass.IndirectOffsetOnAxis(ap=addr[:, a, k:k + 1].bitcast(U32), axis=0),
                        in_=rowv[:, a, k, :], in_offset=None, bounds_check=last_slot, oob_is_err=False)\
                        .then_inc(s["lists"], 16)
            pool.wait_ge(s["zero"], 2)
            pool.wait_ge(s["lists"], 64)
            pool.wait_ge(s["xn2st"], 16)

            lview = lists.rearrange("(c s) w -> c s w", s=S)

            def list_rows(block_):
                return lview[block_] if isinstance(block_, int) else lview[bass.ds(block_, 1)].rearrange("o s w -> (o s) w")

            def take(n, n0):
                b = n0 % 2
                pool.wait_ge(xgs[b], moved(n, n0) - 16)
                pool.tensor_copy(tidx[0:S, b, 0:1].bitcast(I32), slots[:, bass.ds(n, 1), 0].bitcast(I32)).then_inc(s["tix"], 1)

            def keep(n, n0):
                b = n0 % 2
                if not isinstance(n, int) or n >= 2:
                    pool.wait_ge(sc[b], moved(n, n0) - 16)
                pool.tensor_copy(vgb[0:S, b, 1:2].bitcast(I32), slots[:, bass.ds(n, 1), 1].bitcast(I32))
                pool.tensor_copy(vgb[0:S, b, 2:3], slots[:, bass.ds(n, 1), 2]).then_inc(s["vg"], 1)

            def gather(n, b):
                if isinstance(n, int) and n < 2:
                    pool.wait_ge(s["tidx"], 16 * (n + 1))
                else:
                    pool.wait_ge(s["tix"], n - 1)
                if not isinstance(n, int) or n >= 2:
                    pool.wait_ge(s["xgT"], n - 1)
                pool.nop(nofuse=True)
                pool.indirect_dma_start(
                    out=xg[b], out_offset=None, in_=xn2_dram[:, :],
                    in_offset=bass.IndirectOffsetOnAxis(ap=tidx[0:S, b, 0:1].bitcast(U32), axis=0),
                    bounds_check=last_token, oob_is_err=False).then_inc(xgs[b], 16)

            def scatter(n, b):
                pool.wait_ge(s["vg"], n + 1)
                pool.wait_ge(s["y_"], 2 * n + 2)
                pool.nop(nofuse=True)
                pool.indirect_dma_start(
                    out=y_dram[:, :], out_offset=bass.IndirectOffsetOnAxis(ap=vgb[0:S, b, 1:2].bitcast(U32), axis=0),
                    in_=ysb[b].rearrange("p a n -> p (a n)"), in_offset=None, bounds_check=last_row,
                    oob_is_err=False).then_inc(sc[b], 16)

            pool.dma_start(tidx[0:S, 0, :], list_rows(0)).then_inc(s["tidx"], 16)
            gather(0, 0)
            pool.dma_start(tidx[0:S, 1, :], list_rows(NC)).then_inc(s["tidx"], 16)
            gather(1, 1)
            pool.dma_start(slots, lists.rearrange("(e c s) w -> s e c w", c=NC, s=S)[:, :, 0, :]).then_inc(s["rows"], 16)
            first_lo(pool, 3, "lo_p")

            pool.wait_ge(s["rows"], 16)
            take(2, 2)
            gather(2, 0)
            keep(0, 0)
            take(3, 3)
            gather(3, 1)

            def step(n, n0, scat=True, more=True):
                b = n0 % 2
                moe_lo(pool, n, n0, 0, "lo_p")
                moe_lo(pool, n, n0, 1, "lo_p")
                if scat:
                    scatter(n - 2, b)
                moe_lo(pool, n, n0, 2, "lo_p")
                moe_lo(pool, n, n0, 3, "lo_p")
                if scat:
                    keep(n - 1, n0 - 1)
                moe_lo(pool, n, n0, 4, "lo_p")
                if more:
                    take(n + 3, n0 + 3)
                    gather(n + 3, 1 - b)
                moe_lo(pool, n, n0, 5, "lo_p")

            step(1, 1, scat=False)
            step(2, 2)
            step(3, 3)
            with pool.Fori(0, (NE - 4) // 2 - 2) as it:
                for j in range(2):
                    step(2 * it + 4 + j, 4 + j)
            for n in range(NE - 4, NE):
                step(n, n, more=n < NE - 3)
            last_lo(pool, 0, "lo_p")
            keep(NE - 1, NE - 1)
            last_lo(pool, 1, "lo_p")
            scatter(NE - 2, 0)
            scatter(NE - 1, 1)

            n_over = over_count(pool)
            with pool.If(n_over > 0):
                with pool.Fori(0, n_over) as i:
                    n = NE + i
                    row = pool.value_load(over[0:1, bass.ds(i + 1 + MAXP, 1)].bitcast(I32), min_val=0, max_val=NE * NC - 1)
                    pool.wait_ge(sc[0], moved_extra(i) - 16)
                    pool.wait_ge(sc[1], 8 * NE)
                    pool.dma_start(tidx[0:S, 0, :], list_rows(row)).then_inc(s["tidx"], 16)
                    pool.dma_start(vgb[0:S, 0, :], list_rows(row)).then_inc(s["tidx"], 16)
                    pool.wait_ge(s["tidx"], 64 + 32 * i)
                    pool.sem_inc(s["vg"], 1)
                    pool.nop(nofuse=True)
                    pool.indirect_dma_start(
                        out=xg[0], out_offset=None, in_=xn2_dram[:, :],
                        in_offset=bass.IndirectOffsetOnAxis(ap=tidx[0:S, 0, 0:1].bitcast(U32), axis=0),
                        bounds_check=last_token, oob_is_err=False).then_inc(xgs[0], 16)
                    for q in range(6):
                        over_lo(pool, i, q, "lo_p")
                    scatter(n, 0)

        @block.scalar
        def _(act):
            def vec_in(v, row, n):
                act.dma_start(rows[row:row + n, :], v).then_inc(s["vecs"], 16)

            act.dma_start(rows[V_GMIX:V_GMIX + KD, :], norm_mix_g.rearrange("a (n p) -> (a n) p", p=P)).then_inc(s["gain"], 16)
            vec_in(mu_rkv[0].rearrange("a (n p) -> (a n) p", p=P), V_MRKV, 3 * CT)
            vec_in(mu_x[0].rearrange("a (n p) -> (a n) p", p=P), V_MX, 3 * KD)
            vec_in(r_k[0].rearrange("(n b) d -> n (b d)", b=2), V_RK, CT)
            junk = R(O_V, D)
            for a in range(TT):
                act.wait_ge(x_in[a], 16)
                act.activation(junk, xin[:, a, :], ACT.Square, accum_out=st_[:, a:a + 1]).then_inc(s["rms0"], 1)
                act.wait_ge(s["rms0"], a + 1)
            act.wait_ge(s["consts"], 16)
            act.activation(st_[:, 4:6], st_[:, 0:2], ACT.Sqrt, scale=1.0 / D, bias=eps).then_inc(s["rms0"], 1)
            act.dma_start(R(O_YR, CW, p1=64), w2[0]).then_inc(s["lora2"], 16)
            act.dma_start(R(O_YR, CW, p0=64), a2[0]).then_inc(s["lora2"], 16)
            act.dma_start(R(O_YR + CW, CW), g2[0]).then_inc(s["lora2"], 16)
            for q in range(4):
                act.wait_ge(s["xnT"], 2 * q + 2)
                act.activation(xh[:, 2 * q:2 * q + 2], xnT[:, 2 * q:2 * q + 2, 1:T + 1], ACT.Copy).then_inc(s["xhi"], 1)
            pre_hi(act, 0)
            pre_hi(act, 1)
            act.dma_start(JJ, bias_consts[:, 768:896]).then_inc(s["hank"], 16)
            act.dma_start(rowv.rearrange("p a k w -> p (a k w)").bitcast(I32), slot_rows[:, :]).then_inc(s["rte"], 16)

            def evac(g):
                act.wait_ge(s["half"], g + 1)
                src = banks[6 + g % 2][:, :].rearrange("p (a t) -> p a t", a=2)
                f = ACT.Copy
                if g < 6:
                    dst = pads[g // 2][:, 2 * (g % 2):2 * (g % 2) + 2, 1:T + 1]
                elif g < 10:
                    if g == 6:
                        act.wait_ge(s["lora"], 1)
                    dst = (qb, kb)[g // 2 - 3][:, 2 * (g % 2):2 * (g % 2) + 2, :]
                elif g < 12:
                    dst = ym[:, 2 * (g % 2):2 * (g % 2) + 2, :]
                else:
                    dst, f = Z[:, 2 * (g - 12):2 * (g - 12) + 2, :], ACT.Sigmoid
                act.activation(dst, src, f).then_inc(s["projev"], 1)

            def two(i):
                return banks[i][:, :].rearrange("p (a t) -> p a t", a=2)

            def lora_hidden():
                act.wait_ge(s["lora"], 1)
                lt = R(O_V, 2, T)
                act.activation(lt[0:64, 0, :], banks[2][0:64, 0:T], ACT.Tanh).then_inc(s["lt"], 1)
                act.activation(lt[64:128, 0, :], banks[2][64:128, 0:T], ACT.Copy).then_inc(s["lt"], 1)
                act.activation(lt[:, 1, :], banks[2][:, T:2 * T], ACT.Sigmoid).then_inc(s["lt"], 1)
                act.wait_ge(s["vec"], 1)
                act.dma_start(bias_rows[:, 0:NV], R(O_B, NV, p1=H)).then_inc(s["vecst"], 16)

            def lora_outputs():
                act.wait_ge(s["loraout"], 1)
                for ct in range(CT):
                    act.activation(Kc[:, ct, :], banks[3 + ct // 2][:, T * (ct % 2):T * (ct % 2) + T], ACT.Sigmoid,
                                   bias=VT[:, V_W0 + ct:V_W0 + ct + 1]).then_inc(s["sgm"], 1)
                act.wait_ge(s["vecst"], 16)
                for ct in range(CT):
                    act.activation(Bc[:, ct, :], banks[(5, 0)[ct // 2]][:, T * (ct % 2):T * (ct % 2) + T], ACT.Sigmoid,
                                   bias=VT[:, V_A0 + ct:V_A0 + ct + 1]).then_inc(s["sgm"], 1)
                for i in range(2):
                    act.activation(gg[:, 2 * i:2 * i + 2, :], two(1 + i), ACT.Copy).then_inc(s["gout"], 1)
                act.wait_ge(s["xlo"], 4)
                act.dma_start(HK, bass.AP(bias_rows.tensor, 0, [[1, P], [384, H], [1, 2 * P]])).then_inc(s["hank"], 16)

            def decays(ct):
                for c in range(2):
                    act.activation(EP[:, ct, c, 1:P + 1], cs[:, ct, P * c:P * c + P], ACT.Exp, scale=-DECAY,
                                   bias=cb[:, ct, c:c + 1]).then_inc(s["expd"], 1)
                    act.activation(EN[:, ct, P * c:P * c + P], cs[:, ct, P * c:P * c + P], ACT.Exp, scale=DECAY,
                                   bias=ncb[:, ct, c:c + 1]).then_inc(s["expd"], 1)

            def root(i, b0, b1):
                act.wait_ge(s["ssum"], i + 1)
                for j, bank_i in enumerate((b0, b1)):
                    act.activation(sqb[:, i, 512 * j:512 * j + 512], banks[bank_i][:, :], ACT.Sqrt, scale=1.0 / HD,
                                   bias=eps).then_inc(s["qks"], 1)

            def tokens(i, dst, bank_i):
                act.wait_ge(s["tokT"], i + 1)
                act.activation(dst, banks[bank_i][:, :], ACT.Copy).then_inc(s["tok"], 1)

            for g in range(12):
                if g >= 1:
                    pre_hi(act, g + 1)
                evac(g)
                if g == 1:
                    lora_hidden()
                elif g == 3:
                    lora_outputs()
                elif g == 6:
                    act.wait_ge(s["cbias"], 2)
                    act.activation(EP[:, :, :, 0], cb, ACT.Exp).then_inc(s["ebc"], 1)
                    act.activation(st_[:, 8:12], ncb[:, :, 1], ACT.Exp).then_inc(s["ebc"], 1)
                    decays(0)
                    decays(1)
                elif g == 7:
                    decays(2)
                    decays(3)
                    act.wait_ge(s["rk_ss"], 1)
                    for i in range(2):
                        act.activation(nr[:, 2 * i:2 * i + 2, :], two(i), ACT.Sqrt).then_inc(s["rk_nr"], 1)
                elif g == 9:
                    act.wait_ge(s["v_ch"], 1)
                    tokens(0, Vtok[:, 0, :], 0)
                    tokens(1, Vtok[:, 1, :], 1)
                elif g == 10:
                    root(0, 4, 5)
                elif g == 11:
                    root(1, 0, 1)

            def exps(h):
                act.wait_ge(s["nmx"], h + 1)
                for q, (lo, hi) in enumerate(((0, 256), (256, 384))):
                    act.activation(PR[:, h % 3, lo:hi], banks[6 + h % 2][:, lo:hi], ACT.Exp, bias=mx[:, h, q:q + 1],
                                   accum_out=rs[:, h, q:q + 1]).then_inc(s["prob"], 1)

            def pt_copy(h):
                act.wait_ge(s["pT"], h + 1)
                act.activation(PT_[:, h % 2, :], banks[6 + h % 2][:, 0:384], ACT.Copy).then_inc(s["pTc"], 1)

            def head_out(h):
                hp = slice(HD * (h % 2), HD * (h % 2) + HD)
                act.wait_ge(s["av"], h + 1)
                act.activation(ym[hp, h // 2, :], banks[6 + h % 2][hp, 0:T], ACT.Copy).then_inc(s["avc"], 1)

            for c in range(2):
                for b in range(2):
                    for u in range(4):
                        act.wait_ge(s["gram"], 8 * c + 4 * b + u + 1)
                        if c == 1 and u == 0 and b == 0:
                            act.wait_ge(s["y"], 1)
                        act.activation(GRo[b][:, u].rearrange("p a i -> p (a i)"), banks[u][:, :], ACT.Copy)\
                           .then_inc(s["gcp"], 1)
                for lev in range(1, 7):
                    L = 6 * c + lev - 1
                    if L == 1:
                        act.wait_ge(s["vtT"], 2)
                        act.activation(vtm[:, 1, :], banks[7][:, :], ACT.Copy).then_inc(s["vtok"], 1)
                    if L >= 10:
                        evac(L + 2)
                    for b in range(2):
                        n = 2 * L + b
                        act.wait_ge(s["t1"], n + 1)
                        if n >= 2:
                            act.wait_ge(s["dx"], n - 1)
                        act.activation(T1o[b].rearrange("p u i -> p (u i)"), banks[3 * b][:, :], ACT.Copy)\
                           .then_inc(s["t1c"], 1)
                    if L == 0:
                        act.wait_ge(s["vtT"], 1)
                        act.activation(vtm[:, 0, :], banks[6][:, :], ACT.Copy).then_inc(s["vtok"], 1)
                    if L == 1:
                        tokens(2, Btok, 6)
                        tokens(3, Ktok, 7)
                    if 2 <= L < H + 2:
                        pt_copy(L - 2)
                    if 3 <= L < H + 3:
                        head_out(L - 3)
                    if L in LEVEL_LO:
                        pre_hi(act, LEVEL_LO[L])
                    if 1 <= L < H + 1:
                        exps(L - 1)
                if c == 1:
                    evac(14)
                    pre_hi(act, 17)
                act.wait_ge(s["z"], c + 1)
                for q in range(2):
                    act.activation(Zb.rearrange("p (v q n) -> p q v n", v=CT, q=2)[:, q],
                                   banks[3 * q][:, 0:CT * HD].rearrange("p (v n) -> p v n", v=CT), ACT.Copy)\
                       .then_inc(s["zc"], 1)
                if c == 1:
                    evac(15)
                    pre_hi(act, 18)
                act.wait_ge(s["u"], c + 1)
                act.activation(Ub, banks[1][:, :], ACT.Copy).then_inc(s["uc"], 1)
                act.wait_ge(s["y"], c + 1)
                act.activation(yraw[:, :, c, :], banks[2][:, :].rearrange("p (a i) -> p a i", a=CT), ACT.Copy)\
                   .then_inc(s["yc"], 1)

            def y_hi(b, src):
                act.activation(ysp[:, b, 0], src, ACT.Copy).then_inc(s["ysplit"], 1)

            pre_hi(act, 19)
            evac(16)
            act.wait_ge(s["lnv"], 1)
            for i in range(2):
                act.activation(Bc[:, 2 * i:2 * i + 2, :], two(2 + i), ACT.Sqrt, scale=1.0 / HD, bias=lnx_eps)\
                   .then_inc(s["lnsd"], 1)
            evac(17)
            pre_hi(act, 20)
            evac(18)
            pre_hi(act, 21)
            evac(19)
            y_hi(1, ym)
            pre_hi(act, 22)
            act.wait_ge(s["yr"], 1)
            y_hi(0, yr)
            act.dma_start(xrs, x[0].rearrange("(a p) d -> p a d", p=P)).then_inc(s["xre"], 16)
            pre_hi(act, 23)
            pre_hi(act, 24)
            pre_hi(act, 25)
            act.wait_ge(s["ylo"], 2)
            act.dma_start(gbc, bcast(norm_ffn_g[0], 0, P)).then_inc(s["gbc"], 16)
            for j in range(4):
                act.dma_start(Wr[:, 2 * j:2 * j + 2, 0:NG], w_grp[0, 256 * j:256 * j + 256].rearrange("(p q) n -> p q n", q=2))\
                   .then_inc(s["wr"], 16)
                act.dma_start(Wr[:, 2 * j:2 * j + 2, NG:NG + NE], w_exp[0, 256 * j:256 * j + 256].rearrange("(p q) n -> p q n", q=2))\
                   .then_inc(s["wr"], 16)
            act.dma_start(gcol, norm_ffn_g[0].rearrange("(j p q) -> p j q", j=4, q=2)).then_inc(s["wr"], 16)
            act.dma_start(brc[:, 0:NG], bcast(b_grp[0], 0, P)).then_inc(s["wr"], 16)
            act.dma_start(brc[:, NG:NG + NE], bcast(b_exp[0], 0, P)).then_inc(s["wr"], 16)
            for n, (lo, hi) in ((6, (0, 4)), (7, (4, 6)), (8, (6, 8))):
                act.wait_ge(s["hm"], n)
                act.activation(hh[:, lo:hi], hTm[:, lo:hi], ACT.Copy).then_inc(s["hhi"], 1)
            pre_hi(act, 26)
            pre_hi(act, 27)

            junk2 = R(O_B, 256)
            for j in range(4):
                act.wait_ge(s["x2"], j + 1)
                for a in range(TT):
                    act.activation(junk2, xrs[:, a, 256 * j:256 * j + 256], ACT.Square,
                                   accum_out=sq2[:, a, j:j + 1]).then_inc(s["r2"], 1)
                    act.wait_ge(s["r2"], TT * j + a + 1)
                if j < 3:
                    act.wait_ge(s["x2T"], j + 1)
                    act.activation(hTm[:, 2 * j:2 * j + 2, :], two(j), ACT.Copy).then_inc(s["x2Tc"], 1)
                    first_hi(act, j)
            act.wait_ge(s["r2s"], 1)
            act.activation(st_[:, 4:6], st_[:, 2:4], ACT.Sqrt, scale=1.0 / D, bias=eps).then_inc(s["r2q"], 1)
            act.wait_ge(s["rn"], 1)
            for a in range(TT):
                act.activation(R(O_XNT, TT, D)[:, a, :], xrs[:, a, :], ACT.Copy, scale=st_[:, 6 + a:7 + a])\
                   .then_inc(s["xn2r"], 1)
            act.wait_ge(s["rt"], 1)
            act.activation(R(O_B + 80, 2, NG), R(O_B + 80, 2, NG), ACT.Exp).then_inc(s["gates"], 1)
            act.wait_ge(s["rt"], 2)
            act.activation(R(O_B + 100, 2), R(O_B + 100, 2), ACT.Exp).then_inc(s["gates"], 1)
            act.wait_ge(s["xn2"], TT)
            act.dma_start(xn2_dram.rearrange("(a p) d -> p a d", p=P), R(O_XNT, TT, D)).then_inc(s["xn2st"], 16)
            def t_gate(n, extra=False):
                act.wait_ge(s["half"], gate_done(n, extra))
                if not isinstance(n, int) or n >= 1:
                    act.wait_ge(s["gf"], n)
                act.activation(tg, banks[0][S:2 * S, :], ACT.Copy).then_inc(s["tg"], 1)

            def t_up(n):
                act.wait_ge(s["half"], up_done(n))
                if not isinstance(n, int) or n >= 1:
                    act.wait_ge(s["uf"], n)
                act.activation(tu, banks[1][S:2 * S, :], ACT.Copy).then_inc(s["tu"], 1)

            def sigm(n):
                act.wait_ge(s["gf"], n + 1)
                if not isinstance(n, int) or n >= 1:
                    act.wait_ge(s["h"], n)
                act.activation(sg, gf, ACT.Silu).then_inc(s["sg"], 1)

            def t_down(n, b, j, late=False):
                act.wait_ge(s["vg"], n + 1)
                act.wait_ge(s["half"], down_done(n, j, late))
                if not isinstance(n, int) or n >= 1 or j:
                    act.wait_ge(s["y_"], 2 * n + j)
                act.activation(ty, banks[2 + j][S:2 * S, :], ACT.Copy, scale=vgb[0:S, b, 2:3]).then_inc(s["ty"], 1)

            first_hi(act, 3)
            t_gate(0)
            sigm(0)

            def step(n, n0):
                b = n0 % 2
                moe_hi(act, n, n0, 0)
                if not isinstance(n, int) or n >= 2:
                    t_down(n - 2, b, 1)
                moe_hi(act, n, n0, 1)
                t_up(n - 1)
                moe_hi(act, n, n0, 2)
                moe_hi(act, n, n0, 3)
                t_gate(n)
                moe_hi(act, n, n0, 4)
                sigm(n)
                t_down(n - 1, 1 - b, 0)
                moe_hi(act, n, n0, 5)

            step(1, 1)
            with act.Fori(0, (NE - 2) // 2) as it:
                for j in range(2):
                    step(2 * it + 2 + j, 2 + j)
            last_hi(act, 0)
            t_down(NE - 2, 0, 1)
            last_hi(act, 1)
            t_up(NE - 1)
            t_down(NE - 1, 1, 0, late=True)
            t_down(NE - 1, 1, 1, late=True)

            n_over = over_count(act)
            with act.If(n_over > 0):
                with act.Fori(0, n_over) as i:
                    n = NE + i
                    for q in range(3):
                        over_hi(act, i, q)
                    t_gate(n, extra=True)
                    sigm(n)
                    for q in range(3, 6):
                        over_hi(act, i, q)
                    t_up(n)
                    t_down(n, 0, 0, late=True)
                    t_down(n, 0, 1, late=True)

        @block.vector
        def _(dve):
            chain = [0]

            def link(ins):
                chain[0] += 1
                ins.then_inc(s["ch_d"], 1)
                dve.wait_ge(s["ch_d"], chain[0])

            def flink(ins, name, count):
                ins.then_inc(s[name], 1)
                dve.wait_ge(s[name], count)

            dve.memset(xnT[:, :, 0:1], 0.0)
            dve.wait_ge(s["rms0"], 3)
            link(dve.reciprocal(st_[:, 6:8], st_[:, 4:6]))
            for a in range(TT):
                dve.tensor_scalar(xin[:, a, :], xin[:, a, :], st_[:, 6 + a:7 + a], None, ALU.mult).then_inc(s["xsn"], 1)
            dve.wait_ge(s["gmixT"], 1)
            flink(dve.tensor_copy(gcol0, banks[0][:, 0:KD]), "gmix", 1)

            def xl_part(q):
                dve.wait_ge(s["xhi"], q + 1)
                dve.tensor_tensor(xl[:, 2 * q:2 * q + 2], xnT[:, 2 * q:2 * q + 2, 1:T + 1], xh[:, 2 * q:2 * q + 2].bitcast(F32),
                                  ALU.subtract).then_inc(s["xlo"], 1)

            for q in range(4):
                dve.wait_ge(s["xT"], q + 1)
                for k in (2 * q, 2 * q + 1):
                    dve.tensor_scalar(xnT[:, k, 1:T + 1], banks[2 + q][:, T * (k % 2):T * (k % 2) + T],
                                      gcol0[:, k:k + 1], None, ALU.mult).then_inc(s["xnT"], 1)
                if q >= 1:
                    dve.wait_ge(s["xnT"], 2 * q)
                    xl_part(q - 1)
            dve.wait_ge(s["xnT"], KD)
            xl_part(3)
            pre_lo(dve, 0, "lo_d")
            pre_lo(dve, 1, "lo_d")
            dve.wait_ge(s["vecT"], 1)
            flink(dve.tensor_copy(VT, banks[1][:, 0:NVEC]), "PT", 1)
            link(dve.tensor_scalar(gqk[:, 0:1], VT[:, V_QG:V_QG + 1], HD ** -0.5, None, ALU.mult))
            dve.wait_ge(s["vecmm"], 1)
            dve.tensor_tensor(R(O_B, NV, p1=H), banks[0][0:H, 0:NV], R(O_G + 384, NV, p1=H), ALU.add).then_inc(s["vec"], 1)
            for g in range(2, 4):
                pre_lo(dve, g, "lo_d")

            for p_ in pads:
                link(dve.memset(p_[:, :, 0:1], 0.0))

            def shift_mix(i, mi, dst):
                p_ = pads[i]
                dve.wait_ge(s["projev"], 2 * i + 2)
                link(dve.tensor_tensor(df, p_[:, :, 0:T], p_[:, :, 1:T + 1], ALU.subtract))
                for ct in range(CT):
                    ins = dve.scalar_tensor_tensor(out=dst[:, ct, :], in0=df[:, ct, :],
                                                   scalar=VT[:, V_MRKV + CT * mi + ct:V_MRKV + CT * mi + ct + 1],
                                                   in1=p_[:, ct, 1:T + 1], op0=ALU.mult, op1=ALU.add)
                link(ins)

            shift_mix(0, 1, kk)
            pre_lo(dve, 4, "lo_d")
            for ct in range(CT):
                ins = dve.tensor_scalar(kn[:, ct, :], kk[:, ct, :], VT[:, V_KK + ct:V_KK + ct + 1], None, ALU.mult)
            link(ins)
            dve.tensor_tensor(nr, kn, kn, ALU.mult).then_inc(s["rk_sq"], 1)
            pre_lo(dve, 5, "lo_d")
            dve.wait_ge(s["sgm"], 4)
            for ct in range(CT):
                for c in range(2):
                    ins = dve.tensor_tensor_scan(cs[:, ct, P * c:P * c + P], ones,
                                                 Kc[:, ct, P * c:P * c + P], 0.0, ALU.mult, ALU.add)
            link(ins)
            mid = cs.rearrange("p c (b t) -> p c b t", b=2)[:, :, :, P // 2 - 1]
            dve.tensor_scalar(cb, mid, DECAY, None, ALU.mult).then_inc(s["cbias"], 1)
            dve.tensor_scalar(ncb, mid, -DECAY, None, ALU.mult).then_inc(s["cbias"], 1)
            pre_lo(dve, 6, "lo_d")
            shift_mix(1, 0, rr)
            pre_lo(dve, 7, "lo_d")
            dve.wait_ge(s["loraout"], 1)
            shift_mix(2, 2, vc)
            dve.sem_inc(s["v_ch"], 1)
            pre_lo(dve, 8, "lo_d")
            dve.wait_ge(s["sgm"], 8)
            for ct in range(CT):
                ins = dve.tensor_scalar(df[:, ct, :], Bc[:, ct, :], 1.0, VT[:, V_KA + ct:V_KA + ct + 1],
                                        ALU.subtract, ALU.mult)
            link(ins)
            link(dve.scalar_tensor_tensor(out=kk, in0=df, scalar=1.0, in1=kk, op0=ALU.add, op1=ALU.mult))
            for ct in range(CT):
                ins = dve.scalar_tensor_tensor(out=df[:, ct, :], in0=rr[:, ct, :], scalar=VT[:, V_RK + ct:V_RK + ct + 1],
                                               in1=kk[:, ct, :], op0=ALU.mult, op1=ALU.mult)
            flink(ins, "bonus", 1)
            pre_lo(dve, 9, "lo_d")
            dve.wait_ge(s["rk_nr"], 2)
            link(dve.tensor_scalar(nr, nr, 1e-12, None, ALU.max))
            link(dve.reciprocal(nr, nr))
            link(dve.tensor_tensor(kn, kn, nr, ALU.mult))
            link(dve.tensor_tensor(Bc, Bc, kn, ALU.mult))
            pre_lo(dve, 10, "lo_d")
            dve.wait_ge(s["expd"], 16)
            dve.wait_ge(s["ebc"], 2)

            def c4(t):
                return t.rearrange("p c (b t) -> p c b t", b=2)

            link(dve.tensor_tensor(sc1, st_[:, 8:12], EP[:, :, 0, P], ALU.mult))
            dve.tensor_tensor(Bc, Bc, EN, ALU.mult).then_inc(s["bk"], 1)
            dve.tensor_tensor(Kc, kk, EN, ALU.mult).then_inc(s["bk"], 1)
            pre_lo(dve, 11, "lo_d")
            for ct in range(CT):
                dve.tensor_tensor(AR[:, ct, :, 1, :], c4(rr)[:, ct], EP[:, ct, :, 1:P + 1], ALU.mult)
                ins = dve.scalar_tensor_tensor(out=AR[:, ct, :, 0, :], in0=c4(kn)[:, ct], scalar=-1.0,
                                               in1=EP[:, ct, :, 0:P], op0=ALU.mult, op1=ALU.mult)
            ins.then_inc(s["ar"], 1)
            dve.wait_ge(s["bons"], 1)
            dve.wait_ge(s["tokT"], 2)
            for i in range(2):
                ins = dve.tensor_tensor(vc[:, 2 * i:2 * i + 2, :], vc[:, 2 * i:2 * i + 2, :],
                                        banks[2 + i][:, :].rearrange("p (a t) -> p a t", a=2), ALU.mult)
            ins.then_inc(s["bonv"], 1)
            pre_lo(dve, 12, "lo_d")

            def hmax(h):
                dve.wait_ge(s["score"], h + 1)
                bk_ = banks[6 + h % 2]
                dve.reduce_max(mx[:, h, 0:1], bk_[:, 0:256], AX.X)
                link(dve.reduce_max(mx[:, h, 1:2], bk_[:, 256:384], AX.X))
                dve.tensor_scalar(mx[:, h, :], mx[:, h, :], -1.0, None, ALU.mult).then_inc(s["nmx"], 1)

            def hnorm(h):
                dve.wait_ge(s["prob"], 2 * h + 2)
                link(dve.reciprocal(rs[:, h, :], rs[:, h, :]))
                for q, (lo, hi) in enumerate(((0, 256), (256, 384))):
                    ins = dve.tensor_scalar(PR[:, h % 3, lo:hi], PR[:, h % 3, lo:hi], rs[:, h, q:q + 1], None, ALU.mult)
                ins.then_inc(s["pnorm"], 1)

            def qk_norm(i, t, gain):
                dve.wait_ge(s["qks"], 2 * i + 2)
                link(dve.reciprocal(sqb[:, i, :], sqb[:, i, :]))
                tf = t.rearrange("p c t -> p (c t)")
                dve.scalar_tensor_tensor(out=tf, in0=tf, scalar=gain, in1=sqb[:, i, :], op0=ALU.mult, op1=ALU.mult)\
                   .then_inc(s["qkn"], 1)

            qk_norm(0, qb, gqk[:, 0:1])

            for c in range(2):
                for b in range(2):
                    n = 2 * c + b
                    dve.wait_ge(s["gl"], n + 1)
                    dve.wait_ge(s["gsel"], 4 * n + 4)
                    for q in range(2):
                        v = XXo[b].rearrange("p (v q) x i -> p q v x i", q=2)[:, q, :, 0, :]
                        link(dve.tensor_tensor(v, banks[4 + q][:, 0:2 * P].rearrange("p (u i) -> p u i", u=2),
                                               bcast(cst[:, C_M0T:C_M0T + P], 1, 2), ALU.mult))
                    link(dve.tensor_tensor(XXo[b][:, :, 1, :], GRo[b][:, :, 0, :], bcast(masks[:, 0, :], 1, 4), ALU.mult))
                    for q in range(2):
                        ins = dve.tensor_tensor(XXo[b][:, :, q, :], XXo[b][:, :, q, :], bcast(ident, 1, 4), ALU.add)
                    ins.then_inc(s["x0"], 1)
                for lev in range(1, 7):
                    L = 6 * c + lev - 1
                    for b in range(2):
                        n = 2 * L + b
                        dve.wait_ge(s["dx"], n + 1)
                        if n >= 2:
                            dve.wait_ge(s["xx"], n - 1)
                        for i in range(2):
                            q = slice(0 if lev < 6 else 1, 2)
                            v = XXo[b][:, 2 * i:2 * i + 2, q, :]
                            d = banks[3 * b + 1 + i][:, :].rearrange("p (u q i) -> p u q i", u=2, q=2)[:, :, q, :]
                            ins = dve.tensor_tensor(v, v, d, ALU.add)
                        ins.then_inc(s["xx"], 1)
                    if L == 0:
                        qk_norm(1, kb, VT[:, V_KG:V_KG + 1])
                    if 1 <= L < H + 1:
                        hmax(L - 1)
                        hnorm(L - 1)
                    if L in LEVEL_LO:
                        pre_lo(dve, LEVEL_LO[L], "lo_d")
                if c == 0:
                    dve.wait_ge(s["st"], 1)
                    for ct in range(CT):
                        ins = dve.tensor_scalar(St[:, ct, :], banks[3][:, HD * ct:HD * ct + HD], sc1[:, ct:ct + 1], None,
                                                ALU.mult)
                    ins.then_inc(s["stc"], 1)
            pre_lo(dve, 17, "lo_d")
            pre_lo(dve, 18, "lo_d")

            dve.wait_ge(s["lnm"], 1)

            def two(i):
                return banks[i][:, :].rearrange("p (a t) -> p a t", a=2)

            dve.wait_ge(s["avc"], H)
            for i in range(2):
                ins = dve.scalar_tensor_tensor(out=c4(yr)[:, 2 * i:2 * i + 2], in0=c4(two(i)), scalar=-1.0 / HD,
                                               in1=yraw[:, 2 * i:2 * i + 2], op0=ALU.mult, op1=ALU.add)
            link(ins)
            dve.tensor_tensor(Kc, yr, yr, ALU.mult).then_inc(s["lnsq"], 1)
            pre_lo(dve, 19, "lo_d")
            dve.wait_ge(s["lnsd"], 2)
            link(dve.reciprocal(Bc, Bc))
            link(dve.tensor_tensor(yr, yr, Bc, ALU.mult))
            for ct in range(CT):
                ins = dve.tensor_scalar(yr[:, ct, :], yr[:, ct, :], VT[:, V_LG + ct:V_LG + ct + 1],
                                        VT[:, V_LB + ct:V_LB + ct + 1], ALU.mult, ALU.add)
            link(ins)
            link(dve.tensor_tensor(yr, yr, vc, ALU.add))
            dve.wait_ge(s["gout"], 2)
            flink(dve.tensor_tensor(yr, yr, gg, ALU.mult), "yr", 1)
            pre_lo(dve, 20, "lo_d")
            pre_lo(dve, 21, "lo_d")
            dve.wait_ge(s["ysplit"], 1)
            dve.tensor_tensor(ysp[:, 1, 1], ym, ysp[:, 1, 0].bitcast(F32), ALU.subtract).then_inc(s["ylo"], 1)
            dve.wait_ge(s["ysplit"], 2)
            dve.tensor_tensor(ysp[:, 0, 1], yr, ysp[:, 0, 0].bitcast(F32), ALU.subtract).then_inc(s["ylo"], 1)

            def mix(g):
                j, br = (g - 20) % 2, 1 - (g - 20) // 2
                for i in range(2):
                    q = 4 * j + 2 * i
                    dve.wait_ge(s["half"], g + 1)
                    src = two(2 * (g % 2) + i)
                    sig = Z[:, 8 * br + q:8 * br + q + 2, :]
                    if g < 22:
                        dve.tensor_tensor(hTm[:, q:q + 2, :], src, sig, ALU.mult).then_inc(s["hm"], 1)
                    else:
                        link(dve.tensor_tensor(Bc[:, 2 * i:2 * i + 2, :], src, sig, ALU.mult))
                        dve.wait_ge(s["hm"], 4)
                        dve.tensor_tensor(hTm[:, q:q + 2, :], hTm[:, q:q + 2, :], Bc[:, 2 * i:2 * i + 2, :], ALU.add)\
                           .then_inc(s["hm"], 1)

            mix(20)
            pre_lo(dve, 22, "lo_d")
            mix(21)
            pre_lo(dve, 23, "lo_d")
            mix(22)
            pre_lo(dve, 24, "lo_d")
            def h_lo(n, lo, hi):
                dve.wait_ge(s["hhi"], n)
                dve.tensor_tensor(hl[:, lo:hi], hTm[:, lo:hi], hh[:, lo:hi].bitcast(F32), ALU.subtract).then_inc(s["hlo"], 1)

            dve.wait_ge(s["half"], 24)
            h_lo(1, 0, 4)
            mix(23)
            h_lo(2, 4, 6)
            h_lo(3, 6, 8)
            pre_lo(dve, 25, "lo_d")
            dve.wait_ge(s["xre"], 16)
            for g in range(24, 28):
                if g < 26:
                    pre_lo(dve, g + 2, "lo_d")
                dve.wait_ge(s["half"], g + 1)
                v = xrs[:, :, 256 * (g - 24):256 * (g - 23)]
                dve.tensor_tensor(v, v, two(4 + g % 2), ALU.add).then_inc(s["x2"], 1)
                if g == 26:
                    first_lo(dve, 0, "lo_d")
                    first_lo(dve, 1, "lo_d")
                if g == 25:
                    dve.wait_ge(s["wr"], 16 * 11)
                    dve.tensor_tensor(Wr, Wr, bcast(gcol.rearrange("p j q -> p (j q)"), 2, NG + NE), ALU.mult)\
                       .then_inc(s["wrg"], 1)
            dve.wait_ge(s["x2T"], 4)
            dve.tensor_copy(hTm[:, 6:8, :], two(3)).then_inc(s["x2Tc"], 1)
            dve.wait_ge(s["r2"], 8)
            dve.tensor_reduce(st_[:, 2:4], sq2, AX.X, ALU.add).then_inc(s["r2s"], 1)
            dve.wait_ge(s["r2q"], 1)
            flink(dve.reciprocal(st_[:, 6:8], st_[:, 4:6]), "rn", 1)

            lg = R(O_B, 2, NG + NE)
            eg = R(O_B + 80, 2, NG)
            d21 = R(O_B + 100, 2)
            one1, one2, sel, key = (R(O_B + 128 + 64 * i, 2, NE) for i in range(4))
            lem = R(O_B + 384, 2, NE)
            cum = R(O_B + 448, 2, NE)
            sm = R(O_B + 520, 8, 2)
            ggrp = R(O_B + 540, 2, NG)
            gk = R(O_B + 550, 2, NG)
            descg, desce = cst[:, C_DESC:C_DESC + NG], cst[:, C_DESC + NG:C_DESC + NG + NE]
            dve.wait_ge(s["logit"], 1)
            for a in range(TT):
                ins = dve.scalar_tensor_tensor(out=lg[:, a, :], in0=banks[6 + a][:, 0:NG + NE], scalar=st_[:, 6 + a:7 + a],
                                               in1=brc, op0=ALU.mult, op1=ALU.add)
            link(ins)

            def first_max(onehot, tmp, val, m_, desc, n, km, then=None):
                link(dve.tensor_reduce(m_, val, AX.X, ALU.max))
                if then:
                    then()
                link(dve.tensor_tensor(tmp, val, bcast(m_, 2, n), ALU.is_equal))
                link(dve.tensor_tensor(tmp, tmp, bcast(desc, 1, 2), ALU.mult))
                link(dve.tensor_reduce(km, tmp, AX.X, ALU.max))
                link(dve.tensor_tensor(onehot, tmp, bcast(km, 2, n), ALU.is_equal))

            first_max(ggrp, gk, lg[:, :, 0:NG], sm[:, 0, :], descg, NG, sm[:, 1, :])
            flink(dve.tensor_tensor(eg, lg[:, :, 0:NG], bcast(sm[:, 0, :], 2, NG), ALU.subtract), "rt", 1)
            link(dve.tensor_scalar(gk, ggrp, 1.0, BIG, ALU.subtract, ALU.mult))
            for a in range(2):
                ins = dve.tensor_tensor(lem[:, a, :].rearrange("p (g e) -> p g e", g=NG),
                                        lg[:, a, NG:NG + NE].rearrange("p (g e) -> p g e", g=NG),
                                        bcast(gk[:, a, :], 2, EG), ALU.add)
            link(ins)
            first_max(one1, key, lem, sm[:, 2, :], desce, NE, sm[:, 3, :])
            link(dve.scalar_tensor_tensor(out=lem, in0=one1, scalar=-3.0 * BIG, in1=lem, op0=ALU.mult, op1=ALU.add))
            first_max(one2, key, lem, sm[:, 4, :], desce, NE, sm[:, 5, :],
                      then=lambda: dve.tensor_tensor(d21, sm[:, 4, :], sm[:, 2, :], ALU.subtract).then_inc(s["rt"], 1))
            flink(dve.tensor_tensor(sel, one1, one2, ALU.add), "cum", 1)
            dve.wait_ge(s["gates"], 2)
            link(dve.tensor_reduce(sm[:, 6, :], eg, AX.X, ALU.add))
            link(dve.tensor_scalar(sm[:, 7, :], d21, 1.0, None, ALU.add))
            link(dve.tensor_tensor(sm[:, 6, :], sm[:, 6, :], sm[:, 7, :], ALU.mult))
            link(dve.reciprocal(sm[:, 6, :], sm[:, 6, :]))
            dve.wait_ge(s["rte"], 16)
            dve.tensor_copy(rowv[:, :, 0, 2], sm[:, 6, :])
            dve.tensor_tensor(rowv[:, :, 1, 2], sm[:, 6, :], d21, ALU.mult)
            dve.wait_ge(s["cumd"], 1)
            link(dve.tensor_tensor(cum, banks[5][:, 0:2 * NE].rearrange("p (a n) -> p a n", a=2),
                                   bcast(cst[:, C_EB:C_EB + NE], 1, 2), ALU.add))
            for k, oh in enumerate((one1, one2)):
                link(dve.tensor_tensor(key, oh, cum, ALU.mult))
                link(dve.tensor_reduce(sm[:, k, :], key, AX.X, ALU.add))
                ins = dve.tensor_copy(addr[:, :, k].bitcast(U32), sm[:, k, :])
            ins.then_inc(s["addr"], 1)
            first_lo(dve, 2, "lo_d")
            def xsplit(n, b):
                dve.wait_ge(s["xgT"], n + 1)
                if not isinstance(n, int) or n >= 2:
                    dve.wait_ge(s["half"], up_done(n - 2))
                src = banks[6][:, 0:KD * S].rearrange("p (k t) -> p k t", k=KD)
                flink(dve.tensor_copy(xsx[b][:, :, 0:S], src), "xsx", 2 * n + 1)
                dve.tensor_tensor(xsx[b][:, :, S:2 * S], src, xsx[b][:, :, 0:S].bitcast(F32), ALU.subtract)\
                   .then_inc(s["xsx"], 1)

            def fold_gate(n):
                dve.wait_ge(s["tg"], n + 1)
                dve.tensor_tensor(gf, banks[0][0:S, :], tg, ALU.add).then_inc(s["gf"], 1)

            def hidden(n):
                dve.wait_ge(s["tu"], n + 1)
                flink(dve.tensor_tensor(ub, banks[1][0:S, :], tu, ALU.add), "uf", n + 1)
                if not isinstance(n, int) or n >= 1:
                    dve.wait_ge(s["hT"], n)
                dve.wait_ge(s["sg"], n + 1)
                dve.tensor_tensor(hb, ub, sg, ALU.mult).then_inc(s["h"], 1)

            def hsplit(n, late=False):
                dve.wait_ge(s["hT"], n + 1)
                if not isinstance(n, int) or n >= 1:
                    dve.wait_ge(s["half"], down_done(n - 1, 1, late))
                src = banks[7][:, 0:4 * S].rearrange("p (k t) -> p k t", k=4)
                flink(dve.tensor_copy(xsh[:, :, 0:S], src), "hs", 2 * n + 1)
                dve.tensor_tensor(xsh[:, :, S:2 * S], src, xsh[:, :, 0:S].bitcast(F32), ALU.subtract)\
                   .then_inc(s["hs"], 1)

            def fold_down(n, n0, j):
                b = n0 % 2
                dve.wait_ge(s["ty"], 2 * n + j + 1)
                if j == 0 and (not isinstance(n, int) or n >= 2):
                    dve.wait_ge(sc[b], moved(n, n0) - 16)
                dve.scalar_tensor_tensor(out=ysb[b][:, j, :], in0=banks[2 + j][0:S, :], scalar=vgb[0:S, b, 2:3], in1=ty,
                                         op0=ALU.mult, op1=ALU.add).then_inc(s["y_"], 1)

            dve.wait_ge(s["half"], 2 * PRE)
            xsplit(0, 0)
            first_lo(dve, 3, "lo_d")
            fold_gate(0)

            def step(n, n0, head=False, tail=False):
                b = n0 % 2
                moe_lo(dve, n, n0, 0, "lo_d")
                if not head:
                    fold_down(n - 2, n0 - 2, 1)
                moe_lo(dve, n, n0, 1, "lo_d")
                hidden(n - 1)
                moe_lo(dve, n, n0, 2, "lo_d")
                hsplit(n - 1)
                moe_lo(dve, n, n0, 3, "lo_d")
                if not tail:
                    xsplit(n + 1, 1 - b)
                fold_gate(n)
                moe_lo(dve, n, n0, 4, "lo_d")
                fold_down(n - 1, n0 - 1, 0)
                moe_lo(dve, n, n0, 5, "lo_d")

            xsplit(1, 1)
            step(1, 1, head=True)
            step(2, 2)
            step(3, 3)
            with dve.Fori(0, (NE - 4) // 2 - 2) as it:
                for j in range(2):
                    step(2 * it + 4 + j, 4 + j)
            step(NE - 4, NE - 4)

            q0 = slice(S, S + MAXP)
            XP = (NC - 1) * NE
            cnt, one, inc = R(O_XNT, NE)[q0], R(O_XNT + 32, XP)[q0], R(O_XNT + 256, XP)[q0]
            fl, flat_fl = R(O_XNT + 512, NC - 1, NE)[q0], R(O_XNT + 512, XP)[q0]
            pick, found = R(O_XNT + 768, NC - 1, NE)[q0], R(O_XNT + 1024, 4)[q0]
            dve.wait_ge(s["cumd"], 2)
            dve.memset(one, 1.0)
            link(dve.tensor_copy(cnt, banks[4][q0, 0:NE]))
            for c in range(NC - 1):
                ins = dve.tensor_scalar(fl[:, c, :], cnt, S * (c + 1) + 0.5, None, ALU.is_gt)
            link(ins)
            link(dve.tensor_tensor_scan(inc, one, flat_fl, 0.0, ALU.mult, ALU.add))
            link(dve.tensor_copy(over[0:1, 0:1].bitcast(I32), inc[0:1, XP - 1:XP]))
            link(dve.tensor_tensor(inc, inc, flat_fl, ALU.mult))
            link(dve.tensor_scalar(flat_fl, inc, cst[q0, C_PI:C_PI + 1], None, ALU.is_equal))
            link(dve.tensor_tensor(pick, fl, bcast(cst[q0, C_EB:C_EB + NE], 1, NC - 1), ALU.mult))
            link(dve.tensor_reduce(found[:, 0:1], pick.rearrange("p c e -> p (c e)"), AX.X, ALU.add))
            link(dve.tensor_tensor(pick, fl, bcast(cst[q0, C_IP:C_IP + NC - 1], 2, NE), ALU.mult))
            link(dve.tensor_reduce(found[:, 1:2], pick.rearrange("p c e -> p (c e)"), AX.X, ALU.add))
            link(dve.tensor_scalar(found[:, 2:3], found[:, 0:1], 1.0 / T, None, ALU.mult))
            dve.scalar_tensor_tensor(out=found[:, 3:4], in0=found[:, 0:1], scalar=NC / T, in1=found[:, 1:2],
                                     op0=ALU.mult, op1=ALU.add).then_inc(s["found"], 1)
            dve.wait_ge(s["foundT"], 1)
            dve.tensor_copy(over[0:1, 1:1 + 2 * MAXP].bitcast(I32), banks[5][0:1, 0:2 * MAXP]).then_inc(s["ovf"], 1)

            step(NE - 3, NE - 3)
            step(NE - 2, NE - 2)

            step(NE - 1, NE - 1, tail=True)
            last_lo(dve, 0, "lo_d")
            fold_down(NE - 2, NE - 2, 1)
            last_lo(dve, 1, "lo_d")
            hidden(NE - 1)
            hsplit(NE - 1)
            fold_down(NE - 1, NE - 1, 0)
            fold_down(NE - 1, NE - 1, 1)

            n_over = over_count(dve)
            with dve.If(n_over > 0):
                with dve.Fori(0, n_over) as i:
                    n = NE + i
                    xsplit(n, 0)
                    for q in range(3):
                        over_lo(dve, i, q, "lo_d")
                    fold_gate(n)
                    for q in range(3, 6):
                        over_lo(dve, i, q, "lo_d")
                    hidden(n)
                    hsplit(n, late=True)
                    dve.wait_ge(sc[0], moved_extra(i) - 16)
                    dve.wait_ge(sc[1], 8 * NE)
                    for j in range(2):
                        dve.wait_ge(s["ty"], 2 * n + j + 1)
                        dve.scalar_tensor_tensor(out=ysb[0][:, j, :], in0=banks[2 + j][0:S, :], scalar=vgb[0:S, 0, 2:3], in1=ty,
                                                 op0=ALU.mult, op1=ALU.add).then_inc(s["y_"], 1)

            for i in range(4):
                v = xrs[:, i // 2, 512 * (i % 2):512 * (i % 2) + 512]
                dve.wait_ge(y_in[i], 16)
                link(dve.tensor_tensor(v, v, yall[:, i, 0, :], ALU.add))
                dve.tensor_tensor(v, v, yall[:, i, 1, :], ALU.add).then_inc(s["fin"], 1)

        @block.tensor
        def _(pe):
            pe.wait_ge(s["consts"], 16)
            pe.wait_ge(s["gain"], 16)
            pe.transpose(banks[0][:, 0:KD], R(O_K, P, p1=KD), ident[0:KD, 0:KD]).then_inc(s["gmixT"], 1)
            pe.wait_ge(s["xsn"], TT)
            for q in range(4):
                for k in (2 * q, 2 * q + 1):
                    for a in range(TT):
                        o = T * (k % 2) + P * a
                        ins = pe.transpose(banks[2 + q][:, o:o + P], xin[:, a, P * k:P * k + P], ident)
                ins.then_inc(s["xT"], 1)

            def passes(bank_ap, stat, mov, first, last, fresh):
                for i, (a, b) in enumerate(((0, 0), (0, 1), (1, 0))):
                    ins = pe.matmul(bank_ap, stat[a], mov[b], start=(first and i == 0 and fresh),
                                    stop=(last and i == 2), skip_group_check=True)
                return ins

            def ready(g):
                pe.wait_ge(s["lo_d"], g + 1)
                pe.wait_ge(s["lo_p"], g + 1)

            def project(g):
                ready(g)
                if g >= 2:
                    pe.wait_ge(s["projev"], g - 1)
                h_, l_ = part_view(wh, g % NB, "cols"), part_view(wl, g % NB, "cols")
                for a in range(2):
                    for k in range(KD):
                        if g == 0 and a == 0 and k % 2 == 0:
                            pe.wait_ge(s["xlo"], k // 2 + 1)
                        ins = passes(banks[6 + g % 2][:, T * a:T * a + T],
                                     (h_[:, k, P * a:P * a + P], l_[:, k, P * a:P * a + P]),
                                     (xh[:, k, :], xl[:, k, :]), k == 0, k == KD - 1, True)
                ins.then_inc(s["half"], 1)

            def lora_in():
                pe.wait_ge(s["musplit"], 1)
                for a in range(2):
                    for k in range(KD):
                        pe.matmul(banks[2][:, T * a:T * a + T], WL[:, k, P * a:P * a + P], xnT[:, k, 1:T + 1],
                                  start=(k == 0), stop=False)
                        ins = pe.matmul(banks[2][:, T * a:T * a + T], WM[:, k, P * a:P * a + P], xnT[:, k, 0:T],
                                        start=False, stop=(k == KD - 1))
                ins.then_inc(s["lora"], 1)

            def lora_out():
                pe.wait_ge(s["lt"], 3)
                pe.wait_ge(s["lora2"], 48)
                pe.wait_ge(s["vec"], 1)
                lt = R(O_V, 2, T)
                w2s = R(O_YR, CW)
                g2s = R(O_YR + CW, CW)
                for ct in range(CT):
                    o = T * (ct % 2)
                    pe.matmul(banks[3 + ct // 2][:, o:o + T], w2s[0:64, P * ct:P * ct + P], lt[0:64, 0, :], start=True, stop=True)
                    pe.matmul(banks[(5, 0)[ct // 2]][:, o:o + T], w2s[64:128, P * ct:P * ct + P], lt[64:128, 0, :],
                              start=True, stop=True)
                    ins = pe.matmul(banks[1 + ct // 2][:, o:o + T], g2s[:, P * ct:P * ct + P], lt[:, 1, :], start=True, stop=True)
                ins.then_inc(s["loraout"], 1)

            def head_sums(src, bank_0, bank_1):
                for j, bank_i in enumerate((bank_0, bank_1)):
                    ins = pe.matmul(banks[bank_i][:, :], bones, src[:, 512 * j:512 * j + 512], start=True, stop=True)
                return ins

            def flat_ct(t):
                return t.rearrange("p c t -> p (c t)")

            def to_tokens(src, a, bank_i):
                for ct in range(CT):
                    ins = pe.transpose(banks[bank_i][:, P * ct:P * ct + P], src[:, ct, P * a:P * a + P], ident)
                return ins

            for g in range(12):
                project(g)
                if g == 0:
                    pe.wait_ge(s["vecs"], 16 * 6)
                    pe.wait_ge(s["vecs2"], 16 * 7)
                    pe.transpose(banks[1][:, 0:NVEC], R(O_K, P, p1=NVEC), ident[0:NVEC, 0:NVEC]).then_inc(s["vecT"], 1)
                    pe.wait_ge(s["biasc"], 32)
                    pe.wait_ge(s["gmix"], 1)
                    pe.matmul(banks[0][0:H, 0:NV], R(O_G + 768, H, p1=32), R(O_G, NV, p1=32), start=True, stop=True)\
                      .then_inc(s["vecmm"], 1)
                elif g == 1:
                    lora_in()
                elif g == 3:
                    lora_out()
                elif g == 7:
                    pe.wait_ge(s["rk_sq"], 1)
                    pe.wait_ge(s["sgm"], 8)
                    pe.wait_ge(s["gout"], 2)
                    head_sums(flat_ct(nr), 0, 1).then_inc(s["rk_ss"], 1)
                elif g == 8:
                    pe.wait_ge(s["v_ch"], 1)
                    pe.wait_ge(s["rk_nr"], 2)
                    for a in range(2):
                        to_tokens(vc, a, a).then_inc(s["tokT"], 1)
                elif g == 9:
                    pe.wait_ge(s["bonus"], 1)
                    head_sums(flat_ct(df), 2, 3).then_inc(s["bons"], 1)
                    pe.wait_ge(s["sq"], 1)
                    head_sums(sqb[:, 0, :], 4, 5).then_inc(s["ssum"], 1)
                elif g == 10:
                    pe.wait_ge(s["sq"], 2)
                    pe.wait_ge(s["tok"], 2)
                    head_sums(sqb[:, 1, :], 0, 1).then_inc(s["ssum"], 1)

            def heads_of(h):
                return slice(HD * (h % 2), HD * (h % 2) + HD), h // 2

            def scores(h):
                hp, ct = heads_of(h)
                if h == 0:
                    pe.wait_ge(s["qkn"], 2)
                    pe.wait_ge(s["hank"], 32)
                if h < 2:
                    pe.wait_ge(s["tok"], 3 + h)
                else:
                    pe.wait_ge(s["avc"], h - 1)
                bk_ = banks[6 + h % 2]
                pe.matmul(bk_[:, 0:256], JJ, HK[:, h, :], start=True, stop=False)
                pe.matmul(bk_[:, 0:256], qb[hp, ct, P:T], kb[hp, ct, :], start=False, stop=True)
                pe.matmul(bk_[:, 256:384], JJ, HK[:, h, P:2 * P], start=True, stop=False)
                pe.matmul(bk_[:, 256:384], qb[hp, ct, 0:P], kb[hp, ct, 0:P], start=False, stop=True)\
                  .then_inc(s["score"], 1)

            def turn(h):
                pe.wait_ge(s["pnorm"], h + 1)
                for a in range(3):
                    ins = pe.transpose(banks[6 + h % 2][:, P * a:P * a + P], PR[:, h % 3, P * a:P * a + P], ident)
                ins.then_inc(s["pT"], 1)

            def values(h):
                hp, ct = heads_of(h)
                pe.wait_ge(s["pTc"], h + 1)
                if h == 0:
                    pe.wait_ge(s["vtok"], 2)
                o, pt = banks[6 + h % 2], PT_[:, h % 2, :].rearrange("p (a t) -> p a t", a=3)
                pe.matmul(o[hp, 0:P], vtm[:, 0, HD * h:HD * h + HD], pt[:, 2, :], start=True, stop=True)
                pe.matmul(o[hp, P:T], vtm[:, 0, HD * h:HD * h + HD], pt[:, 0, :], start=True, stop=False)
                pe.matmul(o[hp, P:T], vtm[:, 1, HD * h:HD * h + HD], pt[:, 1, :], start=False, stop=True)\
                  .then_inc(s["av"], 1)

            def early_gap(L):
                if L == 0:
                    pe.wait_ge(s["projev"], 12)
                    to_tokens(ym, 0, 6).then_inc(s["vtT"], 1)
                if L == 1:
                    pe.wait_ge(s["vtok"], 2)
                    to_tokens(Bc, 0, 6).then_inc(s["tokT"], 1)
                    to_tokens(Kc, 0, 7).then_inc(s["tokT"], 1)
                if 2 <= L < H + 2:
                    turn(L - 2)
                if 3 <= L < H + 3:
                    values(L - 3)
                if L == 11:
                    project(14)

            def late_gap(L):
                if L == 0:
                    to_tokens(ym, 1, 7).then_inc(s["vtT"], 1)
                if 1 <= L < H + 1:
                    scores(L - 1)
                if 9 <= L < 11:
                    pe.wait_ge(s["avc"], L - 2)
                    project(L + 3)

            pe.wait_ge(s["ar"], 1)
            pe.wait_ge(s["qks"], 4)
            pe.wait_ge(s["bonv"], 1)
            for c in range(2):
                tok = slice(P * c, P * c + P)
                if c == 1:
                    pe.wait_ge(s["yc"], 1)
                    pe.wait_ge(s["stc"], 1)
                for b in range(2):
                    for u in range(4):
                        hp, ct = heads_of(4 * b + u)
                        if b == 1:
                            pe.wait_ge(s["gcp"], 8 * c + u + 1)
                        ar = AR[hp, ct, c].rearrange("p a i -> p (a i)")
                        pe.matmul(banks[u][:, 0:256], Bc[hp, ct, tok], ar, start=True, stop=True)
                        pe.matmul(banks[u][:, 256:512], Kc[hp, ct, tok], ar, start=True, stop=True).then_inc(s["gram"], 1)
                    if b == 1:
                        pe.wait_ge(s["x0"], 2 * c + 1)
                    for u in range(4):
                        hp, ct = heads_of(4 * b + u)
                        ins = pe.matmul(banks[4 + u % 2][:, P * (u // 2):P * (u // 2) + P], AR[hp, ct, c, 0, :], Bc[hp, ct, tok],
                                        start=True, stop=True)
                    ins.then_inc(s["gl"], 1)
                for lev in range(1, 7):
                    L = 6 * c + lev - 1
                    for b in range(2):
                        n = 2 * L + b
                        pe.wait_ge(s["nt"], n + 1)
                        pe.wait_ge(s["x0"], 2 * c + 1 + b)
                        if n >= 2:
                            pe.wait_ge(s["xx"], n - 1)
                            pe.wait_ge(s["t1c"], n - 1)
                        if lev == 1:
                            pe.wait_ge(s["gcp"], 8 * c + 5 + 3 * b)
                        for u in range(4):
                            ins = pe.matmul(banks[3 * b][:, P * u:P * u + P], NTo[b][:, u, :], XXo[b][:, u, 0, :],
                                            start=True, stop=True)
                        ins.then_inc(s["t1"], 1)
                    early_gap(L)
                    for b in range(2):
                        n = 2 * L + b
                        pe.wait_ge(s["t1c"], n + 1)
                        if lev == 1:
                            pe.wait_ge(s["gcp"], 8 * c + 7 + b)
                            pe.wait_ge(s["x0"], 2 * c + 1 + b)
                        for u in range(4):
                            o = banks[3 * b + 1 + u // 2]
                            c0 = 256 * (u % 2)
                            if lev < 6:
                                pe.matmul(o[:, c0:c0 + P], XXo[b][:, u, 1, :], T1o[b][:, u, :], start=True, stop=True)
                            ins = pe.matmul(o[:, c0 + P:c0 + 2 * P], T1o[b][:, u, :], XXo[b][:, u, 1, :],
                                            start=True, stop=True)
                        ins.then_inc(s["dx"], 1)
                    late_gap(L)
                pe.wait_ge(s["xx"], 12 * c + 12)
                if c == 0:
                    pe.wait_ge(s["tok"], 4)
                for h in range(H):
                    hp, ct = heads_of(h)
                    v_ = Vtok[:, c, HD * h:HD * h + HD]
                    zo = banks[3 * (h % 2)][:, HD * ct:HD * ct + HD]
                    ins = pe.matmul(zo, GRo[h // 4][:, h % 4, 2, :], v_, start=True, stop=(c == 0))
                    if c == 1:
                        ins = pe.matmul(zo, AR[hp, ct, 1, 0, :], St[hp, ct, :], start=False, stop=True)
                ins.then_inc(s["z"], 1)
                if c == 1:
                    project(15)
                pe.wait_ge(s["zc"], 2 * c + 2)
                for h in range(H):
                    ins = pe.matmul(banks[1][:, HD * h:HD * h + HD], XXo[h // 4][:, h % 4, 1, :],
                                    Zb[:, HD * h:HD * h + HD], start=True, stop=True)
                ins.then_inc(s["u"], 1)
                pe.wait_ge(s["uc"], c + 1)
                if c == 0:
                    for h in range(H):
                        hp, ct = heads_of(h)
                        so = banks[3][hp, HD * ct:HD * ct + HD]
                        pe.matmul(so, Btok[:, HD * h:HD * h + HD], Ub[:, HD * h:HD * h + HD], start=True, stop=False)
                        ins = pe.matmul(so, Ktok[:, HD * h:HD * h + HD], Vtok[:, 0, HD * h:HD * h + HD],
                                        start=False, stop=True)
                    ins.then_inc(s["st"], 1)
                for h in range(H):
                    hp, ct = heads_of(h)
                    yo = banks[2][hp, P * ct:P * ct + P]
                    G_ = GRo[h // 4][:, h % 4]
                    pe.matmul(yo, Vtok[:, c, HD * h:HD * h + HD], G_[:, 3, :], start=True, stop=False)
                    ins = pe.matmul(yo, Ub[:, HD * h:HD * h + HD], G_[:, 1, :], start=False, stop=(c == 0))
                    if c == 1:
                        ins = pe.matmul(yo, St[hp, ct, :], AR[hp, ct, 1, 1, :], start=False, stop=True)
                ins.then_inc(s["y"], 1)

            pe.wait_ge(s["yc"], 2)
            for i in range(2):
                ins = pe.matmul(banks[i][:, :].rearrange("p (a c i) -> p a c i", a=2, c=2), bones,
                                yraw[:, 2 * i:2 * i + 2], start=True, stop=True)
            ins.then_inc(s["lnm"], 1)
            project(16)
            pe.wait_ge(s["lnsq"], 1)
            head_sums(flat_ct(Kc), 2, 3).then_inc(s["lnv"], 1)
            for g in range(17, 20):
                project(g)

            pe.wait_ge(s["lnsd"], 2)
            for g in range(20, 24):
                ready(g)
                pe.wait_ge(s["ysplit"], 1 if g < 22 else 2)
                pe.wait_ge(s["ylo"], 1 if g < 22 else 2)
                if g >= 22:
                    pe.wait_ge(s["hm"], 2 * (g - 21))
                br = 1 - (g - 20) // 2
                h_, l_ = part_view(wh, g % NB, "br"), part_view(wl, g % NB, "br")
                for q in range(4):
                    for k in range(CT):
                        ins = passes(banks[2 * (g % 2) + q // 2][:, T * (q % 2):T * (q % 2) + T],
                                     (h_[:, k, P * q:P * q + P], l_[:, k, P * q:P * q + P]),
                                     (ysp[:, br, 0, k, :], ysp[:, br, 1, k, :]), k == 0, k == CT - 1, True)
                ins.then_inc(s["half"], 1)
            NR_ = NG + NE

            def turn_x2(j):
                pe.wait_ge(s["x2"], j + 1)
                v = xrs[:, :, 256 * j:256 * j + 256].rearrange("p a (c q) -> p a q c", q=2)
                for q in range(2):
                    for a in range(TT):
                        ins = pe.transpose(banks[j][:, T * q + P * a:T * q + P * a + P], v[:, a, q, :], ident)
                ins.then_inc(s["x2T"], 1)

            def logits(j):
                pe.wait_ge(s["x2Tc"], j + 1)
                for a in range(TT):
                    for k in (2 * j, 2 * j + 1):
                        ins = pe.matmul(banks[6 + a][:, 0:NR_], hTm[:, k, P * a:P * a + P], Wr[:, k, :],
                                        start=(k == 0), stop=(k == KD - 1))
                return ins

            for g in range(24, 28):
                ready(g)
                if g >= 26:
                    pe.wait_ge(s["x2"], g - 25)
                h_, l_ = part_view(wh, g % NB, "cols"), part_view(wl, g % NB, "cols")
                for a in range(TT):
                    tk = slice(P * a, P * a + P)
                    for k in range(KD):
                        if g == 24 and a == 0 and k in (0, 4, 6):
                            pe.wait_ge(s["hlo"], (1, 2, 3)[(0, 4, 6).index(k)])
                        ins = passes(banks[4 + g % 2][:, T * a:T * a + T], (hh[:, k, tk], hl[:, k, tk]),
                                     (h_[:, k, :], l_[:, k, :]), k == 0, k == KD - 1, True)
                ins.then_inc(s["half"], 1)
                if g >= 25:
                    turn_x2(g - 25)
            pe.wait_ge(s["wrg"], 1)
            for j in range(3):
                logits(j)
            turn_x2(3)
            logits(3).then_inc(s["logit"], 1)
            pe.wait_ge(s["cum"], 1)
            sel = R(O_B + 256, 2, NE)
            pe.matmul(banks[5][:, 0:NE], tri, sel[:, 0, :], start=True, stop=True)
            pe.matmul(banks[5][:, NE:2 * NE], tri, sel[:, 1, :], start=True, stop=False)
            pe.matmul(banks[5][:, NE:2 * NE], ones, sel[:, 0, :], start=False, stop=True).then_inc(s["cumd"], 1)
            pe.matmul(banks[4][:, 0:NE], ones, sel[:, 0, :], start=True, stop=False)
            pe.matmul(banks[4][:, 0:NE], ones, sel[:, 1, :], start=False, stop=True).then_inc(s["cumd"], 1)

            def turn_x(n, b, gathered):
                pe.wait_ge(xgs[b], gathered)
                if not isinstance(n, int) or n >= 1:
                    pe.wait_ge(s["xsx"], 2 * n)
                pe.nop(nofuse=True)
                v = xg[b].rearrange("p (q k) -> p q k", k=KD)
                for k in range(KD):
                    ins = pe.transpose(banks[6][:, S * k:S * k + S], v[:, :, k], ident[0:S, 0:S])
                ins.then_inc(s["xgT"], 1)

            def wide(bank_i, stat, buf, k0, first, last):
                h_, l_ = part_view(wh, buf, "rows"), part_view(wl, buf, "rows")
                for k in range(4):
                    pe.matmul(banks[bank_i][0:2 * S, :], stat[:, k0 + k, :], h_[:, k, :], start=(first and k == 0), stop=False)
                    ins = pe.matmul(banks[bank_i][0:2 * S, :], stat[:, k0 + k, :], l_[:, k, :], start=False,
                                    stop=(last and k == 3))
                return ins

            def gate_half(n, b, g, buf, j):
                ready(g)
                if j == 0:
                    pe.wait_ge(s["xsx"], 2 * n + 2)
                    if not isinstance(n, int) or n >= 1:
                        pe.wait_ge(s["gf"], n)
                ins = wide(0, xsx[b], buf, 4 * j, j == 0, j == 1)
                ins.then_inc(s["half"], 1)

            def up_half(n, b, g, buf, j):
                ready(g)
                if j == 0 and (not isinstance(n, int) or n >= 1):
                    pe.wait_ge(s["uf"], n)
                ins = wide(1, xsx[b], buf, 4 * j, j == 0, j == 1)
                ins.then_inc(s["half"], 1)

            def turn_h(n):
                pe.wait_ge(s["h"], n + 1)
                if not isinstance(n, int) or n >= 1:
                    pe.wait_ge(s["hs"], 2 * n)
                pe.nop(nofuse=True)
                v = hb.rearrange("p (q k) -> p q k", k=4)
                for k in range(4):
                    ins = pe.transpose(banks[7][:, S * k:S * k + S], v[:, :, k], ident[0:S, 0:S])
                ins.then_inc(s["hT"], 1)

            def down_half(n, g, buf, j):
                ready(g)
                if j == 0:
                    pe.wait_ge(s["hs"], 2 * n + 2)
                if not isinstance(n, int) or n >= 1:
                    pe.wait_ge(s["y_"], 2 * n - 1 + j)
                ins = wide(2 + j, xsh, buf, 0, True, True)
                ins.then_inc(s["half"], 1)

            turn_x(0, 0, 16)
            for j in range(2):
                gate_half(0, 0, 2 * PRE + j, (2 * PRE + j) % NB, j)
            turn_x(1, 1, 16)
            for j in range(2):
                up_half(0, 0, 2 * PRE + 2 + j, (2 * PRE + 2 + j) % NB, j)

            def step(n, n0, tail=False):
                b = n0 % 2
                place = [moe_place(n0, i)[0] for i in range(6)]
                for j in range(2):
                    gate_half(n, b, moe_half(n, j), place[j], j)
                turn_h(n - 1)
                if not tail:
                    turn_x(n + 1, 1 - b, moved(n + 1, n0 + 1))
                for j in range(2):
                    down_half(n - 1, moe_half(n, 2 + j), place[2 + j], j)
                for j in range(2):
                    up_half(n, b, moe_half(n, 4 + j), place[4 + j], j)

            step(1, 1)
            with pe.Fori(0, (NE - 4) // 2 - 1) as it:
                for j in range(2):
                    step(2 * it + 2 + j, 2 + j)
            step(NE - 4, NE - 4)
            pe.wait_ge(s["found"], 1)
            q0 = slice(S, S + MAXP)
            found = R(O_XNT + 1024, 4)[q0]
            for i in range(2):
                ins = pe.matmul(banks[5][0:1, MAXP * i:MAXP * i + MAXP], found[:, 2 + i:3 + i], ident[q0, q0],
                                start=True, stop=True)
            ins.then_inc(s["foundT"], 1)
            step(NE - 3, NE - 3)
            step(NE - 2, NE - 2)
            step(NE - 1, NE - 1, tail=True)
            turn_h(NE - 1)
            for j in range(2):
                g = 2 * PRE + 2 * LAST + j
                down_half(NE - 1, g, g % NB, j)

            n_over = over_count(pe)
            with pe.If(n_over > 0):
                with pe.Fori(0, n_over) as i:
                    n = NE + i
                    turn_x(n, 0, moved_extra(i))
                    for j in range(2):
                        gate_half(n, 0, over_half(i, j), (2 * PRE + j) % NB, j)
                    for j in range(2):
                        up_half(n, 0, over_half(i, 2 + j), (2 * PRE + 2 + j) % NB, j)
                    turn_h(n)
                    for j in range(2):
                        down_half(n, over_half(i, 4 + j), (2 * PRE + 4 + j) % NB, j)


_INS = ['x', 'norm_mix_g', 'norm_ffn_g', 'w_in', 'mu_rkv', 'mu_x', 'w0', 'w1', 'w2', 'a0', 'a1', 'a2', 'g1', 'g2',
        'k_k', 'k_a', 'r_k', 'lnx_g', 'lnx_b', 'q_gain', 'k_gain', 'rel_bias', 'w_br_rwkv', 'w_br_moba', 'w_out',
        'w_grp', 'b_grp', 'w_exp', 'b_exp', 'w_gate', 'w_up', 'w_down']


def shape_constants():
    import math

    import numpy as np
    i = np.arange(P)
    c = np.zeros((P, NCONST), np.float32)
    c[:, C_ID:C_ID + P] = np.eye(P)
    c[:, C_BO:C_BO + P] = (i[:, None] // HD == i[None, :] // HD)
    for lev in range(7):
        half = 1 << lev
        m = (i[:, None] // (2 * half) == i[None, :] // (2 * half)) & (i[:, None] % (2 * half) < half) \
            & (i[None, :] % (2 * half) >= half)
        c[:, C_MK + lev * P:C_MK + (lev + 1) * P] = m
    c[:, C_TRI:C_TRI + P] = i[:, None] < i[None, :]
    c[:, C_ONE:C_ONE + P] = 1
    c[:, C_DESC:C_DESC + NG] = np.arange(NG, 0, -1)
    c[:, C_DESC + NG:C_DESC + NG + NE] = np.arange(NE, 0, -1)
    c[:, C_EB:C_EB + NE] = T * np.arange(NE)
    c[:, C_IP:C_IP + 8] = np.arange(1, 9)
    c[:, C_PI] = i - S + 1
    c[:, C_M0T:C_M0T + P] = c[:, C_MK:C_MK + P].T
    c[:, C_EPS:C_EPS + 2] = NORM_EPS, LNX_EPS
    bc_ = np.zeros((P, 896), np.float32)
    for m in range(NV):
        n = T - 1 - m
        if n < 0:
            bc_[:, 384 + m] = -BIG
            continue
        if n < 16:
            b = n
        else:
            b = min(31, 16 + int(np.float32(np.log(np.float32(n) / np.float32(16))) / np.float32(math.log(8)) * np.float32(16)))
        bc_[b, m] = 1
    bc_[:, 768:896] = np.eye(P)[::-1]
    rows = np.zeros((P, 2, 2, 4), np.int32)
    for a in range(2):
        for k in range(2):
            rows[:, a, k, 0] = P * a + i
            rows[:, a, k, 1] = 2 * (P * a + i) + k
    return c, bc_, rows.reshape(P, 16)


def kernel(**inputs):
    import numpy as _np
    import concourse.bacc as _bacc
    from concourse import mybir as _mybir
    from concourse.bass_utils import run_bass_kernel_spmd as _run

    nc = _bacc.Bacc("TRN2", target_bir_lowering=False, num_devices=1)
    arrays, args = {}, []

    def give(name, a):
        arrays[f"in_{name}_dram"] = a
        args.append(nc.dram_tensor(f"in_{name}_dram", a.shape, _mybir.dt.from_np(a.dtype), kind="ExternalInput").ap())

    for name in _INS:
        give(name, _np.ascontiguousarray(inputs[name]))
    for name, a in zip(("consts", "bias_consts", "slot_rows"), shape_constants()):
        give(name, a)
    args.append(nc.dram_tensor("out_0_dram", (1, T, D), _mybir.dt.float32, kind="ExternalOutput").ap())
    build(nc, *args)
    r = _run(nc, [arrays], core_ids=[0])
    return r.results[0]["out_0_dram"]
```
